# Optimizing a Trainium2 kernel written in Bass

```python
import jax, jax.numpy as jnp
from jax import lax
import numpy as np

D_MODEL = 1024
BATCH = 1
SEQ = 256
DEPTH = 1

CHUNK = 64
N_PREV_CHUNKS = 8
BAND = N_PREV_CHUNKS + 1

D_MIX = D_MODEL
HEAD_DIM = 64
ATTN_WIDTH = D_MIX // 2
N_ATTN_HEADS = ATTN_WIDTH // HEAD_DIM
CONV_WIDTH = D_MIX // 4
CONV_K = 3
POOL_WIDTH = D_MIX - ATTN_WIDTH - CONV_WIDTH
POOL_WINDOWS = (2, 4, 8, 16)
N_POOL_GROUPS = len(POOL_WINDOWS)
POOL_GROUP = POOL_WIDTH // N_POOL_GROUPS
REL_CLIP = 128

D_IN = 3 * ATTN_WIDTH + 3 * CONV_WIDTH + POOL_WIDTH
D_FF = 4 * D_MODEL
EPS = 1e-6
NEG_INF = -1e30


def rms_norm(x, g):
    x32 = x.astype(jnp.float32)
    y = x32 * lax.rsqrt(jnp.mean(x32 * x32, axis=-1, keepdims=True) + EPS)
    return (y * g.astype(jnp.float32)).astype(x.dtype)

def chunked_band_attention(q, k, v, rel_bias):
    b, s, h, d = q.shape
    nc = s // CHUNK
    qc = q.reshape(b, nc, CHUNK, h, d)
    pad = ((0, 0), (N_PREV_CHUNKS, 0), (0, 0), (0, 0), (0, 0))
    kp = jnp.pad(k.reshape(b, nc, CHUNK, h, d), pad)
    vp = jnp.pad(v.reshape(b, nc, CHUNK, h, d), pad)
    band_idx = jnp.arange(nc)[:, None] + jnp.arange(BAND)[None, :]
    kb = kp[:, band_idx].reshape(b, nc, BAND * CHUNK, h, d)
    vb = vp[:, band_idx].reshape(b, nc, BAND * CHUNK, h, d)
    scores = jnp.einsum('bnqhd,bnkhd->bnhqk', qc, kb).astype(jnp.float32) * (d ** -0.5)
    qi = jnp.arange(CHUNK)[:, None]
    kj = jnp.arange(BAND * CHUNK)[None, :]
    dist = qi + N_PREV_CHUNKS * CHUNK - kj
    bias = rel_bias[:, jnp.clip(dist, -REL_CLIP, REL_CLIP) + REL_CLIP].astype(jnp.float32)
    valid = jnp.repeat(band_idx >= N_PREV_CHUNKS, CHUNK, axis=1)
    scores = jnp.where(valid[None, :, None, None, :], scores + bias[None, None], NEG_INF)
    p = jax.nn.softmax(scores, axis=-1).astype(v.dtype)
    out = jnp.einsum('bnhqk,bnkhd->bnqhd', p, vb)
    return out.reshape(b, s, h * d)

def gated_short_conv(gb, gc, hin, conv_w):
    z = gc * hin
    s = z.shape[1]
    zp = jnp.pad(z, ((0, 0), (CONV_K - 1, 0), (0, 0)))
    y = sum(conv_w[i] * zp[:, i:i + s] for i in range(CONV_K))
    return gb * y

def multiscale_pool(u, pool_w, pool_scale):
    b, s, c = u.shape
    u32 = u.astype(jnp.float32)
    cs = jnp.concatenate([jnp.zeros((b, 1, c), jnp.float32), jnp.cumsum(u32, axis=1)], axis=1)
    pos1 = jnp.arange(s) + 1
    outs = []
    for g, w in enumerate(POOL_WINDOWS):
        sl = slice(g * POOL_GROUP, (g + 1) * POOL_GROUP)
        csg = cs[:, :, sl]
        lag = jnp.pad(csg[:, :s + 1 - w], ((0, 0), (w - 1, 0), (0, 0)))
        cnt = jnp.minimum(pos1, w).astype(jnp.float32)[None, :, None]
        m = (csg[:, 1:] - lag) / cnt - u32[:, :, sl]
        outs.append(jnp.einsum('bsc,cd->bsd', m.astype(u.dtype), pool_w[g]))
    return jnp.concatenate(outs, axis=-1) * pool_scale

def first_inputs(seed: int = 0) -> dict:
    key = jax.random.key(seed)
    ks = jax.random.split(key, 13)
    f32 = jnp.float32
    L = DEPTH
    x = jax.random.normal(ks[0], (BATCH, SEQ, D_MODEL), f32)
    norm1_g = 1.0 + 0.05 * jax.random.normal(ks[1], (L, D_MODEL), f32)
    w_in = jax.random.normal(ks[2], (L, D_MODEL, D_IN), f32) * D_MODEL ** -0.5
    q_norm_g = 1.0 + 0.05 * jax.random.normal(ks[3], (L, HEAD_DIM), f32)
    k_norm_g = 1.0 + 0.05 * jax.random.normal(ks[4], (L, HEAD_DIM), f32)
    rel_bias = 0.1 * jax.random.normal(ks[5], (L, N_ATTN_HEADS, 2 * REL_CLIP + 1), f32)
    conv_w = jax.random.normal(ks[6], (L, CONV_K, CONV_WIDTH), f32) * CONV_K ** -0.5
    pool_w = jax.random.normal(ks[7], (L, N_POOL_GROUPS, POOL_GROUP, POOL_GROUP), f32) * POOL_GROUP ** -0.5
    pool_scale = 0.5 + 0.1 * jax.random.normal(ks[8], (L, POOL_WIDTH), f32)
    w_out = jax.random.normal(ks[9], (L, D_MIX, D_MODEL), f32) * D_MIX ** -0.5
    norm2_g = 1.0 + 0.05 * jax.random.normal(ks[10], (L, D_MODEL), f32)
    w_mlp1 = jax.random.normal(ks[11], (L, D_MODEL, D_FF), f32) * D_MODEL ** -0.5
    w_mlp2 = jax.random.normal(ks[12], (L, D_FF, D_MODEL), f32) * D_FF ** -0.5
    return {"x": x, "norm1_g": norm1_g, "w_in": w_in, "q_norm_g": q_norm_g,
            "k_norm_g": k_norm_g, "rel_bias": rel_bias, "conv_w": conv_w,
            "pool_w": pool_w, "pool_scale": pool_scale, "w_out": w_out,
            "norm2_g": norm2_g, "w_mlp1": w_mlp1, "w_mlp2": w_mlp2}

def first_block(x, norm1_g, w_in, q_norm_g, k_norm_g, rel_bias, conv_w, pool_w,
              pool_scale, w_out, norm2_g, w_mlp1, w_mlp2):
    b, s, _ = x.shape
    a = ATTN_WIDTH
    c = CONV_WIDTH
    for l in range(DEPTH):
        h = rms_norm(x, norm1_g[l])
        p = jnp.einsum('bsd,de->bse', h, w_in[l])
        q = p[..., 0:a].reshape(b, s, N_ATTN_HEADS, HEAD_DIM)
        k = p[..., a:2 * a].reshape(b, s, N_ATTN_HEADS, HEAD_DIM)
        v = p[..., 2 * a:3 * a].reshape(b, s, N_ATTN_HEADS, HEAD_DIM)
        o = 3 * a
        gb = p[..., o:o + c]
        gc = p[..., o + c:o + 2 * c]
        hin = p[..., o + 2 * c:o + 3 * c]
        u = p[..., o + 3 * c:]
        q = rms_norm(q, q_norm_g[l])
        k = rms_norm(k, k_norm_g[l])
        y_attn = chunked_band_attention(q, k, v, rel_bias[l])
        y_conv = gated_short_conv(gb, gc, hin, conv_w[l])
        y_pool = multiscale_pool(u, pool_w[l], pool_scale[l])
        mix = jnp.concatenate([y_attn, y_conv, y_pool], axis=-1)
        x = x + jnp.einsum('bse,ed->bsd', mix, w_out[l])
        h2 = rms_norm(x, norm2_g[l])
        f = jnp.square(jax.nn.relu(jnp.einsum('bsd,df->bsf', h2, w_mlp1[l])))
        x = x + jnp.einsum('bsf,fd->bsd', f, w_mlp2[l])
    return x


DEPTH_2 = 2

MEM_DIM = D_MODEL // 4
MEM_HEADS = MEM_DIM // HEAD_DIM
MEM_LEN = 256
FOX_DIM = D_MODEL - MEM_DIM
FOX_HEADS = FOX_DIM // HEAD_DIM
CONV_DIM = D_MODEL - MEM_DIM
CONV_WIDTH_2 = 31
Q_BLOCK = 128
D_FF_2 = ((8 * D_MODEL // 3 + 127) // 128) * 128
N_EXPERTS = 8
TOP_K = 2
EXPERT_FF = 7 * D_MODEL // 2
EXPERT_BLOCK = 128
N_FOX = (DEPTH_2 + 1) // 2
N_CONV = DEPTH_2 // 2
NEG_INF_2 = -1e30


def rms_norm_2(x, g):
    xf = x.astype(jnp.float32)
    y = xf * lax.rsqrt(jnp.mean(xf * xf, axis=-1, keepdims=True) + EPS)
    return (y * g.astype(jnp.float32)).astype(x.dtype)

def layer_norm(x, g, b):
    xf = x.astype(jnp.float32)
    mu = jnp.mean(xf, axis=-1, keepdims=True)
    var = jnp.mean(jnp.square(xf - mu), axis=-1, keepdims=True)
    y = (xf - mu) * lax.rsqrt(var + EPS)
    return (y * g.astype(jnp.float32) + b.astype(jnp.float32)).astype(x.dtype)

def forget_attention(q, k, v, log_f):
    B, S, H, hd = q.shape
    nb = S // Q_BLOCK
    c = jnp.cumsum(log_f, axis=1).transpose(0, 2, 1)
    q_blocks = q.reshape(B, nb, Q_BLOCK, H, hd).transpose(1, 0, 2, 3, 4)
    c_blocks = c.reshape(B, H, nb, Q_BLOCK).transpose(2, 0, 1, 3)
    k_pos = jnp.arange(S)
    scale = hd ** -0.5

    def one_block(args):
        q_b, c_b, blk = args
        s = jnp.einsum('bqhd,bkhd->bhqk', q_b, k, preferred_element_type=jnp.float32) * scale
        s = s + (c_b[..., :, None] - c[:, :, None, :])
        q_pos = blk * Q_BLOCK + jnp.arange(Q_BLOCK)
        s = jnp.where(k_pos[None, :] <= q_pos[:, None], s, NEG_INF_2)
        p = jax.nn.softmax(s, axis=-1).astype(v.dtype)
        return jnp.einsum('bhqk,bkhd->bqhd', p, v)

    o = lax.map(one_block, (q_blocks, c_blocks, jnp.arange(nb)))
    return o.transpose(1, 0, 2, 3, 4).reshape(B, S, H * hd)

def memory_attention(xq, mk, mv, g_q, g_k):
    B, S, _ = xq.shape
    M = mk.shape[1]
    q = rms_norm_2(xq.reshape(B, S, MEM_HEADS, HEAD_DIM), g_q)
    k = rms_norm_2(mk.reshape(B, M, MEM_HEADS, HEAD_DIM), g_k)
    v = mv.reshape(B, M, MEM_HEADS, HEAD_DIM)
    s = jnp.einsum('bshd,bmhd->bhsm', q, k, preferred_element_type=jnp.float32) * (HEAD_DIM ** -0.5)
    p = jax.nn.softmax(s, axis=-1).astype(v.dtype)
    return jnp.einsum('bhsm,bmhd->bshd', p, v).reshape(B, S, MEM_DIM)

def conformer_conv(glu_in, dw, dw_b, ln_g, ln_b):
    a, gate = jnp.split(glu_in, 2, axis=-1)
    u = a * jax.nn.sigmoid(gate)
    u = lax.conv_general_dilated(
        u, dw[:, None, :].astype(u.dtype), window_strides=(1,),
        padding=[(CONV_WIDTH_2 - 1, 0)], dimension_numbers=('NWC', 'WIO', 'NWC'),
        feature_group_count=CONV_DIM) + dw_b.astype(u.dtype)
    return jax.nn.silu(layer_norm(u, ln_g, ln_b))

def swiglu(h, w_gate, w_up, w_down):
    return (jax.nn.silu(h @ w_gate) * (h @ w_up)) @ w_down

def moe_swiglu(h, w_router, w_gate, w_up, w_down):
    B, S, D = h.shape
    xt = h.reshape(-1, D)
    T = xt.shape[0]
    A = T * TOP_K
    logits = (xt @ w_router).astype(jnp.float32)
    top_logit, top_idx = lax.top_k(logits, TOP_K)
    gates = jax.nn.softmax(top_logit, axis=-1)
    flat_e = top_idx.reshape(-1)
    order = jnp.argsort(flat_e)
    sorted_e = flat_e[order]
    sizes = jnp.bincount(flat_e, length=N_EXPERTS).astype(jnp.int32)
    padded = ((sizes + EXPERT_BLOCK - 1) // EXPERT_BLOCK) * EXPERT_BLOCK
    pad_end = jnp.cumsum(padded)
    pad_start = pad_end - padded
    start = jnp.cumsum(sizes) - sizes
    dest = pad_start[sorted_e] + (jnp.arange(A, dtype=jnp.int32) - start[sorted_e])
    n_blocks = -(-A // EXPERT_BLOCK) + N_EXPERTS
    rows = n_blocks * EXPERT_BLOCK
    tok_buf = jnp.full((rows,), T, jnp.int32).at[dest].set((order // TOP_K).astype(jnp.int32))
    gate_buf = jnp.zeros((rows,), jnp.float32).at[dest].set(gates.reshape(-1)[order])
    block_start = jnp.arange(n_blocks, dtype=jnp.int32) * EXPERT_BLOCK
    block_expert = jnp.minimum(jnp.searchsorted(pad_end, block_start, side='right'), N_EXPERTS - 1)
    xt_pad = jnp.concatenate([xt, jnp.zeros((1, D), xt.dtype)], axis=0)
    xs = xt_pad[tok_buf].reshape(n_blocks, EXPERT_BLOCK, D)

    def expert_block(args):
        xb, e = args
        return swiglu(xb, w_gate[e], w_up[e], w_down[e])

    ys = lax.map(expert_block, (xs, block_expert)).reshape(rows, D)
    ys = ys * gate_buf[:, None].astype(ys.dtype)
    out = jnp.zeros((T + 1, D), ys.dtype).at[tok_buf].add(ys)[:T]
    return out.reshape(B, S, D)

def second_inputs(seed: int = 0) -> dict:
    key = jax.random.key(seed)
    ks = iter(jax.random.split(key, 40))

    def nrm(shape, scale):
        return jax.random.normal(next(ks), shape, jnp.float32) * scale

    D = D_MODEL
    fox_in = 3 * FOX_DIM + FOX_HEADS + MEM_DIM
    conv_in = 2 * CONV_DIM + MEM_DIM
    return {
        "x": nrm((BATCH, SEQ, D), 1.0),
        "mem": nrm((BATCH, MEM_LEN, D), 1.0),
        "norm_mix": 1.0 + nrm((DEPTH_2, D), 0.02),
        "norm_mem": 1.0 + nrm((DEPTH_2, D), 0.02),
        "norm_ffn": 1.0 + nrm((DEPTH_2, D), 0.02),
        "w_mem_kv": nrm((DEPTH_2, D, 2 * MEM_DIM), D ** -0.5),
        "g_mq": 1.0 + nrm((DEPTH_2, HEAD_DIM), 0.02),
        "g_mk": 1.0 + nrm((DEPTH_2, HEAD_DIM), 0.02),
        "fox_w_in": nrm((N_FOX, D, fox_in), D ** -0.5),
        "fox_b_f": 3.0 + nrm((N_FOX, FOX_HEADS), 0.5),
        "fox_g_q": 1.0 + nrm((N_FOX, HEAD_DIM), 0.02),
        "fox_g_k": 1.0 + nrm((N_FOX, HEAD_DIM), 0.02),
        "fox_w_out": nrm((N_FOX, FOX_DIM + MEM_DIM, D), 0.5 * D ** -0.5),
        "conv_w_in": nrm((N_CONV, D, conv_in), D ** -0.5),
        "conv_b_in": nrm((N_CONV, 2 * CONV_DIM), 0.02),
        "conv_dw": nrm((N_CONV, CONV_WIDTH_2, CONV_DIM), CONV_WIDTH_2 ** -0.5),
        "conv_dw_b": nrm((N_CONV, CONV_DIM), 0.02),
        "conv_ln_g": 1.0 + nrm((N_CONV, CONV_DIM), 0.02),
        "conv_ln_b": nrm((N_CONV, CONV_DIM), 0.02),
        "conv_w_out": nrm((N_CONV, CONV_DIM + MEM_DIM, D), 0.5 * D ** -0.5),
        "ffn_w_gate": nrm((N_FOX, D, D_FF_2), D ** -0.5),
        "ffn_w_up": nrm((N_FOX, D, D_FF_2), D ** -0.5),
        "ffn_w_down": nrm((N_FOX, D_FF_2, D), 0.5 * D_FF_2 ** -0.5),
        "moe_router": nrm((N_CONV, D, N_EXPERTS), D ** -0.5),
        "moe_w_gate": nrm((N_CONV, N_EXPERTS, D, EXPERT_FF), D ** -0.5),
        "moe_w_up": nrm((N_CONV, N_EXPERTS, D, EXPERT_FF), D ** -0.5),
        "moe_w_down": nrm((N_CONV, N_EXPERTS, EXPERT_FF, D), 0.5 * EXPERT_FF ** -0.5),
    }

def second_block(x, mem, norm_mix, norm_mem, norm_ffn, w_mem_kv, g_mq, g_mk,
              fox_w_in, fox_b_f, fox_g_q, fox_g_k, fox_w_out,
              conv_w_in, conv_b_in, conv_dw, conv_dw_b, conv_ln_g, conv_ln_b, conv_w_out,
              ffn_w_gate, ffn_w_up, ffn_w_down,
              moe_router, moe_w_gate, moe_w_up, moe_w_down):
    B, S, D = x.shape
    h = x
    for i in range(DEPTH_2):
        j = i // 2
        u = rms_norm_2(h, norm_mix[i])
        m = rms_norm_2(mem, norm_mem[i])
        mk, mv = jnp.split(m @ w_mem_kv[i], 2, axis=-1)
        if i % 2 == 0:
            proj = u @ fox_w_in[j]
            q, k, v, f_logit, mq = jnp.split(
                proj, [FOX_DIM, 2 * FOX_DIM, 3 * FOX_DIM, 3 * FOX_DIM + FOX_HEADS], axis=-1)
            q = rms_norm_2(q.reshape(B, S, FOX_HEADS, HEAD_DIM), fox_g_q[j])
            k = rms_norm_2(k.reshape(B, S, FOX_HEADS, HEAD_DIM), fox_g_k[j])
            v = v.reshape(B, S, FOX_HEADS, HEAD_DIM)
            log_f = jax.nn.log_sigmoid((f_logit + fox_b_f[j]).astype(jnp.float32))
            mix = forget_attention(q, k, v, log_f)
            w_out = fox_w_out[j]
        else:
            proj = u @ conv_w_in[j]
            glu_in, mq = jnp.split(proj, [2 * CONV_DIM], axis=-1)
            mix = conformer_conv(glu_in + conv_b_in[j], conv_dw[j], conv_dw_b[j],
                                 conv_ln_g[j], conv_ln_b[j])
            w_out = conv_w_out[j]
        mem_out = memory_attention(mq, mk, mv, g_mq[i], g_mk[i])
        h = h + jnp.concatenate([mix, mem_out], axis=-1) @ w_out
        z = rms_norm_2(h, norm_ffn[i])
        if i % 2 == 0:
            h = h + swiglu(z, ffn_w_gate[j], ffn_w_up[j], ffn_w_down[j])
        else:
            h = h + moe_swiglu(z, moe_router[j], moe_w_gate[j], moe_w_up[j], moe_w_down[j])
    return h


def setup_inputs(seed=0):
    out = dict(first_inputs(seed))
    for name, value in second_inputs(seed + 1).items():
        if name != "x":
            out[name + "_2"] = value
    return out


def reference(
    x, norm1_g, w_in, q_norm_g, k_norm_g, rel_bias, conv_w, pool_w, pool_scale, w_out, norm2_g,
    w_mlp1, w_mlp2, mem_2, norm_mix_2, norm_mem_2, norm_ffn_2, w_mem_kv_2, g_mq_2, g_mk_2,
    fox_w_in_2, fox_b_f_2, fox_g_q_2, fox_g_k_2, fox_w_out_2, conv_w_in_2, conv_b_in_2,
    conv_dw_2, conv_dw_b_2, conv_ln_g_2, conv_ln_b_2, conv_w_out_2, ffn_w_gate_2, ffn_w_up_2,
    ffn_w_down_2, moe_router_2, moe_w_gate_2, moe_w_up_2, moe_w_down_2,
):
    x = first_block(
        x, norm1_g, w_in, q_norm_g, k_norm_g, rel_bias, conv_w, pool_w, pool_scale, w_out,
        norm2_g, w_mlp1, w_mlp2,
    )
    return second_block(
        x, mem_2, norm_mix_2, norm_mem_2, norm_ffn_2, w_mem_kv_2, g_mq_2, g_mk_2, fox_w_in_2,
        fox_b_f_2, fox_g_q_2, fox_g_k_2, fox_w_out_2, conv_w_in_2, conv_b_in_2, conv_dw_2,
        conv_dw_b_2, conv_ln_g_2, conv_ln_b_2, conv_w_out_2, ffn_w_gate_2, ffn_w_up_2,
        ffn_w_down_2, moe_router_2, moe_w_gate_2, moe_w_up_2, moe_w_down_2,
    )


_drawn_inputs = setup_inputs


def setup_inputs(seed=0):
    import zlib

    import numpy as np

    out = dict(_drawn_inputs(seed))
    spreads = {}
    factors = {'q_norm_g': 6.065,
     'k_norm_g': 6.351,
     'rel_bias': 5.111,
     'norm_mix_2': 8.0,
     'norm_mem_2': 8.0,
     'norm_ffn_2': 5.003,
     'g_mq_2': 8.0,
     'g_mk_2': 8.0,
     'fox_g_q_2': 8.0,
     'fox_g_k_2': 8.0,
     'conv_b_in_2': 8.0,
     'conv_dw_b_2': 31.204,
     'conv_ln_g_2': 41.022,
     'conv_ln_b_2': 64.0}
    for name, (base, spread) in spreads.items():
        noise = np.random.default_rng([zlib.crc32(name.encode()), seed]).standard_normal(out[name].shape)
        drawn = base * np.exp(spread * noise) if base else spread * noise
        out[name] = __import__('jax').numpy.asarray(drawn.astype(out[name].dtype))
    for name, factor in factors.items():
        out[name] = (out[name] * factor).astype(out[name].dtype)
    return out
```

```python
from contextlib import ExitStack

import concourse.bass as bass
from concourse import mybir

F32 = mybir.dt.float32
F32R = mybir.dt.float32r
I32 = mybir.dt.int32
U32 = mybir.dt.uint32
ALU = mybir.AluOpType
ACT = mybir.ActivationFunctionType
AX_X = mybir.AxisListType.X

P = 128
D = 1024
KT = D // P
S = 256
NB = S // P
HD = 64
EPS = 1e-6
GRAN = 2048
NRAW = 6
NSPLIT = 3

REL_HEADS = 8
FOX_HEADS = 12
MEM_HEADS = 4
CONV_K = 3
POOL_WINDOWS = (2, 4, 8, 16)
DW_K = 31
CONV_TILES = 6
N_EXPERTS = 8
EXPERT_FF = 3584
MOE_CHUNKS = EXPERT_FF // 512
MOE_GRANULES = 6 * MOE_CHUNKS
MOE_TSTEPS = 3 + MOE_CHUNKS

NORM1, NORM2, NMIX0, NMEM0, NFFN0, NMIX1, NMEM1, NFFN1 = range(8)
NORMS = ("norm1", "norm2", "nmix0", "nmem0", "nffn0", "nmix1", "nmem1", "nffn1")
GQ0, GK0, GFQ, GFK, GMQ0, GMK0, GMQ1, GMK1 = range(8)

REL_LEN = 2 * 255 + 1


def bcast(ap, n):
    return bass.AP(ap.tensor, ap.offset, [*[list(d) for d in ap.ap], [0, n]])


def plan():
    at, n = {}, dict(g=0, t=0, j=0, h=0)
    kinds = []

    def stage(name, g=0, t="", j=0, h=0):
        at[name] = dict(n)
        n["g"] += g
        n["t"] += len(t)
        kinds.extend(t)
        n["j"] += j
        n["h"] += h

    stage("norm1", t="bbbb")
    stage("in0", g=10, j=5)
    stage("conv0", t="aaaa")
    stage("qk0", t="aaaa")
    stage("heads0", h=REL_HEADS)
    stage("mix0", t="bb")
    stage("out0", g=4, j=2)
    stage("norm2", t="bbbb")
    stage("ff0", g=32, t="b" * 16)
    stage("nmix0", t="bbbb")
    stage("in1", g=16, j=8)
    stage("nmem0", t="bbbb")
    stage("mem0", g=2, j=1)
    stage("qk1", t="a" * 8)
    stage("heads1", h=FOX_HEADS + MEM_HEADS)
    stage("mix1", t="bbbb")
    stage("out1", g=4, j=2)
    stage("nffn0", t="bbbb")
    stage("ff1", g=33, t="b" * 11)
    stage("nmix1", t="bbbb")
    stage("in2", g=8, j=4)
    stage("nmem1", t="bbbb")
    stage("mem1", g=2, j=1)
    stage("glu", t="adadad")
    stage("qk2", t="aa")
    stage("heads2", h=MEM_HEADS)
    stage("mix2", t="b")
    stage("out2", g=4, j=2)
    stage("nffn1", t="bbbb")
    stage("moe")
    return at, "".join(kinds)


def block_kernel(nc, a, out):
    at, tkinds = plan()
    is_out_job = [False] * at["moe"]["j"]
    for name in ("out0", "out1", "out2"):
        for k in range(2):
            is_out_job[at[name]["j"] + k] = True

    stream = []

    def rows(w, r0, kts, c0, n):
        return w[r0:r0 + kts * P, c0:c0 + n].rearrange("(t p) n -> p t n", p=P)

    def project(w, c0, n):
        for half in range(2):
            stream.append(([rows(w, half * 512, 4, c0, n)], 4, n))

    w_in, w_out, w1, w2 = a["w_in"][0], a["w_out"][0], a["w_mlp1"][0], a["w_mlp2"][0]
    fox_in, fox_out = a["fox_w_in_2"][0], a["fox_w_out_2"][0]
    fg, fu, fd = a["ffn_w_gate_2"][0], a["ffn_w_up_2"][0], a["ffn_w_down_2"][0]
    conv_in, conv_out = a["conv_w_in_2"][0], a["conv_w_out_2"][0]
    kv = a["w_mem_kv_2"]
    eg, eu, ed = a["moe_w_gate_2"][0], a["moe_w_up_2"][0], a["moe_w_down_2"][0]
    FF0_CHUNKS = w1.shape[1] // 512
    FF1_CHUNKS = fg.shape[1] // 256
    FOXW = FOX_HEADS * HD
    FOX_JOBS = [(3 * FOXW, FOX_HEADS)] + [(c * 384, 384) for c in range(6)] + [(3 * FOXW + FOX_HEADS, 256)]
    CONV_JOBS = [(0, 512), (512, 512), (1024, 512), (1536, 256)]

    for c in range(5):
        project(w_in, c * 512, 512)
    for c in range(2):
        project(w_out, c * 512, 512)
    for c in range(FF0_CHUNKS + 1):
        if c < FF0_CHUNKS:
            project(w1, c * 512, 512)
        if c >= 1:
            for k in range(2):
                stream.append(([rows(w2, (c - 1) * 512 + k * 256, 2, 0, D)], 2, D))
    for c0, n in FOX_JOBS:
        project(fox_in, c0, n)
    project(kv[0], 0, 512)
    for c in range(2):
        project(fox_out, c * 512, 512)
    for c in range(FF1_CHUNKS + 1):
        if c < FF1_CHUNKS:
            for half in range(2):
                stream.append(([rows(fg, half * 512, 4, c * 256, 256), rows(fu, half * 512, 4, c * 256, 256)], 4, 512))
        if c >= 1:
            stream.append(([rows(fd, (c - 1) * 256, 2, 0, D)], 2, D))
    for c0, n in CONV_JOBS:
        project(conv_in, c0, n)
    project(kv[1], 0, 512)
    for c in range(2):
        project(conv_out, c * 512, 512)
    NG = len(stream)
    assert NG == at["moe"]["g"] and MOE_GRANULES % NRAW == 0 and MOE_GRANULES % NSPLIT == 0

    raw_count, seen = [], [0] * NRAW
    for g, (parts, _, _) in enumerate(stream):
        seen[g % NRAW] += 16 * len(parts)
        raw_count.append(seen[g % NRAW])

    def moe_first(c):
        return 0 if c == 0 else 4 + 6 * (c - 1)

    ctx = ExitStack()
    with ctx:
        def sb(name, shape, dt=F32, stack=ctx):
            return stack.enter_context(nc.sbuf_tensor(name, shape, dt))

        def sem(name):
            return ctx.enter_context(nc.semaphore(name))

        x = sb("x", [P, NB, D])
        xn = sb("xn", [P, NB, D])
        raw = sb("raw", [P, NRAW, GRAN])
        w_hi = sb("w_hi", [P, NSPLIT, GRAN], F32R)
        w_lo = sb("w_lo", [P, NSPLIT, GRAN], F32R)
        a_hi = sb("a_hi", [P, KT, S], F32R)
        a_lo = sb("a_lo", [P, KT, S], F32R)
        ident = sb("ident", [P, P])
        ident_r = sb("ident_r", [P, P], F32R)
        gcol = sb("gcol", [P, 8, KT])
        hcol = sb("hcol", [P, 8])
        ss = sb("ss", [P, 8, NB])
        ms = sb("ms", [P, 8, NB])
        rstd = sb("rstd", [P, 8, NB])
        mhalf = sb("mhalf", [P, NB])
        eps = sb("eps", [P, 1])
        negtri = sb("negtri", [P, NB, S])
        iota = sb("iota", [P, P])
        mask_r = sb("mask_r", [P, 2, NB, S], F32R)

        mixers = ExitStack()
        mix = sb("mix", [P, NB, D], stack=mixers)
        qT = sb("qT", [P, 8, S], stack=mixers)
        kT = sb("kT", [P, 8, S], stack=mixers)
        sc = sb("sc", [P, 2, NB, S], stack=mixers)
        pr = sb("pr", [P, 2, NB, S], stack=mixers)
        pT = sb("pT", [P, 2, NB, S], stack=mixers)
        nmax = sb("nmax", [P, 2, NB], stack=mixers)
        psumr = sb("psumr", [P, 2, NB], stack=mixers)
        rinv = sb("rinv", [P, 2, NB], stack=mixers)
        qss = sb("qss", [P, 2, 24], stack=mixers)
        layer = ExitStack()
        proj0 = sb("proj0", [P, NB, 2560], stack=layer)
        relT = sb("relT", [P, REL_HEADS, 384], stack=layer)
        rel_row = sb("rel_row", [REL_HEADS, REL_LEN + 1], stack=layer)
        gbT, gcT = qT[:, 4:6, :], qT[:, 6:8, :]
        hiT, mT = kT[:, 4:6, :], kT[:, 6:8, :]
        zT = sb("zT", [P, 2, S + 2], stack=layer)
        uT = sb("uT", [P, 2, S + 16], stack=layer)
        win = sb("win", [P, 2, 2, S + 16], stack=layer)
        invcnt = sb("invcnt", [P, 2, S], stack=layer)
        yT = sb("yT", [P, 2, S], stack=layer)
        cw = sb("cw", [P, 2, CONV_K], stack=layer)
        pscale = sb("pscale", [P, 2], stack=layer)
        pool_w = sb("pool_w", [P, 2, P], stack=layer)
        layer.close()
        layer = ExitStack()
        mem1 = sb("mem1", [P, NB, D], stack=layer)
        kvm1 = sb("kvm1", [P, NB, 512], stack=layer)
        proj1 = sb("proj1", [P, NB, 2572], stack=layer)
        decay = sb("decay", [P, FOX_HEADS, S], stack=layer)
        fb = sb("fb", [P, FOX_HEADS], stack=layer)
        lf = sb("lf", [P, 4, NB, FOX_HEADS], stack=layer)
        negc = sb("negc", [P, NB, FOX_HEADS], stack=layer)
        layer.close()
        layer = ExitStack()
        mem2 = sb("mem2", [P, NB, D], stack=layer)
        kvm2 = sb("kvm2", [P, NB, 512], stack=layer)
        proj2 = sb("proj2", [P, NB, 1792], stack=layer)
        sig = qT[:, 0:2, :]
        glu = sb("glu", [P, CONV_TILES, S + DW_K - 1], stack=layer)
        dwy = sb("dwy", [P, CONV_TILES, S], stack=layer)
        dwq = sb("dwq", [P, CONV_TILES, S], stack=layer)
        stat = sb("stat", [P, 3, S], stack=layer)
        cb_in = sb("cb_in", [P, 2 * CONV_TILES], stack=layer)
        dw = sb("dw", [P, CONV_TILES, DW_K], stack=layer)
        dwb = sb("dwb", [P, CONV_TILES], stack=layer)
        lng = sb("lng", [P, CONV_TILES], stack=layer)
        lnb = sb("lnb", [P, CONV_TILES], stack=layer)
        onesm = sb("onesm", [P, P], stack=layer)
        layer.close()
        mixers.close()
        ffs = ExitStack()
        f_sb = sb("f_sb", [P, 2, NB, 512], stack=ffs)
        f_hi = sb("f_hi", [P, 2, 4, S], F32R, stack=ffs)
        f_lo = sb("f_lo", [P, 2, 4, S], F32R, stack=ffs)
        ffs.close()
        moes = ExitStack()
        mf_sb = sb("mf_sb", [P, 2, 2, 512], stack=moes)
        mf_hi = sb("mf_hi", [P, 2, 4, P], F32R, stack=moes)
        mf_lo = sb("mf_lo", [P, 2, 4, P], F32R, stack=moes)
        xg_hi = sb("xg_hi", [P, KT, P], F32R, stack=moes)
        xg_lo = sb("xg_lo", [P, KT, P], F32R, stack=moes)
        y_sb = sb("y_sb", [P, D], stack=moes)
        pick = sb("pick", [P, NB, P], stack=moes)
        pickg = sb("pickg", [P, NB, P], stack=moes)
        pickgT = sb("pickgT", [P, S], stack=moes)
        gain_b = sb("gain_b", [P, D], stack=moes)
        router = sb("router", [P, KT, N_EXPERTS], stack=moes)
        logit = sb("logit", [P, NB, N_EXPERTS], stack=moes)
        top = sb("top", [P, NB, N_EXPERTS], stack=moes)
        topi = sb("topi", [P, NB, N_EXPERTS], U32, stack=moes)
        topf = sb("topf", [P, NB, N_EXPERTS], stack=moes)
        gate = sb("gate", [P, 4, NB], stack=moes)
        onehot = sb("onehot", [P, 2, NB, N_EXPERTS], stack=moes)
        chosen = sb("chosen", [P, NB, N_EXPERTS], stack=moes)
        rank = sb("rank", [P, NB, 2 * N_EXPERTS], stack=moes)
        gates = sb("gates", [P, NB, 2 * N_EXPERTS], stack=moes)
        count = sb("count", [P, 2], stack=moes)
        n_items = sb("n_items", [P, 1], I32, stack=moes)
        moes.close()

        bank = [ctx.enter_context(nc.psum_tensor(f"bank{i}", [P, 512], F32)) for i in range(8)]

        rel_rows_dram = nc.dram_tensor("rel_rows_dram", (REL_HEADS, REL_LEN + 1), F32, kind="Internal").ap()
        rel_band_dram = nc.dram_tensor("rel_band_dram", (REL_HEADS, P, 384), F32, kind="Internal").ap()

        raw_in = [sem(f"raw_in{i}") for i in range(NRAW)]
        hi_made, lo_made, w_used = sem("hi_made"), sem("lo_made"), sem("w_used")
        x_in, mem_in, const_in, early_in, l1_in, l2_in, moe_in = (
            sem(n) for n in ("x_in", "mem_in", "const_in", "early_in", "l1_in", "l2_in", "moe_in"))
        rel_in, rel_ext, rel_out, rel_band, rel_back = (
            sem(n) for n in ("rel_in", "rel_ext", "rel_out", "rel_band", "rel_back"))
        pool_zero, mask_made = sem("pool_zero"), sem("mask_made")
        ss_made, rstd_made, xn_made = sem("ss_made"), sem("rstd_made"), sem("xn_made")
        t_psum, t_act, t_dve = sem("t_psum"), sem("t_act"), sem("t_dve")
        j_act, j_dve, x_upd = sem("j_act"), sem("j_dve"), sem("x_upd")
        sq_made, qss_made, qsqrt_made, qk_made = (sem(n) for n in ("sq_made", "qss_made", "qsqrt_made", "qk_made"))
        s_psum, s_sb, s_max, s_exp = sem("s_psum"), sem("s_sb"), sem("s_max"), sem("s_exp")
        p_psum, p_sb, o_psum, o_sb = sem("p_psum"), sem("p_sb"), sem("o_psum"), sem("o_sb")
        y_made, m_made, pool_psum, cp_hi, cp_lo = (sem(n) for n in ("y_made", "m_made", "pool_psum", "cp_hi", "cp_lo"))
        f_made, silu_made, h_made = sem("f_made"), sem("silu_made"), sem("h_made")
        lf_x, lf_ln, lf_made, c_psum, c_sb, dec_psum, dec_sb = (
            sem(n) for n in ("lf_x", "lf_ln", "lf_made", "c_psum", "c_sb", "dec_psum", "dec_sb"))
        dw_made, mu_psum, cent_made, sqc_made, var_psum, sd_made, ln_made, silu2 = (
            sem(n) for n in ("dw_made", "mu_psum", "cent_made", "sqc_made", "var_psum", "sd_made", "ln_made", "silu2"))
        ln_hi, ln_lo = sem("ln_hi"), sem("ln_lo")
        z_made, r_psum, g_exp, ch_made, rk_psum, items_made = (
            sem(n) for n in ("z_made", "r_psum", "g_exp", "ch_made", "rk_psum", "items_made"))
        pick_made, y_act, y_dve, sc_psum = sem("pick_made"), sem("y_act"), sem("y_dve"), sem("sc_psum")
        act_own, dve_own, pool_own = sem("act_own"), sem("dve_own"), sem("pool_own")
        out_done = sem("out_done")

        def raw_at(g, n):
            return raw[:, g % NRAW, 0:n]

        def n_el(g):
            return stream[g][1] * stream[g][2]

        def act_steps(t):
            return sum(k in "ab" for k in tkinds[:t + 1])

        def dve_steps(t):
            return sum(k in "bd" for k in tkinds[:t + 1])

        TA, TD, TM = act_steps(len(tkinds)), dve_steps(len(tkinds)), len(tkinds)

        def plain_jobs(j):
            return sum(not o for o in is_out_job[:j + 1])

        LOADS = dict(
            const=[(ident[:], a["c_ident"]), (gcol[:], a["g_norms"]), (hcol[0:HD, :], a["g_heads"]),
                   (hcol[HD:P, :], a["g_heads"]), (negtri[:], a["c_negtri"]), (iota[:], a["c_iota"]),
                   (pr[:], a["c_masks"])],
            early=[(invcnt[:], a["c_invcnt"]), (cw[:], a["conv_w"]), (pscale[:], a["pool_scale"])],
            l1=[(fb[:], bass.AP(a["fox_b_f_2"].tensor, 0, [[0, P], [1, FOX_HEADS]]))],
            l2=[(cb_in[:], a["conv_b_in_2"]), (dw[:], a["conv_dw_2"]), (dwb[:], a["conv_dw_b_2"]),
                (lng[:], a["conv_ln_g_2"]), (lnb[:], a["conv_ln_b_2"])],
            moe=[(router[:], a["moe_router_2"][0].rearrange("(t p) e -> p t e", p=P)),
                 (gain_b[:], bass.AP(a["norm_ffn_2"].tensor, D, [[0, P], [1, D]]))],
        )

        HEADS0 = [(0, h // 2, h // 2, h % 2 * HD, proj0, 1024 + h * HD, h) for h in range(REL_HEADS)]
        HEADS1 = [(1, h // 2, h // 2, h % 2 * HD, proj1, 2 * FOXW + h * HD, h) for h in range(FOX_HEADS)]
        HEADS1 += [(None, 6 + h // 2, 6 + h // 2, h % 2 * HD, kvm1, 256 + h * HD, h) for h in range(MEM_HEADS)]
        HEADS2 = [(None, 6 + h // 2, 6 + h // 2, h % 2 * HD, kvm2, 256 + h * HD, h) for h in range(MEM_HEADS)]
        MQ1, MQ2 = 3 * FOXW + FOX_HEADS, 1536
        memq, memk = qT[:, 6:8, :], kT[:, 6:8, :]
        at_x = dict(norm2=4, ff0=4, nmix0=8, nffn0=12, ff1=12, nmix1=16, moe=20)
        HM = SM = 2 * FF1_CHUNKS

        def last_t_of_norm(n):
            return at[NORMS[n]]["t"] + 3

        def tokens(t):
            return t.rearrange("(b p) d -> p b d", p=P)

        block = ctx.enter_context(nc.Block())

        @block.sync
        def _(sp):
            sp.dma_start(x[:], tokens(a["x"][0])).then_inc(x_in, 16)
            for g, (parts, kts, n) in enumerate(stream):
                if g >= NRAW:
                    sp.wait_ge(lo_made, g - NRAW + 1)
                if len(parts) == 1:
                    sp.dma_start(raw_at(g, kts * n).rearrange("p (t n) -> p t n", t=kts), parts[0])\
                        .then_inc(raw_in[g % NRAW], 16)
                else:
                    dst = raw_at(g, kts * n).rearrange("p (t u n) -> p t u n", t=kts, u=2)
                    for u in range(2):
                        sp.dma_start(dst[:, :, u, :], parts[u]).then_inc(raw_in[g % NRAW], 16)
            sp.wait_ge(items_made, 1)
            items = sp.value_load(n_items[0:1, 0:1], min_val=N_EXPERTS, max_val=2 * N_EXPERTS)
            with sp.Fori(0, items) as i:
                e = i % N_EXPERTS

                def load(k, src, kts):
                    g = NG + k
                    sp.wait_ge(lo_made, i * MOE_GRANULES + (g - NRAW + 1))
                    sp.dma_start(raw_at(g, GRAN).rearrange("p (t n) -> p t n", t=kts),
                                 src.rearrange("a (t p) n -> p (a t) n", p=P)).then_inc(raw_in[g % NRAW], 16)

                for c in range(MOE_CHUNKS + 1):
                    k = moe_first(c)
                    if c < MOE_CHUNKS:
                        for m, w in enumerate((eg, eu)):
                            for half in range(2):
                                load(k, w[bass.ds(e, 1), half * 512:(half + 1) * 512, c * 512:(c + 1) * 512], 4)
                                k += 1
                    if c >= 1:
                        for half in range(2):
                            r0 = (c - 1) * 512 + half * 256
                            load(k, ed[bass.ds(e, 1), r0:r0 + 256, :], 2)
                            k += 1
            sp.wait_ge(x_upd, items * 4 + (at_x["moe"]))
            sp.dma_start(tokens(out[0]), x[:]).then_inc(out_done, 16)
            sp.wait_ge(out_done, 16)

        @block.gpsimd
        def _(pool):
            pool.memset(pool_w[:], 0.0).then_inc(pool_zero, 1)
            pool.memset(mhalf[:], -0.5).then_inc(pool_own, 1)
            for n in range(8):
                pool.wait_ge(ss_made, 2 * (n + 1))
                pool.tensor_scalar(ms[:, n, :], ss[:, n, :], 1.0 / D, EPS, ALU.mult, ALU.add).then_inc(pool_own, 1)
                pool.wait_ge(pool_own, n + 2)
                pool.tensor_tensor(rstd[:, n, :], ms[:, n, :], mhalf[:], ALU.pow).then_inc(rstd_made, 1)

        @block.tensor
        def _(pe):
            def tstep(t, sources, base=None):
                if base is None:
                    if t >= 2:
                        if tkinds[t - 2] in "bd":
                            pe.wait_ge(t_dve, dve_steps(t - 2))
                        else:
                            pe.wait_ge(t_act, act_steps(t - 2))
                    b = bank[6 + t % 2]
                for k, src in enumerate(sources):
                    mm = pe.transpose(b[:, k * P:(k + 1) * P], src, ident[:])
                mm.then_inc(t_psum, 1)

            def parts3(outs, hi, lo, wh, wl, start, stop):
                for o, h, l in zip(outs, wh, wl):
                    pe.matmul(o, hi, h, start=start, stop=False)
                    pe.matmul(o, hi, l, start=False, stop=False)
                for o, h in zip(outs, wh):
                    mm = pe.matmul(o, lo, h, start=False, stop=stop)
                return mm

            def across(g, n, lhs, kt0, outs, first, last):
                slot = g % NSPLIT
                for kk in range(4):
                    wh = w_hi[:, slot, kk * n:(kk + 1) * n]
                    wl = w_lo[:, slot, kk * n:(kk + 1) * n]
                    for b, o in enumerate(outs):
                        mm = parts3([o], lhs(0, kt0 + kk, b), lhs(1, kt0 + kk, b), [wh], [wl],
                                    first and kk == 0, last and kk == 3)
                mm.then_inc(w_used, 1)

            def down(g, lhs, kt0, outs, first, last):
                slot = g % NSPLIT
                for kk in range(2):
                    wh = [w_hi[:, slot, kk * D + h * 512:kk * D + (h + 1) * 512] for h in range(2)]
                    wl = [w_lo[:, slot, kk * D + h * 512:kk * D + (h + 1) * 512] for h in range(2)]
                    for b, o in enumerate(outs):
                        mm = parts3(o, lhs(0, kt0 + kk, b), lhs(1, kt0 + kk, b), wh, wl,
                                    first and kk == 0, last and kk == 1)
                mm.then_inc(w_used, 1)

            def a_tile(part, kt, b):
                return (a_hi, a_lo)[part][:, kt, b * P:(b + 1) * P]

            def job(j, g, n):
                outs = [bank[2 * (j % 2) + b][:, 0:n] for b in range(NB)]
                for half in range(2):
                    pe.wait_ge(lo_made, g + half + 1)
                    across(g + half, n, a_tile, 4 * half, outs, half == 0, half == 1)

            def jobs(name, widths):
                for k, n in enumerate(widths):
                    j = at[name]["j"] + k
                    if j >= 2:
                        pe.wait_ge(j_act, plain_jobs(j - 2))
                        pe.wait_ge(j_dve, plain_jobs(j - 2))
                    job(j, at[name]["g"] + 2 * k, n)

            def norm_t(name, n):
                pe.wait_ge(xn_made, 2 * (n + 1))
                for s in range(4):
                    tstep(at[name]["t"] + s, [xn[:, b, kt * P:(kt + 1) * P] for kt in (2 * s, 2 * s + 1)
                                              for b in range(NB)])
                pe.wait_ge(t_dve, dve_steps(at[name]["t"] + 3))

            def cols_t(t, src, cols):
                tstep(t, [src[:, b, c:c + P] for c in cols for b in range(NB)])

            def heads(first, todo):
                for i in range(len(todo) + 2):
                    if i < len(todo):
                        h = first + i
                        kind, qt, kt_, r = todo[i][:4]
                        if i >= 2:
                            pe.wait_ge(s_exp, h - 1)
                        for b in range(NB):
                            o = bank[i % 2][:, b * S:(b + 1) * S]
                            mm = pe.matmul(o, qT[r:r + HD, qt, b * P:(b + 1) * P], kT[r:r + HD, kt_, :],
                                           start=True, stop=kind is None)
                            if kind is not None:
                                mm = pe.matmul(o, ident_r[:], mask_r[:, kind, b, :], start=False, stop=True)
                        mm.then_inc(s_psum, 1)
                    if 1 <= i <= len(todo):
                        h = first + i - 1
                        pe.wait_ge(s_exp, h + 1)
                        if i - 1 >= 2:
                            pe.wait_ge(p_sb, h - 1)
                        for b in range(NB):
                            for kt in range(NB):
                                mm = pe.transpose(bank[2 + (i - 1) % 2][:, (kt * NB + b) * P:(kt * NB + b + 1) * P],
                                                  pr[:, (i - 1) % 2, b, kt * P:(kt + 1) * P], ident[:])
                        mm.then_inc(p_psum, 1)
                    if i >= 2:
                        h = first + i - 2
                        v, vc = todo[i - 2][4:6]
                        pe.wait_ge(p_sb, h + 1)
                        if i - 2 >= 2:
                            pe.wait_ge(o_sb, 2 * (h - 1))
                        for b in range(NB):
                            for kt in range(NB):
                                mm = pe.matmul(bank[4 + (i - 2) % 2][:, b * HD:(b + 1) * HD],
                                               pT[:, (i - 2) % 2, kt, b * P:(b + 1) * P],
                                               v[:, kt, vc:vc + HD], start=kt == 0, stop=kt == NB - 1)
                        mm.then_inc(o_psum, 1)

            pe.wait_ge(const_in, 16 * len(LOADS["const"]))
            norm_t("norm1", 0)
            jobs("in0", [512] * 5)
            t = at["conv0"]["t"]
            pe.wait_ge(j_act, plain_jobs(at["in0"]["j"] + 4))
            pe.wait_ge(j_dve, plain_jobs(at["in0"]["j"] + 4))
            for k in range(4):
                cols_t(t + k, proj0, [1536 + 256 * k, 1536 + 256 * k + P])
            pe.wait_ge(qk_made, 2)
            t = at["qk0"]["t"]
            for k in range(4):
                cols_t(t + k, proj0, [256 * k, 256 * k + P])
            pe.wait_ge(t_act, act_steps(t + 3))
            pe.wait_ge(mask_made, 2)
            heads(at["heads0"]["h"], HEADS0)
            pe.wait_ge(m_made, 1)
            pe.wait_ge(s_exp, at["heads0"]["h"] + REL_HEADS)
            for k in range(2):
                mm = pe.matmul(bank[0][:, k * S:(k + 1) * S], pool_w[:, k, :], mT[:, k, :], start=True, stop=True)
            mm.then_inc(pool_psum, 1)
            pe.wait_ge(o_sb, 2 * (at["heads0"]["h"] + REL_HEADS))
            for k in range(2):
                cols_t(at["mix0"]["t"] + k, mix, [256 * k, 256 * k + P])
            pe.wait_ge(t_dve, dve_steps(at["mix0"]["t"] + 1))
            pe.wait_ge(cp_lo, 2)
            jobs("out0", [512] * 2)
            norm_t("norm2", 1)

            def f_tile(buf):
                return lambda p, kt, b: (f_hi, f_lo)[p][:, buf, kt, b * P:(b + 1) * P]

            accs = [[bank[2 * b + h][:] for h in range(2)] for b in range(NB)]

            g, t = at["ff0"]["g"], at["ff0"]["t"]
            for c in range(FF0_CHUNKS + 1):
                ups = [bank[4 + b][:] for b in range(NB)]
                if c < FF0_CHUNKS:
                    if c >= 1:
                        pe.wait_ge(f_made, 2 * c)
                    pe.wait_ge(lo_made, g + 1)
                    across(g, 512, a_tile, 0, ups, True, False)
                    g += 1
                if c >= 1:
                    pe.wait_ge(f_made, 2 * c)
                    for k in range(2):
                        tstep(t, [f_sb[:, (c - 1) % 2, b, kt * P:(kt + 1) * P] for kt in (2 * k, 2 * k + 1)
                                  for b in range(NB)])
                        t += 1
                if c < FF0_CHUNKS:
                    pe.wait_ge(lo_made, g + 1)
                    across(g, 512, a_tile, 4, ups, False, True)
                    g += 1
                if c >= 1:
                    pe.wait_ge(t_dve, dve_steps(t - 1))
                    if c == 1:
                        pe.wait_ge(x_upd, at_x["ff0"])
                    for k in range(2):
                        pe.wait_ge(lo_made, g + 1)
                        down(g, f_tile((c - 1) % 2), 2 * k, accs, c == 1 and k == 0, c == FF0_CHUNKS and k == 1)
                        g += 1

            norm_t("nmix0", NMIX0)
            jobs("in1", [n for _, n in FOX_JOBS])
            norm_t("nmem0", NMEM0)
            jobs("mem0", [512])
            pe.wait_ge(lf_made, 1)
            for b in range(NB):
                for s in range(b + 1):
                    mm = pe.matmul(bank[4][:, b * FOX_HEADS:(b + 1) * FOX_HEADS],
                                   negtri[:, s, b * P:(b + 1) * P], lf[:, 3, s, :], start=s == 0, stop=s == b)
            mm.then_inc(c_psum, 1)
            for k in range(FOX_HEADS // 2):
                bk = bank[4 + (k + 1) % 2]
                if k >= 2:
                    pe.wait_ge(dec_sb, k - 1)
                if k == 1:
                    pe.wait_ge(c_sb, 1)
                for hh in range(2):
                    for s in range(NB):
                        mm = pe.matmul(bk[:, hh * S:(hh + 1) * S],
                                       bcast(lf[:, 3, s, 2 * k + hh], P), negtri[:, s, :],
                                       start=s == 0, stop=s == 1)
                mm.then_inc(dec_psum, 1)
            t = at["qk1"]["t"]
            pe.wait_ge(qk_made, 4)
            for k in range(6):
                cols_t(t + k, proj1, [256 * k, 256 * k + P])
            pe.wait_ge(qk_made, 6)
            cols_t(t + 6, proj1, [MQ1, MQ1 + P])
            cols_t(t + 7, kvm1, [0, P])
            pe.wait_ge(t_act, act_steps(t + 7))
            pe.wait_ge(dec_sb, FOX_HEADS // 2)
            heads(at["heads1"]["h"], HEADS1)
            pe.wait_ge(o_sb, 2 * (at["heads1"]["h"] + len(HEADS1)))
            for k in range(4):
                cols_t(at["mix1"]["t"] + k, mix, [256 * k, 256 * k + P])
            pe.wait_ge(t_dve, dve_steps(at["mix1"]["t"] + 3))
            jobs("out1", [512] * 2)
            norm_t("nffn0", 4)

            g, t = at["ff1"]["g"], at["ff1"]["t"]
            for c in range(FF1_CHUNKS + 1):
                ups = [bank[4 + b][:] for b in range(NB)]
                if c < FF1_CHUNKS:
                    if c >= 1:
                        pe.wait_ge(h_made, 2 * c)
                    pe.wait_ge(lo_made, g + 1)
                    across(g, 512, a_tile, 0, ups, True, False)
                    g += 1
                if c >= 1:
                    pe.wait_ge(h_made, 2 * c)
                    tstep(t, [f_sb[:, (c - 1) % 2, b, kt * P:(kt + 1) * P] for kt in range(2) for b in range(NB)])
                    t += 1
                if c < FF1_CHUNKS:
                    pe.wait_ge(lo_made, g + 1)
                    across(g, 512, a_tile, 4, ups, False, True)
                    g += 1
                if c >= 1:
                    pe.wait_ge(t_dve, dve_steps(t - 1))
                    if c == 1:
                        pe.wait_ge(x_upd, at_x["ff1"])
                    pe.wait_ge(lo_made, g + 1)
                    down(g, f_tile((c - 1) % 2), 0, accs, c == 1, c == FF1_CHUNKS)
                    g += 1

            norm_t("nmix1", NMIX1)
            jobs("in2", [n for _, n in CONV_JOBS])
            norm_t("nmem1", NMEM1)
            jobs("mem1", [512])
            t = at["glu"]["t"]
            pe.wait_ge(j_act, plain_jobs(at["in2"]["j"] + 3))
            pe.wait_ge(j_dve, plain_jobs(at["in2"]["j"] + 3))
            for k in range(3):
                cols_t(t + 2 * k, proj2, [768 + 256 * k, 768 + 256 * k + P])
                cols_t(t + 2 * k + 1, proj2, [256 * k, 256 * k + P])
            pe.wait_ge(qk_made, 8)
            t = at["qk2"]["t"]
            cols_t(t, proj2, [MQ2, MQ2 + P])
            cols_t(t + 1, kvm2, [0, P])
            pe.wait_ge(t_act, act_steps(t + 1))
            heads(at["heads2"]["h"], HEADS2)
            pe.wait_ge(dw_made, 1)
            pe.wait_ge(o_sb, 2 * (at["heads2"]["h"] + len(HEADS2)))
            for k in range(CONV_TILES):
                mm = pe.matmul(bank[0][:, 0:S], onesm[:], dwy[:, k, :], start=k == 0, stop=k == CONV_TILES - 1)
            mm.then_inc(mu_psum, 1)
            cols_t(at["mix2"]["t"], mix, [768, 768 + P])
            pe.wait_ge(sqc_made, 1)
            for k in range(CONV_TILES):
                mm = pe.matmul(bank[1][:, 0:S], onesm[:], dwq[:, k, :], start=k == 0, stop=k == CONV_TILES - 1)
            mm.then_inc(var_psum, 1)
            pe.wait_ge(t_dve, dve_steps(at["mix2"]["t"]))
            pe.wait_ge(ln_lo, 1)
            jobs("out2", [512] * 2)
            norm_t("nffn1", 7)

            pe.wait_ge(moe_in, 16 * len(LOADS["moe"]))
            for b in range(NB):
                for kt in range(KT):
                    for part in range(2):
                        mm = pe.matmul(bank[4][:, b * N_EXPERTS:(b + 1) * N_EXPERTS],
                                       a_tile(part, kt, b).bitcast(F32), router[:, kt, :],
                                       start=kt == 0 and part == 0, stop=kt == KT - 1 and part == 1)
            mm.then_inc(r_psum, 1)
            pe.wait_ge(ch_made, 1)
            for b in range(NB):
                for s in range(b + 1):
                    pe.matmul(bank[5][:, b * N_EXPERTS:(b + 1) * N_EXPERTS],
                              negtri[:, s, b * P:(b + 1) * P], chosen[:, s, :], start=s == 0, stop=s == b)
            for s in range(NB):
                mm = pe.matmul(bank[5][:, 16:24], negtri[:, 0, P:S], chosen[:, s, :], start=s == 0, stop=s == 1)
            mm.then_inc(rk_psum, 1)

            def xg_tile(part, kt, b):
                return (xg_hi, xg_lo)[part][:, kt, :]

            pe.wait_ge(x_upd, at_x["moe"])
            pe.wait_ge(items_made, 1)
            items = pe.value_load(n_items[0:1, 0:1], min_val=N_EXPERTS, max_val=2 * N_EXPERTS)
            with pe.Fori(0, items) as i:
                def t_free(k):
                    pe.wait_ge(t_dve, i * MOE_TSTEPS + (TD + k - 1))

                def w_ready(k):
                    pe.wait_ge(lo_made, i * MOE_GRANULES + (NG + k + 1))

                pe.wait_ge(pick_made, i + 1)
                for k in range(2):
                    t_free(k)
                    for kk in range(4):
                        kt = 4 * k + kk
                        for b in range(NB):
                            mm = pe.matmul(bank[6 + (TM + k) % 2][:, kk * P:(kk + 1) * P],
                                           xn[:, b, kt * P:(kt + 1) * P], pick[:, b, :],
                                           start=b == 0, stop=b == NB - 1)
                    mm.then_inc(t_psum, 1)
                t_free(2)
                for b in range(NB):
                    mm = pe.transpose(bank[6 + TM % 2][:, b * P:(b + 1) * P], pickg[:, b, :], ident[:])
                mm.then_inc(t_psum, 1)
                pe.wait_ge(t_dve, i * MOE_TSTEPS + (TD + 2))
                for c in range(MOE_CHUNKS + 1):
                    k = moe_first(c)
                    gb, ub = (bank[4], bank[5]) if c % 2 == 0 else (bank[2], bank[3])
                    if c < MOE_CHUNKS:
                        if c == 0:
                            pe.wait_ge(x_upd, i * 4 + at_x["moe"])
                        if c >= 2:
                            pe.wait_ge(h_made, i * MOE_CHUNKS + (HM + c - 1))
                        for half in range(2):
                            w_ready(k)
                            across(NG + k, 512, xg_tile, 4 * half, [gb[:]], half == 0, half == 1)
                            k += 1
                    if c >= 1:
                        pe.wait_ge(h_made, i * MOE_CHUNKS + (HM + c))
                        t_free(2 + c)
                        for kt in range(4):
                            mm = pe.transpose(bank[6 + (TM + 2 + c) % 2][:, kt * P:(kt + 1) * P],
                                              mf_sb[:, (c - 1) % 2, 1, kt * P:(kt + 1) * P], ident[:])
                        mm.then_inc(t_psum, 1)
                    if c < MOE_CHUNKS:
                        for half in range(2):
                            w_ready(k)
                            across(NG + k, 512, xg_tile, 4 * half, [ub[:]], half == 0, half == 1)
                            k += 1
                    if c >= 1:
                        pe.wait_ge(t_dve, i * MOE_TSTEPS + (TD + 3 + c))
                        for half in range(2):
                            w_ready(k)
                            down(NG + k, lambda p, kt, b: (mf_hi, mf_lo)[p][:, (c - 1) % 2, kt, :], 2 * half,
                                 [[bank[0][:], bank[1][:]]], c == 1 and half == 0, c == MOE_CHUNKS and half == 1)
                            k += 1
                pe.wait_ge(y_act, i + 1)
                pe.wait_ge(y_dve, i + 1)
                for b in range(NB):
                    for half in range(2):
                        pe.matmul(bank[2 + 2 * b + half][:], pickgT[:, b * P:(b + 1) * P],
                                  y_sb[:, half * 512:(half + 1) * 512], start=True, stop=True).then_inc(sc_psum, 1)

        @block.scalar
        def _(act):
            own = [0]
            done = [0]

            def chained(ins):
                own[0] += 1
                ins.then_inc(act_own, 1)
                act.wait_ge(act_own, own[0])

            def hi(g):
                act.wait_ge(raw_in[g % NRAW], raw_count[g])
                if g >= NSPLIT:
                    act.wait_ge(w_used, g - NSPLIT + 1)
                n = n_el(g)
                act.activation(w_hi[:, g % NSPLIT, 0:n], raw_at(g, n), ACT.Copy).then_inc(hi_made, 1)

            def hi_to(g):
                while done[0] <= min(g, NG - 1):
                    hi(done[0])
                    done[0] += 1

            def t_hi(t, dst, scales=(1.0, 1.0)):
                act.wait_ge(t_psum, t + 1)
                src = bank[6 + t % 2]
                if scales[0] == 1.0:
                    act.activation(dst, src[:].rearrange("p (k s) -> p k s", k=2), ACT.Copy).then_inc(t_act, 1)
                else:
                    act.activation(dst[:, 0, :], src[:, 0:S], ACT.Copy, scale=scales[0])
                    act.activation(dst[:, 1, :], src[:, S:2 * S], ACT.Copy, scale=scales[1]).then_inc(t_act, 1)

            def squares(n, src):
                if n >= 1:
                    act.wait_ge(t_psum, last_t_of_norm(n - 1) + 1)
                for b in range(NB):
                    act.activation(xn[:, b, :], src[:, b, :], ACT.Square, accum_out=ss[:, n, b:b + 1])\
                        .then_inc(ss_made, 1)

            def norm_hi(name, n, gains=True):
                t = at[name]["t"]
                if at[name]["g"]:
                    act.wait_ge(w_used, at[name]["g"])
                for s in range(4):
                    scales = [gcol[:, n, 2 * s + k:2 * s + k + 1] for k in range(2)] if gains else (1.0, 1.0)
                    t_hi(t + s, a_hi[:, 2 * s:2 * s + 2, :], scales)

            def copy_out(j, g_end, dst):
                act.wait_ge(w_used, g_end + 1)
                act.activation(dst, bank[2 * (j % 2)][:, 0:dst.shape[-1]], ACT.Copy).then_inc(j_act, 1)

            def exps(first, todo):
                for i in range(len(todo) + 1):
                    h = first + i
                    if i < len(todo):
                        act.wait_ge(s_max, h + 1)
                        if i >= 2:
                            act.wait_ge(p_psum, h - 1)
                        if i >= 2:
                            act.wait_ge(o_sb, 2 * (h - 1))
                        for b in range(NB):
                            src = bank[i % 2][:, b * S:(b + 1) * S] if todo[i][0] is None else sc[:, i % 2, b, :]
                            ins = act.activation(pr[:, i % 2, b, :], src, ACT.Exp, bias=nmax[:, i % 2, b:b + 1],
                                                 accum_out=psumr[:, i % 2, b:b + 1])
                        ins.then_inc(s_exp, 1)
                    if i >= 1:
                        act.wait_ge(p_psum, h)
                        if i - 1 >= 2:
                            act.wait_ge(o_psum, h - 2)
                        act.activation(pT[:, (i - 1) % 2, :, :],
                                       bank[2 + (i - 1) % 2][:].rearrange("p (k s) -> p k s", k=NB), ACT.Copy)\
                            .then_inc(p_sb, 1)

            def square_heads(src, c0, nh):
                act.activation(mix[:, :, 0:nh * HD], src[:, :, c0:c0 + nh * HD], ACT.Square).then_inc(sq_made, 1)

            def root_heads(q, nh):
                act.wait_ge(qss_made, q + 1)
                act.activation(qss[:, 1, 0:NB * nh], qss[:, 0, 0:NB * nh], ACT.Sqrt, scale=1.0 / HD, bias=eps[:])\
                    .then_inc(qsqrt_made, 1)

            def t_copy(t, dst, gain=None):
                act.wait_ge(t_psum, t + 1)
                src = bank[6 + t % 2][:].rearrange("p (k s) -> p k s", k=2)
                if gain is None:
                    act.activation(dst, src, ACT.Copy).then_inc(t_act, 1)
                else:
                    act.activation(dst, src, ACT.Copy, scale=hcol[:, gain:gain + 1]).then_inc(t_act, 1)

            for dst, src in LOADS["const"]:
                act.dma_start(dst, src).then_inc(const_in, 16)
            act.wait_ge(x_in, 16)
            squares(0, x)
            act.dma_start(rel_row[:, 127:127 + 257], a["rel_bias"]).then_inc(rel_in, 16)
            for dst, src in LOADS["early"]:
                act.dma_start(dst, src).then_inc(early_in, 16)
            act.wait_ge(pool_zero, 1)
            for gr in range(4):
                r = (gr % 2) * HD
                act.dma_start(pool_w[r:r + HD, gr // 2, r:r + HD], a["pool_w"][0, gr]).then_inc(early_in, 16)
            hi_to(2)
            act.wait_ge(const_in, 16 * len(LOADS["const"]))
            norm_hi("norm1", 0)
            act.activation(ident_r[:], ident[:], ACT.Copy).then_inc(mask_made, 1)
            act.activation(mask_r[:], pr[:], ACT.Copy).then_inc(mask_made, 1)
            act.wait_ge(rel_ext, 1)
            act.dma_start(rel_rows_dram, rel_row[:]).then_inc(rel_out, 16)
            act.wait_ge(rel_out, 16)
            act.dma_start(rel_band_dram, bass.AP(rel_rows_dram.tensor, P - 1, [[REL_LEN + 1, REL_HEADS], [-1, P], [1, 384]]))\
                .then_inc(rel_band, 16)
            act.wait_ge(rel_band, 16)
            act.dma_start(relT[:], rel_band_dram.rearrange("h p m -> p h m")).then_inc(rel_back, 16)
            for k in range(5):
                g_end = at["in0"]["g"] + 2 * k + 1
                hi_to(g_end + 2)
                copy_out(at["in0"]["j"] + k, g_end, proj0[:, 0, 512 * k:512 * (k + 1)])
                if k == 1:
                    act.wait_ge(j_act, plain_jobs(at["in0"]["j"] + 1))
                    act.wait_ge(j_dve, plain_jobs(at["in0"]["j"] + 1))
                    square_heads(proj0, 0, REL_HEADS)
                if k == 2:
                    root_heads(0, REL_HEADS)
                    act.wait_ge(qss_made, 1)
                    square_heads(proj0, 512, REL_HEADS)
                if k == 3:
                    root_heads(1, REL_HEADS)
            hi_to(at["out0"]["g"] + 2)
            t = at["conv0"]["t"]
            for k, dst in enumerate((gbT, gcT, hiT, uT[:, :, 16:16 + S])):
                t_copy(t + k, dst)
            t = at["qk0"]["t"]
            for k in range(4):
                t_copy(t + k, (qT, kT)[k // 2][:, 2 * (k % 2):2 * (k % 2) + 2, :], (GQ0, GK0)[k // 2])
            exps(at["heads0"]["h"], HEADS0)
            act.wait_ge(w_used, at["out0"]["g"])
            act.wait_ge(y_made, 1)
            act.activation(a_hi[:, 4:6, :], yT[:], ACT.Copy).then_inc(cp_hi, 1)
            act.wait_ge(pool_psum, 1)
            act.activation(a_hi[:, 6, :], bank[0][:, 0:S], ACT.Copy, scale=pscale[:, 0:1])
            act.activation(a_hi[:, 7, :], bank[0][:, S:2 * S], ACT.Copy, scale=pscale[:, 1:2]).then_inc(cp_hi, 1)
            for k in range(2):
                t_hi(at["mix0"]["t"] + k, a_hi[:, 2 * k:2 * k + 2, :])
            g = at["ff0"]["g"]
            hi_to(g + 2)
            act.wait_ge(x_upd, at_x["ff0"])
            squares(1, x)
            norm_hi("norm2", 1)
            t = at["ff0"]["t"]
            for c in range(FF0_CHUNKS + 1):
                first = g + (0 if c == 0 else 2 + 4 * (c - 1))
                if c >= 1:
                    hi_to(first + 2)
                    for k in range(2):
                        t_hi(t, f_hi[:, (c - 1) % 2, 2 * k:2 * k + 2, :])
                        t += 1
                if c < FF0_CHUNKS:
                    hi_to(first + 3)
                    act.wait_ge(w_used, first + 2)
                    for b in range(NB):
                        f = f_sb[:, c % 2, b, :]
                        chained(act.activation(f, bank[4 + b][:], ACT.Relu))
                        act.activation(f, f, ACT.Square).then_inc(f_made, 1)
            hi_to(at["in1"]["g"] + 2)
            act.wait_ge(x_upd, at_x["nmix0"])
            squares(NMIX0, x)
            act.dma_start(mem1[:], tokens(a["mem_2"][0])).then_inc(mem_in, 16)
            for dst, src in LOADS["l1"]:
                act.dma_start(dst, src).then_inc(l1_in, 16)
            norm_hi("nmix0", NMIX0)
            act.wait_ge(mem_in, 16)
            squares(NMEM0, mem1)
            for k, (c0, n) in enumerate(FOX_JOBS):
                g_end = at["in1"]["g"] + 2 * k + 1
                hi_to(g_end + 2)
                copy_out(at["in1"]["j"] + k, g_end, proj1[:, 0, c0:c0 + n])
                if k == 1:
                    act.wait_ge(lf_x, 1)
                    chained(act.activation(lf[:, 1], lf[:, 1], ACT.Exp, scale=-1.0))
                    act.activation(lf[:, 2], lf[:, 1], ACT.Ln, bias=1.0).then_inc(lf_ln, 1)
                if k == 2:
                    act.wait_ge(j_act, plain_jobs(at["in1"]["j"] + 2))
                    act.wait_ge(j_dve, plain_jobs(at["in1"]["j"] + 2))
                    square_heads(proj1, 0, FOX_HEADS)
                if k == 4:
                    root_heads(2, FOX_HEADS)
                    act.wait_ge(j_act, plain_jobs(at["in1"]["j"] + 4))
                    act.wait_ge(j_dve, plain_jobs(at["in1"]["j"] + 4))
                    square_heads(proj1, FOXW, FOX_HEADS)
                if k == 5:
                    root_heads(3, FOX_HEADS)
            hi_to(at["mem0"]["g"] + 1)
            norm_hi("nmem0", NMEM0)
            copy_out(at["mem0"]["j"], at["mem0"]["g"] + 1, kvm1[:, 0, :])
            for k in range(FOX_HEADS // 2):
                act.wait_ge(dec_psum, k + 1)
                act.activation(decay[:, 2 * k:2 * k + 2, :], bank[4 + (k + 1) % 2][:].rearrange("p (k s) -> p k s", k=2),
                               ACT.Copy).then_inc(dec_sb, 1)
            hi_to(at["out1"]["g"] + 2)
            act.wait_ge(j_act, plain_jobs(at["mem0"]["j"]))
            act.wait_ge(j_dve, plain_jobs(at["mem0"]["j"]))
            square_heads(proj1, MQ1, MEM_HEADS)
            root_heads(4, MEM_HEADS)
            square_heads(kvm1, 0, MEM_HEADS)
            root_heads(5, MEM_HEADS)
            t = at["qk1"]["t"]
            for k in range(6):
                t_copy(t + k, (qT, kT)[k // 3][:, 2 * (k % 3):2 * (k % 3) + 2, :], (GFQ, GFK)[k // 3])
            t_copy(t + 6, memq[:], GMQ0)
            t_copy(t + 7, memk[:], GMK0)
            exps(at["heads1"]["h"], HEADS1)
            act.wait_ge(w_used, at["out1"]["g"])
            for k in range(4):
                t_hi(at["mix1"]["t"] + k, a_hi[:, 2 * k:2 * k + 2, :])
            g = at["ff1"]["g"]
            hi_to(g + 2)
            act.wait_ge(x_upd, at_x["ff1"])
            squares(4, x)
            norm_hi("nffn0", 4)
            t = at["ff1"]["t"]
            for c in range(FF1_CHUNKS + 1):
                first = g + (0 if c == 0 else 2 + 3 * (c - 1))
                if c >= 1:
                    hi_to(first + 2)
                    t_hi(t, f_hi[:, (c - 1) % 2, 0:2, :])
                    t += 1
                if c < FF1_CHUNKS:
                    hi_to(first + 3)
                    act.wait_ge(w_used, first + 2)
                    for b in range(NB):
                        act.activation(f_sb[:, c % 2, b, 256:512], bank[4 + b][:, 0:256], ACT.Silu).then_inc(silu_made, 1)
            hi_to(at["in2"]["g"] + 2)
            act.wait_ge(x_upd, at_x["nmix1"])
            squares(NMIX1, x)
            act.dma_start(mem2[:], tokens(a["mem_2"][0])).then_inc(mem_in, 16)
            for dst, src in LOADS["l2"]:
                act.dma_start(dst, src).then_inc(l2_in, 16)
            norm_hi("nmix1", NMIX1)
            act.wait_ge(mem_in, 32)
            squares(NMEM1, mem2)
            for k, (c0, n) in enumerate(CONV_JOBS):
                g_end = at["in2"]["g"] + 2 * k + 1
                hi_to(g_end + 2)
                copy_out(at["in2"]["j"] + k, g_end, proj2[:, 0, c0:c0 + n])
            hi_to(at["mem1"]["g"] + 1)
            norm_hi("nmem1", NMEM1)
            copy_out(at["mem1"]["j"], at["mem1"]["g"] + 1, kvm2[:, 0, :])
            act.wait_ge(j_act, plain_jobs(at["mem1"]["j"]))
            act.wait_ge(j_dve, plain_jobs(at["mem1"]["j"]))
            square_heads(proj2, MQ2, MEM_HEADS)
            root_heads(6, MEM_HEADS)
            square_heads(kvm2, 0, MEM_HEADS)
            root_heads(7, MEM_HEADS)
            hi_to(at["out2"]["g"] + 2)
            t = at["glu"]["t"]
            act.wait_ge(l2_in, 16 * len(LOADS["l2"]))
            for k in range(3):
                act.wait_ge(t_psum, t + 2 * k + 1)
                if k >= 1:
                    act.wait_ge(t_dve, dve_steps(t + 2 * k - 1))
                for m in range(2):
                    ch = CONV_TILES + 2 * k + m
                    ins = act.activation(sig[:, m, :], bank[6 + (t + 2 * k) % 2][:, m * S:(m + 1) * S], ACT.Sigmoid,
                                         bias=cb_in[:, ch:ch + 1])
                ins.then_inc(t_act, 1)
            t = at["qk2"]["t"]
            t_copy(t, memq[:], GMQ1)
            t_copy(t + 1, memk[:], GMK1)
            exps(at["heads2"]["h"], HEADS2)
            act.wait_ge(w_used, at["out2"]["g"])
            t_hi(at["mix2"]["t"], a_hi[:, 6:8, :])
            act.wait_ge(cent_made, 1)
            act.activation(dwq[:], dwy[:], ACT.Square).then_inc(sqc_made, 1)
            act.wait_ge(var_psum, 1)
            act.activation(stat[:, 1, :], bank[1][:, 0:S], ACT.Sqrt, bias=eps[:]).then_inc(sd_made, 1)
            act.wait_ge(ln_made, 1)
            for k in range(CONV_TILES):
                ins = act.activation(dwq[:, k, :], dwy[:, k, :], ACT.Silu, scale=lng[:, k:k + 1], bias=lnb[:, k:k + 1])
            ins.then_inc(silu2, 1)
            act.wait_ge(silu2, 1)
            act.activation(a_hi[:, 0:CONV_TILES, :], dwq[:], ACT.Copy).then_inc(ln_hi, 1)
            hi_to(NG - 1)
            act.wait_ge(x_upd, at_x["moe"])
            squares(7, x)
            for dst, src in LOADS["moe"]:
                act.dma_start(dst, src).then_inc(moe_in, 16)
            norm_hi("nffn1", 7, gains=False)
            act.wait_ge(z_made, 1)
            act.activation(gate[:, 1, :], gate[:, 0, :], ACT.Exp).then_inc(g_exp, 1)
            act.wait_ge(items_made, 1)
            items = act.value_load(n_items[0:1, 0:1], min_val=N_EXPERTS, max_val=2 * N_EXPERTS)
            with act.Fori(0, items) as i:
                def e_hi(k):
                    g = NG + k
                    act.wait_ge(raw_in[g % NRAW], i * (16 * (MOE_GRANULES // NRAW)) + (seen[g % NRAW] + 16 * (1 + (k // NRAW))))
                    act.wait_ge(w_used, i * MOE_GRANULES + (g - NSPLIT + 1))
                    act.activation(w_hi[:, g % NSPLIT, :], raw_at(g, GRAN), ACT.Copy).then_inc(hi_made, 1)

                def step_in(k):
                    act.wait_ge(t_psum, i * MOE_TSTEPS + (TM + k + 1))

                for k in range(3):
                    e_hi(k)
                for k in range(2):
                    step_in(k)
                    act.activation(xg_hi[:, 4 * k:4 * k + 4, :],
                                   bank[6 + (TM + k) % 2][:].rearrange("p (k s) -> p k s", k=4), ACT.Copy).then_inc(t_act, 1)
                step_in(2)
                act.activation(pickgT[:, 0:P], bank[6 + TM % 2][:, 0:P], ACT.Copy).then_inc(t_act, 1)
                k = 3
                for c in range(MOE_CHUNKS + 1):
                    while k <= min(moe_first(c) + (3 if c < MOE_CHUNKS else 1), MOE_GRANULES - 1):
                        e_hi(k)
                        k += 1
                    if c >= 1:
                        step_in(2 + c)
                        act.activation(mf_hi[:, (c - 1) % 2, :, :],
                                       bank[6 + (TM + 2 + c) % 2][:].rearrange("p (k s) -> p k s", k=4), ACT.Copy)\
                            .then_inc(t_act, 1)
                    if c < MOE_CHUNKS:
                        act.wait_ge(w_used, i * MOE_GRANULES + (NG + moe_first(c) + 2))
                        gb = bank[4] if c % 2 == 0 else bank[2]
                        act.activation(mf_sb[:, c % 2, 0, :], gb[:], ACT.Silu).then_inc(silu_made, 1)
                act.wait_ge(w_used, i * MOE_GRANULES + (NG + MOE_GRANULES))
                act.activation(y_sb[:, 0:512], bank[0][:], ACT.Copy).then_inc(y_act, 1)

        @block.vector
        def _(dve):
            own = [0]
            done = [0]

            def chained(ins):
                own[0] += 1
                ins.then_inc(dve_own, 1)
                dve.wait_ge(dve_own, own[0])

            def lo(g):
                dve.wait_ge(hi_made, g + 1)
                n = n_el(g)
                dve.tensor_tensor(w_lo[:, g % NSPLIT, 0:n], raw_at(g, n), w_hi[:, g % NSPLIT, 0:n].bitcast(F32),
                                  ALU.subtract).then_inc(lo_made, 1)

            def lo_to(g):
                while done[0] <= min(g, NG - 1):
                    lo(done[0])
                    done[0] += 1

            def t_lo(t, dst, hi_part, scales=(1.0, 1.0)):
                dve.wait_ge(t_act, act_steps(t))
                src = bank[6 + t % 2]
                if scales[0] == 1.0:
                    dve.tensor_tensor(dst, src[:].rearrange("p (k s) -> p k s", k=2), hi_part.bitcast(F32),
                                      ALU.subtract).then_inc(t_dve, 1)
                else:
                    for k in range(2):
                        ins = dve.scalar_tensor_tensor(dst[:, k, :], src[:, k * S:(k + 1) * S], scales[k],
                                                       hi_part[:, k, :].bitcast(F32), ALU.mult, ALU.subtract)
                    ins.then_inc(t_dve, 1)

            def normed(n, src):
                dve.wait_ge(rstd_made, n + 1)
                for b in range(NB):
                    dve.tensor_scalar(xn[:, b, :], src[:, b, :], rstd[:, n, b:b + 1], None, ALU.mult).then_inc(xn_made, 1)

            def norm_lo(name, n, gains=True):
                t = at[name]["t"]
                for s in range(4):
                    scales = [gcol[:, n, 2 * s + k:2 * s + k + 1] for k in range(2)] if gains else (1.0, 1.0)
                    t_lo(t + s, a_lo[:, 2 * s:2 * s + 2, :], a_hi[:, 2 * s:2 * s + 2, :], scales)

            def copy_out(j, g_end, dst):
                dve.wait_ge(w_used, g_end + 1)
                dve.tensor_copy(dst, bank[2 * (j % 2) + 1][:, 0:dst.shape[-1]]).then_inc(j_dve, 1)

            def add_out(name):
                for k in range(2):
                    j, g_end = at[name]["j"] + k, at[name]["g"] + 2 * k + 1
                    lo_to(g_end + 3)
                    dve.wait_ge(w_used, g_end + 1)
                    for b in range(NB):
                        xs = x[:, b, k * 512:(k + 1) * 512]
                        dve.tensor_tensor(xs, xs, bank[2 * (j % 2) + b][:], ALU.add).then_inc(x_upd, 1)

            def add_acc(g_end):
                dve.wait_ge(w_used, g_end + 1)
                for b in range(NB):
                    for h in range(2):
                        xs = x[:, b, h * 512:(h + 1) * 512]
                        dve.tensor_tensor(xs, xs, bank[2 * b + h][:], ALU.add).then_inc(x_upd, 1)

            def sum_heads(q, nh):
                dve.wait_ge(sq_made, q + 1)
                for b in range(NB):
                    ins = dve.tensor_reduce(qss[:, 0, b * nh:(b + 1) * nh],
                                            mix[:, b, 0:nh * HD].rearrange("p (h d) -> p h d", d=HD), AX_X, ALU.add)
                ins.then_inc(qss_made, 1)

            def scale_heads(q, src, c0, nh):
                dve.wait_ge(qsqrt_made, q + 1)
                chained(dve.reciprocal(qss[:, 1, 0:NB * nh], qss[:, 1, 0:NB * nh]))
                for b in range(NB):
                    v = src[:, b, c0:c0 + nh * HD].rearrange("p (h d) -> p h d", d=HD)
                    ins = dve.tensor_tensor(v, v, bcast(qss[:, 1, b * nh:(b + 1) * nh], HD), ALU.mult)
                ins.then_inc(qk_made, 1)

            def softmax_sides(first, todo, mixcol):
                for i in range(len(todo) + 2):
                    if i < len(todo):
                        h = first + i
                        kind, hh = todo[i][0], todo[i][6]
                        dve.wait_ge(s_psum, h + 1)
                        if i >= 2:
                            dve.wait_ge(s_exp, h - 1)
                        src = bank[i % 2][:].rearrange("p (b s) -> p b s", b=NB)
                        if kind == 0:
                            for b in range(NB):
                                c0 = P * (1 - b)
                                ins = dve.tensor_tensor(sc[:, i % 2, b, :], src[:, b, :], relT[:, hh, c0:c0 + S], ALU.add)
                            ins.then_inc(s_sb, 1)
                            dve.wait_ge(s_sb, h + 1)
                            src = sc[:, i % 2, :, :]
                        elif kind == 1:
                            for b in range(NB):
                                ins = dve.scalar_tensor_tensor(sc[:, i % 2, b, :], src[:, b, :], negc[:, b, hh:hh + 1],
                                                               decay[:, hh, :], ALU.subtract, ALU.add)
                            ins.then_inc(s_sb, 1)
                            dve.wait_ge(s_sb, h + 1)
                            src = sc[:, i % 2, :, :]
                        dve.tensor_reduce(nmax[:, i % 2, :], src, AX_X, ALU.max, negate=True).then_inc(s_max, 1)
                    if i >= 2:
                        h, k = first + i - 2, (i - 2) % 2
                        dve.wait_ge(s_exp, h + 1)
                        chained(dve.reciprocal(rinv[:, k, :], psumr[:, k, :]))
                        dve.wait_ge(o_psum, h + 1)
                        for b in range(NB):
                            c0 = mixcol + (i - 2) * HD
                            dve.tensor_scalar(mix[:, b, c0:c0 + HD], bank[4 + k][:, b * HD:(b + 1) * HD],
                                              rinv[:, k, b:b + 1], None, ALU.mult).then_inc(o_sb, 1)

            chained(dve.memset(eps[:], EPS))
            dve.memset(zT[:], 0.0)
            dve.wait_ge(const_in, 16 * len(LOADS["const"]))
            chained(dve.memset(uT[:], 0.0))
            normed(0, x)
            lo_to(2)
            norm_lo("norm1", 0)
            for i in (GQ0, GFQ, GMQ0, GMQ1):
                ins = dve.tensor_scalar(hcol[:, i:i + 1], hcol[:, i:i + 1], HD ** -0.5, None, ALU.mult)
            chained(ins)
            dve.wait_ge(rel_in, 16)
            dve.tensor_copy(rel_row[:, 0:127], bcast(rel_row[:, 127], 127))
            dve.tensor_copy(rel_row[:, 384:], bcast(rel_row[:, 383], REL_LEN + 1 - 384)).then_inc(rel_ext, 1)
            for k in range(5):
                g_end = at["in0"]["g"] + 2 * k + 1
                lo_to(g_end + 2)
                copy_out(at["in0"]["j"] + k, g_end, proj0[:, 1, 512 * k:512 * (k + 1)])
                if k == 1:
                    sum_heads(0, REL_HEADS)
                if k == 2:
                    scale_heads(0, proj0, 0, REL_HEADS)
                    sum_heads(1, REL_HEADS)
                if k == 3:
                    scale_heads(1, proj0, 512, REL_HEADS)
            lo_to(at["out0"]["g"] + 2)
            dve.wait_ge(rel_back, 16)
            t = at["conv0"]["t"]
            dve.wait_ge(early_in, 16 * (len(LOADS["early"]) + 4))
            dve.wait_ge(t_act, act_steps(t + 3))
            chained(dve.tensor_tensor(zT[:, :, CONV_K - 1:], gcT, hiT, ALU.mult))
            for i in range(CONV_K):
                for k in range(2):
                    z = zT[:, k, i:i + S]
                    if i == 0:
                        ins = dve.tensor_scalar(yT[:, k, :], z, cw[:, k, 0:1], None, ALU.mult)
                    else:
                        ins = dve.scalar_tensor_tensor(yT[:, k, :], z, cw[:, k, i:i + 1], yT[:, k, :], ALU.mult, ALU.add)
                chained(ins)
            dve.tensor_tensor(yT[:], yT[:], gbT, ALU.mult).then_inc(y_made, 1)
            prev = uT
            for n, w in enumerate(POOL_WINDOWS):
                cur = win[:, n % 2]
                before = uT[:] if n == 0 else win[:, (n - 1) % 2]
                lo_i = w - 1
                chained(dve.tensor_tensor(cur[:, :, lo_i:], before[:, :, lo_i:], before[:, :, lo_i - w // 2:S + 16 - w // 2],
                                          ALU.add))
                k, r = n // 2, (n % 2) * HD
                ins = dve.tensor_tensor(mT[r:r + HD, k, :], cur[r:r + HD, k, 16:], invcnt[r:r + HD, k, :], ALU.mult)
            chained(ins)
            dve.tensor_tensor(mT, mT, uT[:, :, 16:], ALU.subtract).then_inc(m_made, 1)
            softmax_sides(at["heads0"]["h"], HEADS0, 0)
            dve.wait_ge(cp_hi, 1)
            dve.tensor_tensor(a_lo[:, 4:6, :], yT[:], a_hi[:, 4:6, :].bitcast(F32), ALU.subtract).then_inc(cp_lo, 1)
            dve.wait_ge(cp_hi, 2)
            for k in range(2):
                ins = dve.scalar_tensor_tensor(a_lo[:, 6 + k, :], bank[0][:, k * S:(k + 1) * S], pscale[:, k:k + 1],
                                               a_hi[:, 6 + k, :].bitcast(F32), ALU.mult, ALU.subtract)
            ins.then_inc(cp_lo, 1)
            for k in range(2):
                t_lo(at["mix0"]["t"] + k, a_lo[:, 2 * k:2 * k + 2, :], a_hi[:, 2 * k:2 * k + 2, :])
            add_out("out0")
            g = at["ff0"]["g"]
            lo_to(g + 2)
            normed(1, x)
            norm_lo("norm2", 1)
            t = at["ff0"]["t"]
            for c in range(FF0_CHUNKS + 1):
                first = g + (0 if c == 0 else 2 + 4 * (c - 1))
                if c >= 1:
                    lo_to(first + 2)
                    for k in range(2):
                        t_lo(t, f_lo[:, (c - 1) % 2, 2 * k:2 * k + 2, :], f_hi[:, (c - 1) % 2, 2 * k:2 * k + 2, :])
                        t += 1
                lo_to(first + (3 if c < FF0_CHUNKS else 1))
            add_acc(at["in1"]["g"] - 1)
            lo_to(at["in1"]["g"] + 2)
            normed(NMIX0, x)
            norm_lo("nmix0", NMIX0)
            normed(NMEM0, mem1)
            for k, (c0, n) in enumerate(FOX_JOBS):
                g_end = at["in1"]["g"] + 2 * k + 1
                lo_to(g_end + 2)
                copy_out(at["in1"]["j"] + k, g_end, proj1[:, 1, c0:c0 + n])
                if k == 0:
                    dve.wait_ge(l1_in, 16)
                    dve.wait_ge(j_act, plain_jobs(at["in1"]["j"]))
                    dve.wait_ge(j_dve, plain_jobs(at["in1"]["j"]))
                    for b in range(NB):
                        ins = dve.tensor_tensor(lf[:, 0, b, :], proj1[:, b, c0:c0 + n], fb[:], ALU.add)
                    chained(ins)
                    dve.scalar_tensor_tensor(lf[:, 1], lf[:, 0], -1.0, lf[:, 0], ALU.mult, ALU.max).then_inc(lf_x, 1)
                if k == 2:
                    dve.wait_ge(lf_ln, 1)
                    dve.scalar_tensor_tensor(lf[:, 3], lf[:, 0], 0.0, lf[:, 2], ALU.min, ALU.subtract).then_inc(lf_made, 1)
                if k == 3:
                    sum_heads(2, FOX_HEADS)
                if k == 4:
                    scale_heads(2, proj1, 0, FOX_HEADS)
                    sum_heads(3, FOX_HEADS)
                if k == 6:
                    scale_heads(3, proj1, FOXW, FOX_HEADS)
            lo_to(at["mem0"]["g"] + 1)
            norm_lo("nmem0", NMEM0)
            copy_out(at["mem0"]["j"], at["mem0"]["g"] + 1, kvm1[:, 1, :])
            dve.wait_ge(c_psum, 1)
            dve.tensor_copy(negc[:], bank[4][:, 0:NB * FOX_HEADS].rearrange("p (b h) -> p b h", b=NB)).then_inc(c_sb, 1)
            sum_heads(4, MEM_HEADS)
            scale_heads(4, proj1, MQ1, MEM_HEADS)
            sum_heads(5, MEM_HEADS)
            scale_heads(5, kvm1, 0, MEM_HEADS)
            lo_to(at["out1"]["g"] + 2)
            dve.wait_ge(dec_sb, FOX_HEADS // 2)
            softmax_sides(at["heads1"]["h"], HEADS1, 0)
            for k in range(4):
                t_lo(at["mix1"]["t"] + k, a_lo[:, 2 * k:2 * k + 2, :], a_hi[:, 2 * k:2 * k + 2, :])
            add_out("out1")
            g = at["ff1"]["g"]
            lo_to(g + 2)
            normed(4, x)
            norm_lo("nffn0", 4)
            t = at["ff1"]["t"]
            for c in range(FF1_CHUNKS + 1):
                first = g + (0 if c == 0 else 2 + 3 * (c - 1))
                if c >= 1:
                    lo_to(first + 2)
                    t_lo(t, f_lo[:, (c - 1) % 2, 0:2, :], f_hi[:, (c - 1) % 2, 0:2, :])
                    t += 1
                if c < FF1_CHUNKS:
                    lo_to(first + 3)
                    for b in range(NB):
                        dve.wait_ge(silu_made, 2 * c + b + 1)
                        dve.tensor_tensor(f_sb[:, c % 2, b, 0:256], f_sb[:, c % 2, b, 256:512], bank[4 + b][:, 256:512],
                                          ALU.mult).then_inc(h_made, 1)
                else:
                    lo_to(first)
            add_acc(at["in2"]["g"] - 1)
            lo_to(at["in2"]["g"] + 2)
            normed(NMIX1, x)
            norm_lo("nmix1", NMIX1)
            normed(NMEM1, mem2)
            for k, (c0, n) in enumerate(CONV_JOBS):
                g_end = at["in2"]["g"] + 2 * k + 1
                lo_to(g_end + 2)
                copy_out(at["in2"]["j"] + k, g_end, proj2[:, 1, c0:c0 + n])
            lo_to(at["mem1"]["g"] + 1)
            norm_lo("nmem1", NMEM1)
            copy_out(at["mem1"]["j"], at["mem1"]["g"] + 1, kvm2[:, 1, :])
            dve.wait_ge(l2_in, 16 * len(LOADS["l2"]))
            chained(dve.memset(glu[:, :, 0:DW_K - 1], 0.0))
            chained(dve.memset(onesm[:], 1.0 / (CONV_TILES * P)))
            sum_heads(6, MEM_HEADS)
            scale_heads(6, proj2, MQ2, MEM_HEADS)
            sum_heads(7, MEM_HEADS)
            scale_heads(7, kvm2, 0, MEM_HEADS)
            lo_to(at["out2"]["g"] + 2)
            t = at["glu"]["t"]
            for k in range(3):
                dve.wait_ge(t_act, act_steps(t + 2 * k))
                dve.wait_ge(t_psum, t + 2 * k + 2)
                for m in range(2):
                    ch = 2 * k + m
                    ins = dve.scalar_tensor_tensor(glu[:, ch, DW_K - 1:], bank[6 + (t + 2 * k + 1) % 2][:, m * S:(m + 1) * S],
                                                   cb_in[:, ch:ch + 1], sig[:, m, :], ALU.add, ALU.mult)
                ins.then_inc(t_dve, 1)
            softmax_sides(at["heads2"]["h"], HEADS2, 768)
            dve.wait_ge(t_dve, dve_steps(t + 5))
            for i in range(DW_K):
                for k in range(CONV_TILES):
                    u = glu[:, k, i:i + S]
                    if i == 0:
                        ins = dve.tensor_scalar(dwy[:, k, :], u, dw[:, k, 0:1], dwb[:, k:k + 1], ALU.mult, ALU.add)
                    else:
                        if k == 0:
                            dve.wait_ge(dve_own, own[0])
                        ins = dve.scalar_tensor_tensor(dwy[:, k, :], u, dw[:, k, i:i + 1], dwy[:, k, :], ALU.mult, ALU.add)
                if i < DW_K - 1:
                    chained(ins)
            ins.then_inc(dw_made, 1)
            dve.wait_ge(mu_psum, 1)
            dve.tensor_copy(stat[:, 0, :], bank[0][:, 0:S]).then_inc(dw_made, 1)
            dve.wait_ge(dw_made, 2)
            for k in range(CONV_TILES):
                ins = dve.tensor_tensor(dwy[:, k, :], dwy[:, k, :], stat[:, 0, :], ALU.subtract)
            ins.then_inc(cent_made, 1)
            t_lo(at["mix2"]["t"], a_lo[:, 6:8, :], a_hi[:, 6:8, :])
            dve.wait_ge(sd_made, 1)
            chained(dve.reciprocal(stat[:, 2, :], stat[:, 1, :]))
            dve.wait_ge(cent_made, 1)
            for k in range(CONV_TILES):
                ins = dve.tensor_tensor(dwy[:, k, :], dwy[:, k, :], stat[:, 2, :], ALU.mult)
            ins.then_inc(ln_made, 1)
            dve.wait_ge(ln_hi, 1)
            dve.tensor_tensor(a_lo[:, 0:CONV_TILES, :], dwq[:], a_hi[:, 0:CONV_TILES, :].bitcast(F32), ALU.subtract)\
                .then_inc(ln_lo, 1)
            add_out("out2")
            lo_to(NG - 1)
            dve.wait_ge(rstd_made, 8)
            dve.wait_ge(moe_in, 16 * len(LOADS["moe"]))
            for b in range(NB):
                dve.scalar_tensor_tensor(xn[:, b, :], x[:, b, :], rstd[:, 7, b:b + 1], gain_b[:], ALU.mult, ALU.mult)\
                    .then_inc(xn_made, 1)
            norm_lo("nffn1", 7, gains=False)
            dve.wait_ge(r_psum, 1)
            chained(dve.tensor_copy(logit[:], bank[4][:, 0:NB * N_EXPERTS].rearrange("p (b e) -> p b e", b=NB)))
            for b in range(NB):
                ins = dve.max(top[:, b, :], logit[:, b, :])
            chained(ins)
            for b in range(NB):
                ins = dve.max_index(topi[:, b, :], top[:, b, :], logit[:, b, :])
            chained(ins)
            chained(dve.tensor_copy(topf[:], topi[:]))
            dve.tensor_tensor(gate[:, 0, :], top[:, :, 1], top[:, :, 0], ALU.subtract).then_inc(z_made, 1)
            for b in range(NB):
                for m in range(2):
                    ins = dve.tensor_scalar(onehot[:, m, b, :], iota[:, 0:N_EXPERTS], topf[:, b, m:m + 1], None, ALU.is_equal)
            chained(ins)
            dve.tensor_tensor(chosen[:], onehot[:, 0], onehot[:, 1], ALU.add).then_inc(ch_made, 1)
            dve.wait_ge(g_exp, 1)
            chained(dve.tensor_scalar(gate[:, 2, :], gate[:, 1, :], 1.0, None, ALU.add))
            chained(dve.reciprocal(gate[:, 2, :], gate[:, 2, :]))
            chained(dve.tensor_tensor(gate[:, 3, :], gate[:, 1, :], gate[:, 2, :], ALU.mult))
            for b in range(NB):
                chained(dve.tensor_scalar(gates[:, b, 0:N_EXPERTS], onehot[:, 0, b, :], gate[:, 2, b:b + 1], None, ALU.mult))
                chained(dve.scalar_tensor_tensor(gates[:, b, 0:N_EXPERTS], onehot[:, 1, b, :], gate[:, 3, b:b + 1],
                                                 gates[:, b, 0:N_EXPERTS], ALU.mult, ALU.add))
            chained(dve.tensor_copy(gates[:, :, N_EXPERTS:], gates[:, :, 0:N_EXPERTS]))
            dve.wait_ge(rk_psum, 1)
            dve.wait_ge(ch_made, 1)
            chained(dve.scalar_tensor_tensor(rank[:, :, 0:N_EXPERTS],
                                             bank[5][:, 0:NB * N_EXPERTS].rearrange("p (b e) -> p b e", b=NB), -1.0,
                                             chosen[:], ALU.mult, ALU.mult))
            chained(dve.tensor_scalar(rank[:, :, 0:N_EXPERTS], rank[:, :, 0:N_EXPERTS], -1.0, None, ALU.add))
            chained(dve.tensor_scalar(rank[:, :, N_EXPERTS:], rank[:, :, 0:N_EXPERTS], -float(P), None, ALU.add))
            chained(dve.tensor_reduce(count[:, 0:1], bank[5][:, 16:24], AX_X, ALU.min))
            chained(dve.tensor_scalar(count[:, 1:2], count[:, 0:1], -float(P), float(N_EXPERTS), ALU.is_lt, ALU.mult))
            dve.tensor_scalar(n_items[:], count[:, 1:2], float(N_EXPERTS), None, ALU.add).then_inc(items_made, 1)
            dve.wait_ge(items_made, 1)
            items = dve.value_load(n_items[0:1, 0:1], min_val=N_EXPERTS, max_val=2 * N_EXPERTS)
            with dve.Fori(0, items) as i:
                def e_lo(k):
                    g = NG + k
                    dve.wait_ge(hi_made, i * MOE_GRANULES + (g + 1))
                    dve.tensor_tensor(w_lo[:, g % NSPLIT, :], raw_at(g, GRAN), w_hi[:, g % NSPLIT, :].bitcast(F32),
                                      ALU.subtract).then_inc(lo_made, 1)

                def step_hi(k):
                    dve.wait_ge(t_act, i * MOE_TSTEPS + (TA + k + 1))

                for b in range(NB):
                    dve.tensor_scalar(pickg[:, b, :], iota[:], rank[:, b, bass.ds(i, 1)], gates[:, b, bass.ds(i, 1)],
                                      ALU.is_equal, ALU.mult)
                    ins = dve.tensor_scalar(pick[:, b, :], iota[:], rank[:, b, bass.ds(i, 1)], None, ALU.is_equal)
                ins.then_inc(pick_made, 1)
                for k in range(3):
                    e_lo(k)
                for k in range(2):
                    step_hi(k)
                    dve.tensor_tensor(xg_lo[:, 4 * k:4 * k + 4, :],
                                      bank[6 + (TM + k) % 2][:].rearrange("p (k s) -> p k s", k=4),
                                      xg_hi[:, 4 * k:4 * k + 4, :].bitcast(F32), ALU.subtract).then_inc(t_dve, 1)
                step_hi(2)
                dve.tensor_copy(pickgT[:, P:S], bank[6 + TM % 2][:, P:S]).then_inc(t_dve, 1)
                k = 3
                for c in range(MOE_CHUNKS + 1):
                    while k <= min(moe_first(c) + (3 if c < MOE_CHUNKS else 1), MOE_GRANULES - 1):
                        e_lo(k)
                        k += 1
                    if c >= 1:
                        step_hi(2 + c)
                        dve.tensor_tensor(mf_lo[:, (c - 1) % 2, :, :],
                                          bank[6 + (TM + 2 + c) % 2][:].rearrange("p (k s) -> p k s", k=4),
                                          mf_hi[:, (c - 1) % 2, :, :].bitcast(F32), ALU.subtract).then_inc(t_dve, 1)
                    if c < MOE_CHUNKS:
                        while k <= min(moe_first(c) + 5, MOE_GRANULES - 1):
                            e_lo(k)
                            k += 1
                        ub = bank[5] if c % 2 == 0 else bank[3]
                        dve.wait_ge(silu_made, i * MOE_CHUNKS + (SM + c + 1))
                        dve.wait_ge(w_used, i * MOE_GRANULES + (NG + moe_first(c) + 4))
                        dve.tensor_tensor(mf_sb[:, c % 2, 1, :], mf_sb[:, c % 2, 0, :], ub[:], ALU.mult).then_inc(h_made, 1)
                dve.wait_ge(w_used, i * MOE_GRANULES + (NG + MOE_GRANULES))
                dve.tensor_copy(y_sb[:, 512:D], bank[1][:]).then_inc(y_dve, 1)
                for b in range(NB):
                    for half in range(2):
                        dve.wait_ge(sc_psum, i * 4 + (2 * b + half + 1))
                        xs = x[:, b, half * 512:(half + 1) * 512]
                        dve.tensor_tensor(xs, xs, bank[2 + 2 * b + half][:], ALU.add).then_inc(x_upd, 1)


def kernel(**inputs):
    import numpy as np
    from concourse import bacc
    from concourse.bass_utils import run_bass_kernel_spmd

    v = {name: np.ascontiguousarray(array) for name, array in inputs.items()}

    def cols(array, tiles):
        r = array.reshape(*array.shape[:-1], tiles, P)
        return np.ascontiguousarray(np.moveaxis(r, -1, 0))

    norms = [v["norm1_g"][0], v["norm2_g"][0], v["norm_mix_2"][0], v["norm_mem_2"][0], v["norm_ffn_2"][0],
             v["norm_mix_2"][1], v["norm_mem_2"][1], v["norm_ffn_2"][1]]
    heads = [v["q_norm_g"][0], v["k_norm_g"][0], v["fox_g_q_2"][0], v["fox_g_k_2"][0], v["g_mq_2"][0], v["g_mk_2"][0],
             v["g_mq_2"][1], v["g_mk_2"][1]]
    arrays = dict(
        g_norms=cols(np.stack(norms), KT),
        g_heads=np.ascontiguousarray(np.stack(heads).T),
        rel_bias=np.ascontiguousarray(v["rel_bias"][0][:, ::-1]),
        conv_w=np.ascontiguousarray(cols(v["conv_w"][0], 2).transpose(0, 2, 1)),
        pool_scale=cols(v["pool_scale"][0], 2),
        conv_b_in_2=cols(v["conv_b_in_2"][0], 2 * CONV_TILES),
        conv_dw_2=np.ascontiguousarray(cols(v["conv_dw_2"][0], CONV_TILES).transpose(0, 2, 1)),
        conv_dw_b_2=cols(v["conv_dw_b_2"][0], CONV_TILES),
        conv_ln_g_2=cols(v["conv_ln_g_2"][0], CONV_TILES),
        conv_ln_b_2=cols(v["conv_ln_b_2"][0], CONV_TILES),
    )
    for name in ("x", "w_in", "pool_w", "w_out", "w_mlp1", "w_mlp2", "mem_2", "norm_ffn_2", "w_mem_kv_2",
                 "fox_w_in_2", "fox_b_f_2", "fox_w_out_2", "conv_w_in_2", "conv_w_out_2", "ffn_w_gate_2",
                 "ffn_w_up_2", "ffn_w_down_2", "moe_router_2", "moe_w_gate_2", "moe_w_up_2", "moe_w_down_2"):
        arrays[name] = v[name]

    f = np.float32
    p, t = np.arange(P), np.arange(S)
    key, query = t[None, None, :], p[:, None, None] + P * np.arange(NB)[None, :, None]
    arrays["c_ident"] = np.eye(P, dtype=f)
    arrays["c_iota"] = np.broadcast_to(p.astype(f), (P, P)).copy()
    arrays["c_negtri"] = np.where(query <= key, f(-1), f(0)).astype(f)
    arrays["c_masks"] = np.stack([np.where(key // 64 <= query // 64, f(0), f(-1e30)),
                                  np.where(key <= query, f(0), f(-1e30))], axis=1).astype(f)
    windows = np.array(POOL_WINDOWS).reshape(2, 2).repeat(HD, axis=1).T
    arrays["c_invcnt"] = (1.0 / np.minimum(t[None, None, :] + 1, windows[:, :, None])).astype(f)

    nc = bacc.Bacc("TRN2", target_bir_lowering=False, num_devices=1, dynamic_dma_scratch_size=1024)
    a = {name: nc.dram_tensor(f"in_{name}", array.shape, F32, kind="ExternalInput").ap()
         for name, array in arrays.items()}
    out = nc.dram_tensor("out", (1, S, D), F32, kind="ExternalOutput").ap()
    block_kernel(nc, a, out)
    r = run_bass_kernel_spmd(nc, [{f"in_{name}": array for name, array in arrays.items()}], core_ids=[0])
    return r.results[0]["out"]
```

```python
from contextlib import ExitStack

import concourse.bass as bass
from concourse import mybir

F32 = mybir.dt.float32
F32R = mybir.dt.float32r
I32 = mybir.dt.int32
U32 = mybir.dt.uint32
ALU = mybir.AluOpType
ACT = mybir.ActivationFunctionType
AX_X = mybir.AxisListType.X

P = 128
D = 1024
KT = D // P
S = 256
NB = S // P
HD = 64
EPS = 1e-6
GRAN = 2048
NRAW = 6
NSPLIT = 3

REL_HEADS = 8
FOX_HEADS = 12
MEM_HEADS = 4
CONV_K = 3
POOL_WINDOWS = (2, 4, 8, 16)
DW_K = 31
CONV_TILES = 6
PE_TAPS = 16
N_DIAG = 12
N_EXPERTS = 8
EXPERT_FF = 3584
MOE_CHUNKS = EXPERT_FF // 512
MOE_GRANULES = 6 * MOE_CHUNKS
MOE_TSTEPS = 3 + MOE_CHUNKS
PICKG_CHUNK, GATHER_CHUNK = 3, MOE_CHUNKS - 1

NORM1, NORM2, NMEM0, NMIX0, NFFN0, NMEM1, NMIX1, NFFN1 = range(8)
A_STAGES = ("norm1", "mix0", "norm2", "nmix0", "mix1", "nffn0", "nmix1", "mix2", "nffn1")
A_TILES = 12
MEM_CHUNKS = range(2, 6)
GQ0, GK0, GFQ, GFK, GMQ0, GMK0, GMQ1, GMK1 = range(8)

REL_LEN = 2 * 255 + 1


def bcast(ap, n):
    return bass.AP(ap.tensor, ap.offset, [*[list(d) for d in ap.ap], [0, n]])


def a_at(buf, name, kt, n=1):
    i = (A_STAGES.index(name) * KT + kt) % A_TILES
    return buf[:, i:i + n, :]


def plan():
    at, n = {}, dict(g=0, t=0, j=0, h=0)
    kinds = []

    def stage(name, g=0, t="", j=0, h=0):
        at[name] = dict(n)
        n["g"] += g
        n["t"] += len(t)
        kinds.extend(t)
        n["j"] += j
        n["h"] += h

    stage("norm1", t="bbbb")
    stage("in0", g=10, j=5)
    stage("conv0", t="aaaa")
    stage("qk0", t="aaaa")
    stage("heads0", h=REL_HEADS)
    stage("mix0", t="bb")
    stage("out0", g=4, j=2)
    stage("norm2", t="bbbb")
    stage("ff0", g=32, t="b" * (16 + len(MEM_CHUNKS)))
    stage("mem0", g=2)
    stage("nmix0", t="bbbb")
    stage("in1", g=16, j=8)
    stage("qk1", t="a" * 8)
    stage("heads1", h=FOX_HEADS + MEM_HEADS)
    stage("mix1", t="bbbb")
    stage("out1", g=4, j=2)
    stage("nffn0", t="bbbb")
    stage("ff1", g=33, t="b" * (11 + len(MEM_CHUNKS)))
    stage("mem1", g=2)
    stage("nmix1", t="bbbb")
    stage("in2", g=8, j=4)
    stage("glu", t="adadad")
    stage("qk2", t="aa")
    stage("heads2", h=MEM_HEADS)
    stage("mix2", t="b")
    stage("out2", g=4, j=2)
    stage("nffn1", t="bbbb")
    stage("moe")
    return at, "".join(kinds)


def block_kernel(nc, a, out):
    at, tkinds = plan()
    is_out_job = [False] * at["moe"]["j"]
    for name in ("out0", "out1", "out2"):
        for k in range(2):
            is_out_job[at[name]["j"] + k] = True

    stream = []

    def rows(w, r0, kts, c0, n):
        return w[r0:r0 + kts * P, c0:c0 + n].rearrange("(t p) n -> p t n", p=P)

    def project(w, c0, n):
        for half in range(2):
            stream.append(([rows(w, half * 512, 4, c0, n)], 4, n))

    w_in, w_out, w1, w2 = a["w_in"][0], a["w_out"][0], a["w_mlp1"][0], a["w_mlp2"][0]
    fox_in, fox_out = a["fox_w_in_2"][0], a["fox_w_out_2"][0]
    fg, fu, fd = a["ffn_w_gate_2"][0], a["ffn_w_up_2"][0], a["ffn_w_down_2"][0]
    conv_in, conv_out = a["conv_w_in_2"][0], a["conv_w_out_2"][0]
    kv = a["w_mem_kv_2"]
    eg, eu, ed = a["moe_w_gate_2"][0], a["moe_w_up_2"][0], a["moe_w_down_2"][0]
    FF0_CHUNKS = w1.shape[1] // 512
    FF1_CHUNKS = fg.shape[1] // 256
    FOXW = FOX_HEADS * HD
    FOX_JOBS = [(3 * FOXW, FOX_HEADS)] + [(c * 384, 384) for c in range(6)] + [(3 * FOXW + FOX_HEADS, 256)]
    CONV_JOBS = [(0, 512), (512, 512), (1024, 512), (1536, 256)]

    for c in range(5):
        project(w_in, c * 512, 512)
    for c in range(2):
        project(w_out, c * 512, 512)
    for c in range(FF0_CHUNKS + 1):
        if c < FF0_CHUNKS:
            project(w1, c * 512, 512)
        if c >= 1:
            for k in range(2):
                stream.append(([rows(w2, (c - 1) * 512 + k * 256, 2, 0, D)], 2, D))
    project(kv[0], 0, 512)
    for c0, n in FOX_JOBS:
        project(fox_in, c0, n)
    for c in range(2):
        project(fox_out, c * 512, 512)
    for c in range(FF1_CHUNKS + 1):
        if c < FF1_CHUNKS:
            for half in range(2):
                stream.append(([rows(fg, half * 512, 4, c * 256, 256), rows(fu, half * 512, 4, c * 256, 256)], 4, 512))
        if c >= 1:
            stream.append(([rows(fd, (c - 1) * 256, 2, 0, D)], 2, D))
    project(kv[1], 0, 512)
    for c0, n in CONV_JOBS:
        project(conv_in, c0, n)
    for c in range(2):
        project(conv_out, c * 512, 512)
    NG = len(stream)
    assert NG == at["moe"]["g"] and MOE_GRANULES % NRAW == 0 and MOE_GRANULES % NSPLIT == 0

    raw_count, seen = [], [0] * NRAW
    for g, (parts, _, _) in enumerate(stream):
        seen[g % NRAW] += 16 * len(parts)
        raw_count.append(seen[g % NRAW])

    def moe_first(c):
        return 0 if c == 0 else 4 + 6 * (c - 1)

    ctx = ExitStack()
    with ctx:
        def sb(name, shape, dt=F32, stack=ctx):
            return stack.enter_context(nc.sbuf_tensor(name, shape, dt))

        def sem(name):
            return ctx.enter_context(nc.semaphore(name))

        x = sb("x", [P, NB, D])
        raw = sb("raw", [P, NRAW, GRAN])
        w_hi = sb("w_hi", [P, NSPLIT, GRAN], F32R)
        w_lo = sb("w_lo", [P, NSPLIT, GRAN], F32R)
        a_hi = sb("a_hi", [P, A_TILES, S], F32R)
        a_lo = sb("a_lo", [P, A_TILES, S], F32R)
        ident = sb("ident", [P, P])
        ident_r = sb("ident_r", [P, P], F32R)
        gcol = sb("gcol", [P, 8, KT])
        hcol = sb("hcol", [P, 8])
        ss = sb("ss", [P, 8, NB])
        ms = sb("ms", [P, 8, NB])
        rstd = sb("rstd", [P, 8, NB])
        mhalf = sb("mhalf", [P, NB])
        eps = sb("eps", [P, 1])
        negtri = sb("negtri", [P, NB, S])
        iota = sb("iota", [P, P])
        mask_r = sb("mask_r", [P, 2, NB, S], F32R)

        mixers = ExitStack()
        mix = sb("mix", [P, NB, D], stack=mixers)
        qT = sb("qT", [P, 8, S], stack=mixers)
        kT = sb("kT", [P, 8, S], stack=mixers)
        sc = sb("sc", [P, 2, NB, S], stack=mixers)
        pr = sb("pr", [P, 2, NB, S], stack=mixers)
        pT = sb("pT", [P, 2, NB, S], stack=mixers)
        nmax = sb("nmax", [P, 2, NB], stack=mixers)
        psumr = sb("psumr", [P, 2, NB], stack=mixers)
        rinv = sb("rinv", [P, 2, NB], stack=mixers)
        qss = sb("qss", [P, 2, 24], stack=mixers)
        layer = ExitStack()
        proj0 = sb("proj0", [P, NB, 2560], stack=layer)
        relT = sb("relT", [P, REL_HEADS, 384], stack=layer)
        rel_row = sb("rel_row", [REL_HEADS, REL_LEN + 1], stack=layer)
        gbT, gcT = qT[:, 4:6, :], qT[:, 6:8, :]
        hiT, mT = kT[:, 4:6, :], kT[:, 6:8, :]
        zT = sb("zT", [P, 2, S + 2], stack=layer)
        uT = sb("uT", [P, 2, S + 16], stack=layer)
        win = sb("win", [P, 2, 2, S + 16], stack=layer)
        invcnt = sb("invcnt", [P, 2, S], stack=layer)
        yT = sb("yT", [P, 2, S], stack=layer)
        cw = sb("cw", [P, 2, CONV_K], stack=layer)
        pscale = sb("pscale", [P, 2], stack=layer)
        pool_w = sb("pool_w", [P, 2, P], stack=layer)
        layer.close()
        layer = ExitStack()
        proj1 = sb("proj1", [P, NB, 2572], stack=layer)
        kvm1 = sb("kvm1", [P, NB, 512], stack=layer)
        decay = sb("decay", [P, FOX_HEADS, S], stack=layer)
        fb = sb("fb", [P, FOX_HEADS], stack=layer)
        lf = sb("lf", [P, 4, NB, FOX_HEADS], stack=layer)
        negc = sb("negc", [P, NB, FOX_HEADS], stack=layer)
        layer.close()
        layer = ExitStack()
        proj2 = sb("proj2", [P, NB, 1792], stack=layer)
        sig = qT[:, 0:2, :]
        glu = sb("glu", [P, CONV_TILES, S + DW_K - 1], stack=layer)
        kvm2 = sb("kvm2", [P, NB, 512], stack=layer)
        dwy = sb("dwy", [P, CONV_TILES, S], stack=layer)
        dwq = sb("dwq", [P, CONV_TILES, S], stack=layer)
        diag = dwq[:].rearrange("p k s -> p (k s)").rearrange("p (n c) -> p n c", c=P)
        stat = sb("stat", [P, 3, S], stack=layer)
        cb_in = sb("cb_in", [P, 2 * CONV_TILES], stack=layer)
        dw = sb("dw", [P, CONV_TILES, DW_K], stack=layer)
        dwb = sb("dwb", [P, CONV_TILES], stack=layer)
        lng = sb("lng", [P, CONV_TILES], stack=layer)
        lnb = sb("lnb", [P, CONV_TILES], stack=layer)
        onesm = sb("onesm", [P, P], stack=layer)
        layer.close()
        mixers.close()
        ffs = ExitStack()
        f_sb = sb("f_sb", [P, 2, NB, 512], stack=ffs)
        f_hi = sb("f_hi", [P, 2, 4, S], F32R, stack=ffs)
        f_lo = sb("f_lo", [P, 2, 4, S], F32R, stack=ffs)
        m_hi = sb("m_hi", [P, KT, S], F32R, stack=ffs)
        m_lo = sb("m_lo", [P, KT, S], F32R, stack=ffs)
        mem = sb("mem", [P, NB, D], stack=ffs)
        squares_ff = sb("squares_ff", [P, NB, D], stack=ffs)
        ffs.close()
        moes = ExitStack()
        mf_sb = sb("mf_sb", [P, 2, 2, 512], stack=moes)
        mf_hi = sb("mf_hi", [P, 2, 4, P], F32R, stack=moes)
        mf_lo = sb("mf_lo", [P, 2, 4, P], F32R, stack=moes)
        xg_hi = sb("xg_hi", [P, KT, P], F32R, stack=moes)
        xg_lo = sb("xg_lo", [P, KT, P], F32R, stack=moes)
        y_sb = sb("y_sb", [P, D], stack=moes)
        zrow = sb("zrow", [P, NB, D], stack=moes)
        z_hi = sb("z_hi", [P, NB, D], F32R, stack=moes)
        z_lo = sb("z_lo", [P, NB, D], F32R, stack=moes)
        pick = sb("pick", [P, NB, P], F32R, stack=moes)
        pickg = sb("pickg", [P, NB, P], stack=moes)
        pickgT = sb("pickgT", [P, S], stack=moes)
        gain_b = sb("gain_b", [P, D], stack=moes)
        router = sb("router", [P, KT, N_EXPERTS], stack=moes)
        router_hi = sb("router_hi", [P, KT, N_EXPERTS], F32R, stack=moes)
        router_lo = sb("router_lo", [P, KT, N_EXPERTS], F32R, stack=moes)
        logit_t = sb("logit_t", [N_EXPERTS, S], stack=moes)
        logit = sb("logit", [P, NB, N_EXPERTS], stack=moes)
        top = sb("top", [P, NB, N_EXPERTS], stack=moes)
        topi = sb("topi", [P, NB, N_EXPERTS], U32, stack=moes)
        topf = sb("topf", [P, NB, N_EXPERTS], stack=moes)
        gate = sb("gate", [P, 4, NB], stack=moes)
        onehot = sb("onehot", [P, 2, NB, N_EXPERTS], stack=moes)
        chosen = sb("chosen", [P, NB, N_EXPERTS], stack=moes)
        rank = sb("rank", [P, NB, 2 * N_EXPERTS + 1], stack=moes)
        gates = sb("gates", [P, NB, 2 * N_EXPERTS], stack=moes)
        count = sb("count", [P, 2], stack=moes)
        n_items = sb("n_items", [P, 1], I32, stack=moes)
        moes.close()

        bank = [ctx.enter_context(nc.psum_tensor(f"bank{i}", [P, 512], F32)) for i in range(8)]

        rel_rows_dram = nc.dram_tensor("rel_rows_dram", (REL_HEADS, REL_LEN + 1), F32, kind="Internal").ap()
        rel_band_dram = nc.dram_tensor("rel_band_dram", (REL_HEADS, P, 384), F32, kind="Internal").ap()

        x_in = [sem(f"x_in{h}") for h in range(2)]
        raw_in = [sem(f"raw_in{i}") for i in range(NRAW)]
        hi_made, lo_made, w_used = sem("hi_made"), sem("lo_made"), sem("w_used")
        start_in, mem_in, const_in, early_in, l1_in, l2_in, moe_in = (
            sem(n) for n in ("start_in", "mem_in", "const_in", "early_in", "l1_in", "l2_in", "moe_in"))
        rel_in, rel_ext, rel_out, rel_band, rel_back = (
            sem(n) for n in ("rel_in", "rel_ext", "rel_out", "rel_band", "rel_back"))
        pool_zero, mask_made = sem("pool_zero"), sem("mask_made")
        ss_made, rstd_made = sem("ss_made"), sem("rstd_made")
        kv_act, kv_dve = sem("kv_act"), sem("kv_dve")
        t_psum, t_act, t_dve = sem("t_psum"), sem("t_act"), sem("t_dve")
        j_act, j_dve, x_upd = sem("j_act"), sem("j_dve"), sem("x_upd")
        sq_made, qss_made, qsqrt_made, qk_made = (sem(n) for n in ("sq_made", "qss_made", "qsqrt_made", "qk_made"))
        s_psum, s_sb, s_max, s_exp = sem("s_psum"), sem("s_sb"), sem("s_max"), sem("s_exp")
        p_psum, p_sb, o_psum, o_sb = sem("p_psum"), sem("p_sb"), sem("o_psum"), sem("o_sb")
        y_made, m_made, pool_psum, cp_hi, cp_lo = (sem(n) for n in ("y_made", "m_made", "pool_psum", "cp_hi", "cp_lo"))
        f_made, silu_made, h_made = sem("f_made"), sem("silu_made"), sem("h_made")
        lf_x, lf_ln, lf_made, c_psum, c_sb, dec_psum, dec_sb = (
            sem(n) for n in ("lf_x", "lf_ln", "lf_made", "c_psum", "c_sb", "dec_psum", "dec_sb"))
        diag_made, tap_used, dw_acc = sem("diag_made"), sem("tap_used"), sem("dw_acc")
        mu_made, mu_psum, cent_made, sqc_made, var_psum, sd_made, ln_made, silu2 = (
            sem(n) for n in ("mu_made", "mu_psum", "cent_made", "sqc_made", "var_psum", "sd_made", "ln_made", "silu2"))
        ln_hi, ln_lo = sem("ln_hi"), sem("ln_lo")
        z_made, zhi_made, zlo_made, gap_made, router_hi_made, router_lo_made, r_sb, rt_psum, r_psum, g_exp, ch_made, rk_psum, items_made = (
            sem(n) for n in ("z_made", "zhi_made", "zlo_made", "gap_made", "router_hi_made", "router_lo_made", "r_sb", "rt_psum", "r_psum", "g_exp", "ch_made", "rk_psum", "items_made"))
        pickg_made, pick_made, y_act, y_dve, sc_psum = sem("pickg_made"), sem("pick_made"), sem("y_act"), sem("y_dve"), sem("sc_psum")
        act_own, dve_own, pool_own = sem("act_own"), sem("dve_own"), sem("pool_own")
        out_done = sem("out_done")

        def raw_at(g, n):
            return raw[:, g % NRAW, 0:n]

        def n_el(g):
            return stream[g][1] * stream[g][2]

        def act_steps(t):
            return sum(k in "ab" for k in tkinds[:t + 1])

        def dve_steps(t):
            return sum(k in "bd" for k in tkinds[:t + 1])

        CHUNK_STEP = {c: c - 1 + (c >= PICKG_CHUNK) + 2 * (c > GATHER_CHUNK) for c in range(1, MOE_CHUNKS + 1)}
        PICKG_STEP, GATHER_STEP = PICKG_CHUNK - 1, GATHER_CHUNK + 1
        TA, TD, TM = act_steps(len(tkinds)), dve_steps(len(tkinds)), len(tkinds)

        def plain_jobs(j):
            return sum(not o for o in is_out_job[:j + 1])

        LOADS = dict(
            const=[(hcol[0:HD, :], a["g_heads"]),
                   (hcol[HD:P, :], a["g_heads"]), (negtri[:], a["c_negtri"]), (iota[:], a["c_iota"]),
                   (pr[:], a["c_masks"])],
            early=[(invcnt[:], a["c_invcnt"]), (cw[:], a["conv_w"]), (pscale[:], a["pool_scale"])],
            l1=[(fb[:], bass.AP(a["fox_b_f_2"].tensor, 0, [[0, P], [1, FOX_HEADS]]))],
            l2=[(cb_in[:], a["conv_b_in_2"]), (dw[:], a["conv_dw_2"]), (dwb[:], a["conv_dw_b_2"]),
                (lng[:], a["conv_ln_g_2"]), (lnb[:], a["conv_ln_b_2"])],
            moe=[(router[:], a["moe_router_2"][0].rearrange("(t p) e -> p t e", p=P)),
                 (gain_b[:], bass.AP(a["norm_ffn_2"].tensor, D, [[0, P], [1, D]]))],
        )

        HEADS0 = [(0, h // 2, h // 2, h % 2 * HD, proj0, 1024 + h * HD, h) for h in range(REL_HEADS)]
        HEADS1 = [(1, h // 2, h // 2, h % 2 * HD, proj1, 2 * FOXW + h * HD, h) for h in range(FOX_HEADS)]
        HEADS1 += [(None, 6 + h // 2, 6 + h // 2, h % 2 * HD, kvm1, 256 + h * HD, h) for h in range(MEM_HEADS)]
        HEADS2 = [(None, 6 + h // 2, 6 + h // 2, h % 2 * HD, kvm2, 256 + h * HD, h) for h in range(MEM_HEADS)]
        MQ1, MQ2 = 3 * FOXW + FOX_HEADS, 1536
        memq, memk = qT[:, 6:8, :], kT[:, 6:8, :]
        at_x = dict(norm2=4, ff0=4, nmix0=8, nffn0=12, ff1=12, nmix1=16, nffn1=20, moe=20)
        HM = SM = 2 * FF1_CHUNKS

        def tokens(t):
            return t.rearrange("(b p) d -> p b d", p=P)

        block = ctx.enter_context(nc.Block())

        @block.sync
        def _(sp):
            sp.dma_start(ident[:], a["c_ident"]).then_inc(start_in, 16)
            sp.dma_start(gcol[:], a["g_norms"]).then_inc(start_in, 16)
            for h in range(2):
                sp.dma_start(x[:, :, h * 512:(h + 1) * 512], tokens(a["x"][0])[:, :, h * 512:(h + 1) * 512])\
                    .then_inc(x_in[h], 16)
            for g, (parts, kts, n) in enumerate(stream):
                if g >= NRAW:
                    sp.wait_ge(lo_made, g - NRAW + 1)
                if len(parts) == 1:
                    sp.dma_start(raw_at(g, kts * n).rearrange("p (t n) -> p t n", t=kts), parts[0])\
                        .then_inc(raw_in[g % NRAW], 16)
                else:
                    dst = raw_at(g, kts * n).rearrange("p (t u n) -> p t u n", t=kts, u=2)
                    for u in range(2):
                        sp.dma_start(dst[:, :, u, :], parts[u]).then_inc(raw_in[g % NRAW], 16)

            def load_expert(i):
                e = i % N_EXPERTS

                def load(k, src, kts):
                    g = NG + k
                    sp.wait_ge(lo_made, i * MOE_GRANULES + (g - NRAW + 1))
                    sp.dma_start(raw_at(g, GRAN).rearrange("p (t n) -> p t n", t=kts),
                                 src.rearrange("a (t p) n -> p (a t) n", p=P)).then_inc(raw_in[g % NRAW], 16)

                for c in range(MOE_CHUNKS + 1):
                    k = moe_first(c)
                    if c < MOE_CHUNKS:
                        for m, w in enumerate((eg, eu)):
                            for half in range(2):
                                load(k, w[bass.ds(e, 1), half * 512:(half + 1) * 512, c * 512:(c + 1) * 512], 4)
                                k += 1
                    if c >= 1:
                        for half in range(2):
                            r0 = (c - 1) * 512 + half * 256
                            load(k, ed[bass.ds(e, 1), r0:r0 + 256, :], 2)
                            k += 1

            with sp.Fori(0, N_EXPERTS) as i:
                load_expert(i)
            sp.wait_ge(items_made, 1)
            items = sp.value_load(n_items[0:1, 0:1], min_val=N_EXPERTS, max_val=2 * N_EXPERTS)
            with sp.If(items - N_EXPERTS):
                with sp.Fori(N_EXPERTS, 2 * N_EXPERTS) as i:
                    load_expert(i)
            for b in range(NB):
                sp.wait_ge(x_upd, items * 4 + (at_x["moe"] + 2 * (b + 1)))
                sp.dma_start(out[0, b * P:(b + 1) * P, :], x[:, b, :]).then_inc(out_done, 16)
            sp.wait_ge(out_done, 16 * NB)

        @block.gpsimd
        def _(pool):
            pool.memset(pool_w[:], 0.0).then_inc(pool_zero, 1)
            pool.memset(mhalf[:], -0.5).then_inc(pool_own, 1)
            for n in range(8):
                pool.wait_ge(ss_made, 2 * (n + 1))
                pool.tensor_scalar(ms[:, n, :], ss[:, n, :], 1.0 / D, EPS, ALU.mult, ALU.add).then_inc(pool_own, 1)
                pool.wait_ge(pool_own, n + 2)
                pool.tensor_tensor(rstd[:, n, :], ms[:, n, :], mhalf[:], ALU.pow).then_inc(rstd_made, 1)

        @block.tensor
        def _(pe):
            def tstep(t, sources, base=None):
                if base is None:
                    if t >= 2:
                        if tkinds[t - 2] in "bd":
                            pe.wait_ge(t_dve, dve_steps(t - 2))
                        else:
                            pe.wait_ge(t_act, act_steps(t - 2))
                    b = bank[6 + t % 2]
                for k, src in enumerate(sources):
                    mm = pe.transpose(b[:, k * P:(k + 1) * P], src, ident[:])
                mm.then_inc(t_psum, 1)

            def parts3(outs, hi, lo, wh, wl, start, stop):
                for o, h, l in zip(outs, wh, wl):
                    pe.matmul(o, hi, h, start=start, stop=False)
                    pe.matmul(o, hi, l, start=False, stop=False)
                for o, h in zip(outs, wh):
                    mm = pe.matmul(o, lo, h, start=False, stop=stop)
                return mm

            def across(g, n, lhs, kt0, outs, first, last, middle=None):
                slot = g % NSPLIT
                for kk in range(4):
                    if kk == 2 and middle is not None:
                        middle()
                    wh = w_hi[:, slot, kk * n:(kk + 1) * n]
                    wl = w_lo[:, slot, kk * n:(kk + 1) * n]
                    for b, o in enumerate(outs):
                        mm = parts3([o], lhs(0, kt0 + kk, b), lhs(1, kt0 + kk, b), [wh], [wl],
                                    first and kk == 0, last and kk == 3)
                mm.then_inc(w_used, 1)

            def down(g, lhs, kt0, outs, first, last):
                slot = g % NSPLIT
                for kk in range(2):
                    wh = [w_hi[:, slot, kk * D + h * 512:kk * D + (h + 1) * 512] for h in range(2)]
                    wl = [w_lo[:, slot, kk * D + h * 512:kk * D + (h + 1) * 512] for h in range(2)]
                    for b, o in enumerate(outs):
                        mm = parts3(o, lhs(0, kt0 + kk, b), lhs(1, kt0 + kk, b), wh, wl,
                                    first and kk == 0, last and kk == 1)
                mm.then_inc(w_used, 1)

            def a_tile(name):
                return lambda part, kt, b: a_at((a_hi, a_lo)[part], name, kt)[:, 0, b * P:(b + 1) * P]

            def norm_t(name, half, src, made, count):
                pe.wait_ge(made, count)
                for s in (2 * half, 2 * half + 1):
                    tstep(at[name]["t"] + s, [src[:, b, kt * P:(kt + 1) * P] for kt in (2 * s, 2 * s + 1)
                                              for b in range(NB)])

            def x_t(name, half):
                norm_t(name, half, x, x_upd, at_x[name] - 2 + 2 * half)

            def norm_ready(name, half):
                pe.wait_ge(t_dve, dve_steps(at[name]["t"] + 2 * half + 1))

            def job(j, g, n, name, norm, middle):
                outs = [bank[2 * (j % 2) + b][:, 0:n] for b in range(NB)]
                for half in range(2):
                    if norm:
                        norm_ready(name, half)
                    pe.wait_ge(lo_made, g + half + 1)
                    across(g + half, n, a_tile(name), 4 * half, outs, half == 0, half == 1,
                           middle if half == 0 else None)

            def jobs(stage, widths, name, norm=False):
                for k, n in enumerate(widths):
                    j = at[stage]["j"] + k
                    if j >= 2:
                        pe.wait_ge(j_act, plain_jobs(j - 2))
                        pe.wait_ge(j_dve, plain_jobs(j - 2))
                    job(j, at[stage]["g"] + 2 * k, n, name, norm and k == 0, None)

            def out_jobs(stage, mixed, name):
                j, g = at[stage]["j"], at[stage]["g"]
                for k in range(2):
                    pe.wait_ge(j_act, plain_jobs(j + k - 2))
                    pe.wait_ge(j_dve, plain_jobs(j + k - 2))
                    outs = [bank[2 * ((j + k) % 2) + b][:] for b in range(NB)]
                    for half in range(2):
                        if k == 1 and half == 1:
                            x_t(name, 0)
                        pe.wait_ge(lo_made, g + 2 * k + half + 1)
                        across(g + 2 * k + half, 512, a_tile(mixed), 4 * half, outs, half == 0, half == 1)

            def mem_job(stage, name):
                g = at[stage]["g"]
                for half in range(2):
                    pe.wait_ge(lo_made, g + half + 1)
                    across(g + half, 512, lambda part, kt, b: (m_hi, m_lo)[part][:, kt, b * P:(b + 1) * P], 4 * half,
                           [bank[4][:], bank[5][:]], half == 0, half == 1)
                    x_t(name, half)

            def mem_t(t, c, loads):
                if c in MEM_CHUNKS:
                    pe.wait_ge(mem_in, 16 * loads)
                    s = c - MEM_CHUNKS[0]
                    tstep(t, [mem[:, b, kt * P:(kt + 1) * P] for kt in (2 * s, 2 * s + 1) for b in range(NB)])
                    return t + 1
                return t

            def cols_t(t, src, cols):
                tstep(t, [src[:, b, c:c + P] for c in cols for b in range(NB)])

            def heads(first, todo, between=None):
                for i in range(len(todo) + 2):
                    if i < len(todo):
                        h = first + i
                        kind, qt, kt_, r = todo[i][:4]
                        if i >= 2:
                            pe.wait_ge(s_exp, h - 1)
                        for b in range(NB):
                            o = bank[i % 2][:, b * S:(b + 1) * S]
                            mm = pe.matmul(o, qT[r:r + HD, qt, b * P:(b + 1) * P], kT[r:r + HD, kt_, :],
                                           start=True, stop=kind is None)
                            if kind is not None:
                                mm = pe.matmul(o, ident_r[:], mask_r[:, kind, b, :], start=False, stop=True)
                        mm.then_inc(s_psum, 1)
                    if 1 <= i <= len(todo):
                        h = first + i - 1
                        pe.wait_ge(s_exp, h + 1)
                        if i - 1 >= 2:
                            pe.wait_ge(p_sb, h - 1)
                        for b in range(NB):
                            for kt in range(NB):
                                mm = pe.transpose(bank[2 + (i - 1) % 2][:, (kt * NB + b) * P:(kt * NB + b + 1) * P],
                                                  pr[:, (i - 1) % 2, b, kt * P:(kt + 1) * P], ident[:])
                        mm.then_inc(p_psum, 1)
                    if i >= 2:
                        h = first + i - 2
                        v, vc = todo[i - 2][4:6]
                        pe.wait_ge(p_sb, h + 1)
                        if i - 2 >= 2:
                            pe.wait_ge(o_sb, 2 * (h - 1))
                        for b in range(NB):
                            for kt in range(NB):
                                mm = pe.matmul(bank[4 + (i - 2) % 2][:, b * HD:(b + 1) * HD],
                                               pT[:, (i - 2) % 2, kt, b * P:(b + 1) * P],
                                               v[:, kt, vc:vc + HD], start=kt == 0, stop=kt == NB - 1)
                        mm.then_inc(o_psum, 1)
                    if between is not None:
                        between(i)

            pe.wait_ge(start_in, 32)
            for half in range(2):
                norm_t("norm1", half, x, x_in[half], 16)
            jobs("in0", [512] * 5, "norm1", norm=True)
            t = at["conv0"]["t"]
            pe.wait_ge(j_act, plain_jobs(at["in0"]["j"] + 4))
            pe.wait_ge(j_dve, plain_jobs(at["in0"]["j"] + 4))
            for k in range(4):
                cols_t(t + k, proj0, [1536 + 256 * k, 1536 + 256 * k + P])
            pe.wait_ge(qk_made, 2)
            t = at["qk0"]["t"]
            for k in range(4):
                cols_t(t + k, proj0, [256 * k, 256 * k + P])
            pe.wait_ge(t_act, act_steps(t + 3))
            pe.wait_ge(mask_made, 2)
            heads(at["heads0"]["h"], HEADS0)
            pe.wait_ge(m_made, 1)
            pe.wait_ge(s_exp, at["heads0"]["h"] + REL_HEADS)
            for k in range(2):
                mm = pe.matmul(bank[0][:, k * S:(k + 1) * S], pool_w[:, k, :], mT[:, k, :], start=True, stop=True)
            mm.then_inc(pool_psum, 1)
            pe.wait_ge(o_sb, 2 * (at["heads0"]["h"] + REL_HEADS))
            for k in range(2):
                cols_t(at["mix0"]["t"] + k, mix, [256 * k, 256 * k + P])
            pe.wait_ge(t_dve, dve_steps(at["mix0"]["t"] + 1))
            pe.wait_ge(cp_lo, 2)
            out_jobs("out0", "mix0", "norm2")

            def f_tile(buf):
                return lambda p, kt, b: (f_hi, f_lo)[p][:, buf, kt, b * P:(b + 1) * P]

            accs = [[bank[2 * b + h][:] for h in range(2)] for b in range(NB)]

            g, t = at["ff0"]["g"], at["ff0"]["t"]
            norm_ready("norm2", 0)
            for c in range(FF0_CHUNKS + 1):
                ups = [bank[4 + b][:] for b in range(NB)]
                if c < FF0_CHUNKS:
                    if c >= 1:
                        pe.wait_ge(f_made, 2 * c)
                    pe.wait_ge(lo_made, g + 1)
                    across(g, 512, a_tile("norm2"), 0, ups, True, False, (lambda: x_t("norm2", 1)) if c == 0 else None)
                    g += 1
                t = mem_t(t, c, 1)
                if c >= 1:
                    pe.wait_ge(f_made, 2 * c)
                    for k in range(2):
                        tstep(t, [f_sb[:, (c - 1) % 2, b, kt * P:(kt + 1) * P] for kt in (2 * k, 2 * k + 1)
                                  for b in range(NB)])
                        t += 1
                if c < FF0_CHUNKS:
                    pe.wait_ge(lo_made, g + 1)
                    if c == 0:
                        norm_ready("norm2", 1)
                    across(g, 512, a_tile("norm2"), 4, ups, False, True)
                    g += 1
                if c >= 1:
                    pe.wait_ge(t_dve, dve_steps(t - 1))
                    if c == 1:
                        pe.wait_ge(x_upd, at_x["ff0"])
                    for k in range(2):
                        pe.wait_ge(lo_made, g + 1)
                        down(g, f_tile((c - 1) % 2), 2 * k, accs, c == 1 and k == 0, c == FF0_CHUNKS and k == 1)
                        g += 1

            mem_job("mem0", "nmix0")
            jobs("in1", [n for _, n in FOX_JOBS], "nmix0", norm=True)
            pe.wait_ge(kv_act, 1)
            pe.wait_ge(kv_dve, 1)
            pe.wait_ge(lf_made, 1)
            for b in range(NB):
                for s in range(b + 1):
                    mm = pe.matmul(bank[4][:, b * FOX_HEADS:(b + 1) * FOX_HEADS],
                                   negtri[:, s, b * P:(b + 1) * P], lf[:, 3, s, :], start=s == 0, stop=s == b)
            mm.then_inc(c_psum, 1)
            for k in range(FOX_HEADS // 2):
                bk = bank[4 + (k + 1) % 2]
                if k >= 2:
                    pe.wait_ge(dec_sb, k - 1)
                if k == 1:
                    pe.wait_ge(c_sb, 1)
                for hh in range(2):
                    for s in range(NB):
                        mm = pe.matmul(bk[:, hh * S:(hh + 1) * S],
                                       bcast(lf[:, 3, s, 2 * k + hh], P), negtri[:, s, :],
                                       start=s == 0, stop=s == 1)
                mm.then_inc(dec_psum, 1)
            t = at["qk1"]["t"]
            pe.wait_ge(qk_made, 4)
            for k in range(6):
                cols_t(t + k, proj1, [256 * k, 256 * k + P])
            pe.wait_ge(qk_made, 6)
            cols_t(t + 6, proj1, [MQ1, MQ1 + P])
            cols_t(t + 7, kvm1, [0, P])
            pe.wait_ge(t_act, act_steps(t + 7))
            pe.wait_ge(dec_sb, FOX_HEADS // 2)
            heads(at["heads1"]["h"], HEADS1)
            pe.wait_ge(o_sb, 2 * (at["heads1"]["h"] + len(HEADS1)))
            for k in range(4):
                cols_t(at["mix1"]["t"] + k, mix, [256 * k, 256 * k + P])
            pe.wait_ge(t_dve, dve_steps(at["mix1"]["t"] + 3))
            out_jobs("out1", "mix1", "nffn0")

            g, t = at["ff1"]["g"], at["ff1"]["t"]
            norm_ready("nffn0", 0)
            for c in range(FF1_CHUNKS + 1):
                ups = [bank[4 + b][:] for b in range(NB)]
                if c < FF1_CHUNKS:
                    if c >= 1:
                        pe.wait_ge(h_made, 2 * c)
                    pe.wait_ge(lo_made, g + 1)
                    across(g, 512, a_tile("nffn0"), 0, ups, True, False, (lambda: x_t("nffn0", 1)) if c == 0 else None)
                    g += 1
                t = mem_t(t, c, 2)
                if c >= 1:
                    pe.wait_ge(h_made, 2 * c)
                    tstep(t, [f_sb[:, (c - 1) % 2, b, kt * P:(kt + 1) * P] for kt in range(2) for b in range(NB)])
                    t += 1
                if c < FF1_CHUNKS:
                    pe.wait_ge(lo_made, g + 1)
                    if c == 0:
                        norm_ready("nffn0", 1)
                    across(g, 512, a_tile("nffn0"), 4, ups, False, True)
                    g += 1
                if c >= 1:
                    pe.wait_ge(t_dve, dve_steps(t - 1))
                    if c == 1:
                        pe.wait_ge(x_upd, at_x["ff1"])
                    pe.wait_ge(lo_made, g + 1)
                    down(g, f_tile((c - 1) % 2), 0, accs, c == 1, c == FF1_CHUNKS)
                    g += 1

            mem_job("mem1", "nmix1")
            jobs("in2", [n for _, n in CONV_JOBS], "nmix1", norm=True)
            t = at["glu"]["t"]
            pe.wait_ge(j_act, plain_jobs(at["in2"]["j"] + 3))
            pe.wait_ge(j_dve, plain_jobs(at["in2"]["j"] + 3))
            for k in range(3):
                cols_t(t + 2 * k, proj2, [768 + 256 * k, 768 + 256 * k + P])
                cols_t(t + 2 * k + 1, proj2, [256 * k, 256 * k + P])
            pe.wait_ge(qk_made, 8)
            t = at["qk2"]["t"]
            cols_t(t, proj2, [MQ2, MQ2 + P])
            cols_t(t + 1, kvm2, [0, P])
            pe.wait_ge(t_act, act_steps(t + 1))

            def taps(k):
                if k >= 2:
                    pe.wait_ge(dw_acc, k - 1)
                for i in range(PE_TAPS):
                    pe.wait_ge(diag_made, k * PE_TAPS + i + 1)
                    mm = pe.matmul(bank[6 + k % 2][:, 0:S], diag[:, (k * PE_TAPS + i) % N_DIAG, :], glu[:, k, i:i + S],
                                   start=i == 0, stop=i == PE_TAPS - 1)
                    mm.then_inc(tap_used, 1)

            pe.wait_ge(t_dve, dve_steps(at["glu"]["t"] + 5))
            heads(at["heads2"]["h"], HEADS2, taps)
            pe.wait_ge(dw_acc, CONV_TILES)
            pe.wait_ge(o_sb, 2 * (at["heads2"]["h"] + len(HEADS2)))
            for k in range(CONV_TILES):
                mm = pe.matmul(bank[0][:, 0:S], onesm[:], dwy[:, k, :], start=k == 0, stop=k == CONV_TILES - 1)
            mm.then_inc(mu_psum, 1)
            cols_t(at["mix2"]["t"], mix, [768, 768 + P])
            pe.wait_ge(sqc_made, 1)
            for k in range(CONV_TILES):
                mm = pe.matmul(bank[1][:, 0:S], onesm[:], dwq[:, k, :], start=k == 0, stop=k == CONV_TILES - 1)
            mm.then_inc(var_psum, 1)
            pe.wait_ge(t_dve, dve_steps(at["mix2"]["t"]))
            pe.wait_ge(ln_lo, CONV_TILES // 2)
            out_jobs("out2", "mix2", "nffn1")

            pe.wait_ge(router_lo_made, 1)
            for half in range(2):
                if half == 1:
                    x_t("nffn1", 1)
                norm_ready("nffn1", half)
                for kt in range(4 * half, 4 * half + 4):
                    hi, lo = (a_at(part, "nffn1", kt)[:, 0, :] for part in (a_hi, a_lo))
                    for n, (w, tile) in enumerate(((router_hi, hi), (router_lo, hi), (router_hi, lo))):
                        mm = pe.matmul(bank[4][0:N_EXPERTS, 0:S], w[:, kt, :], tile,
                                       start=kt == 0 and n == 0, stop=kt == KT - 1 and n == 2)
            mm.then_inc(r_psum, 1)
            pe.wait_ge(r_sb, 1)
            for b in range(NB):
                mm = pe.transpose(bank[5][:, b * N_EXPERTS:(b + 1) * N_EXPERTS], logit_t[:, b * P:(b + 1) * P],
                                  ident[0:N_EXPERTS, 0:N_EXPERTS])
            mm.then_inc(rt_psum, 1)
            pe.wait_ge(ch_made, 1)
            for b in range(NB):
                for s in range(b + 1):
                    pe.matmul(bank[4][:, b * N_EXPERTS:(b + 1) * N_EXPERTS],
                              negtri[:, s, b * P:(b + 1) * P], chosen[:, s, :], start=s == 0, stop=s == b)
            for s in range(NB):
                mm = pe.matmul(bank[4][:, 16:24], negtri[:, 0, P:S], chosen[:, s, :], start=s == 0, stop=s == 1)
            mm.then_inc(rk_psum, 1)

            def xg_tile(part, kt, b):
                return (xg_hi, xg_lo)[part][:, kt, :]

            pe.wait_ge(x_upd, at_x["moe"])

            def gather(k, dst):
                for kk in range(4):
                    kt = 4 * k + kk
                    for b in range(NB):
                        for part in (z_hi, z_lo):
                            mm = pe.matmul(dst[:, kk * P:(kk + 1) * P], part[:, b, kt * P:(kt + 1) * P], pick[:, b, :],
                                           start=b == 0 and part is z_hi, stop=b == NB - 1 and part is z_lo)
                mm.then_inc(t_psum, 1)

            def scatter():
                for b in range(NB):
                    for half in range(2):
                        pe.matmul(bank[2 - 2 * b + half][:], pickgT[:, b * P:(b + 1) * P],
                                  y_sb[:, half * 512:(half + 1) * 512], start=True, stop=True).then_inc(sc_psum, 1)

            pe.wait_ge(zlo_made, 1)
            pe.wait_ge(pick_made, 1)
            for k in range(2):
                pe.wait_ge(t_dve, TD + k - 1)
                gather(k, bank[6 + (TM + k) % 2])
            pe.wait_ge(items_made, 1)
            items = pe.value_load(n_items[0:1, 0:1], min_val=N_EXPERTS, max_val=2 * N_EXPERTS)
            with pe.Fori(0, items) as i:
                def t_free(k):
                    pe.wait_ge(t_dve, i * MOE_TSTEPS + (TD + 2 + k - 1))

                def w_ready(k):
                    pe.wait_ge(lo_made, i * MOE_GRANULES + (NG + k + 1))

                def chunk_t(c):
                    pe.wait_ge(h_made, i * MOE_CHUNKS + (HM + c))
                    t_free(CHUNK_STEP[c])
                    for kt in range(4):
                        mm = pe.transpose(bank[6 + (TM + CHUNK_STEP[c]) % 2][:, kt * P:(kt + 1) * P],
                                          mf_sb[:, (c - 1) % 2, 1, kt * P:(kt + 1) * P], ident[:])
                    mm.then_inc(t_psum, 1)

                pe.wait_ge(t_dve, i * MOE_TSTEPS + (TD + 2))
                for c in range(MOE_CHUNKS + 1):
                    k = moe_first(c)
                    gb, ub = (bank[4], bank[5]) if c % 2 == 0 else (bank[2], bank[3])
                    if c < MOE_CHUNKS:
                        if c == 1:
                            pe.wait_ge(x_upd, i * 4 + (at_x["moe"] + 4))
                        if c >= 2:
                            pe.wait_ge(h_made, i * MOE_CHUNKS + (HM + c - 1))
                        for half in range(2):
                            w_ready(k)
                            across(NG + k, 512, xg_tile, 4 * half, [gb[:]], half == 0, half == 1)
                            k += 1
                    if c == 0:
                        pe.wait_ge(y_act, i + 1)
                        pe.wait_ge(y_dve, i + 1)
                        scatter()
                    if c == PICKG_CHUNK:
                        pe.wait_ge(pickg_made, i + 1)
                        t_free(PICKG_STEP)
                        for b in range(NB):
                            mm = pe.transpose(bank[6 + (TM + PICKG_STEP) % 2][:, b * P:(b + 1) * P], pickg[:, b, :], ident[:])
                        mm.then_inc(t_psum, 1)
                    if 1 <= c < MOE_CHUNKS:
                        chunk_t(c)
                    if c < MOE_CHUNKS:
                        for half in range(2):
                            w_ready(k)
                            across(NG + k, 512, xg_tile, 4 * half, [ub[:]], half == 0, half == 1)
                            k += 1
                    if c == GATHER_CHUNK:
                        pe.wait_ge(pick_made, i + 2)
                        for kk in range(2):
                            t_free(GATHER_STEP + kk)
                            gather(kk, bank[6 + (TM + GATHER_STEP + kk) % 2])
                        chunk_t(c + 1)
                    if c >= 1:
                        pe.wait_ge(t_dve, i * MOE_TSTEPS + (TD + 2 + CHUNK_STEP[c] + 1))
                        for half in range(2):
                            w_ready(k)
                            down(NG + k, lambda p, kt, b: (mf_hi, mf_lo)[p][:, (c - 1) % 2, kt, :], 2 * half,
                                 [[bank[0][:], bank[1][:]]], c == 1 and half == 0, c == MOE_CHUNKS and half == 1)
                            k += 1
            pe.wait_ge(y_act, items + 1)
            pe.wait_ge(y_dve, items + 1)
            scatter()

        @block.scalar
        def _(act):
            own = [0]
            done = [0]

            def chained(ins):
                own[0] += 1
                ins.then_inc(act_own, 1)
                act.wait_ge(act_own, own[0])

            def hi(g):
                act.wait_ge(raw_in[g % NRAW], raw_count[g])
                if g >= NSPLIT:
                    act.wait_ge(w_used, g - NSPLIT + 1)
                n = n_el(g)
                act.activation(w_hi[:, g % NSPLIT, 0:n], raw_at(g, n), ACT.Copy).then_inc(hi_made, 1)

            def hi_to(g):
                while done[0] <= min(g, NG - 1):
                    hi(done[0])
                    done[0] += 1

            def gains(n, s):
                return [gcol[:, n, 2 * s + k:2 * s + k + 1] for k in range(2)]

            def t_hi(t, dst, scales=(1.0, 1.0)):
                act.wait_ge(t_psum, t + 1)
                src = bank[6 + t % 2]
                if scales[0] == 1.0:
                    act.activation(dst, src[:].rearrange("p (k s) -> p k s", k=2), ACT.Copy).then_inc(t_act, 1)
                else:
                    act.activation(dst[:, 0, :], src[:, 0:S], ACT.Copy, scale=scales[0])
                    act.activation(dst[:, 1, :], src[:, S:2 * S], ACT.Copy, scale=scales[1]).then_inc(t_act, 1)

            def squares(n, src, scratch):
                if n >= 1:
                    act.wait_ge(ss_made, 2 * n)
                for b in range(NB):
                    act.activation(scratch[:, b, :], src[:, b, :], ACT.Square, accum_out=ss[:, n, b:b + 1])\
                        .then_inc(ss_made, 1)

            def norm_hi(name, n, half):
                for s in (2 * half, 2 * half + 1):
                    t_hi(at[name]["t"] + s, a_at(a_hi, name, 2 * s, 2), gains(n, s))

            def mem_hi(t, c, n):
                if c in MEM_CHUNKS:
                    s = c - MEM_CHUNKS[0]
                    t_hi(t, m_hi[:, 2 * s:2 * s + 2, :], gains(n, s))
                    return t + 1
                return t

            def out_norm(stage, name, n):
                g = at[stage]["g"]
                hi_to(g + 4)
                norm_hi(name, n, 0)
                hi_to(g + 5)
                act.wait_ge(w_used, g + 3)
                norm_hi(name, n, 1)
                hi_to(g + 6)
                squares(n, x, mix)

            def mem_out(stage, name, n, m, dst):
                g = at[stage]["g"]
                hi_to(g + 2)
                norm_hi(name, n, 0)
                hi_to(g + 3)
                norm_hi(name, n, 1)
                act.wait_ge(w_used, g + 2)
                act.wait_ge(rstd_made, m + 1)
                act.activation(dst, bank[4][:], ACT.Copy, scale=rstd[:, m, 0:1]).then_inc(kv_act, 1)
                hi_to(g + 4)
                squares(n, x, squares_ff)
                act.wait_ge(rstd_made, n + 1)

            def copy_out(j, g_end, dst, n):
                act.wait_ge(w_used, g_end + 1)
                act.activation(dst, bank[2 * (j % 2)][:, 0:dst.shape[-1]], ACT.Copy, scale=rstd[:, n, 0:1]).then_inc(j_act, 1)

            def exps(first, todo, before=None):
                for i in range(len(todo) + 1):
                    if before is not None:
                        before(i)
                    h = first + i
                    if i < len(todo):
                        act.wait_ge(s_max, h + 1)
                        if i >= 2:
                            act.wait_ge(p_psum, h - 1)
                        if i >= 2:
                            act.wait_ge(o_sb, 2 * (h - 1))
                        for b in range(NB):
                            src = bank[i % 2][:, b * S:(b + 1) * S] if todo[i][0] is None else sc[:, i % 2, b, :]
                            ins = act.activation(pr[:, i % 2, b, :], src, ACT.Exp, bias=nmax[:, i % 2, b:b + 1],
                                                 accum_out=psumr[:, i % 2, b:b + 1])
                        ins.then_inc(s_exp, 1)
                    if i >= 1:
                        act.wait_ge(p_psum, h)
                        if i - 1 >= 2:
                            act.wait_ge(o_psum, h - 2)
                        act.activation(pT[:, (i - 1) % 2, :, :],
                                       bank[2 + (i - 1) % 2][:].rearrange("p (k s) -> p k s", k=NB), ACT.Copy)\
                            .then_inc(p_sb, 1)

            def square_heads(src, c0, nh):
                act.activation(mix[:, :, 0:nh * HD], src[:, :, c0:c0 + nh * HD], ACT.Square).then_inc(sq_made, 1)

            def root_heads(q, nh):
                act.wait_ge(qss_made, q + 1)
                act.activation(qss[:, 1, 0:NB * nh], qss[:, 0, 0:NB * nh], ACT.Sqrt, scale=1.0 / HD, bias=eps[:])\
                    .then_inc(qsqrt_made, 1)

            def t_copy(t, dst, gain=None):
                act.wait_ge(t_psum, t + 1)
                src = bank[6 + t % 2][:].rearrange("p (k s) -> p k s", k=2)
                if gain is None:
                    act.activation(dst, src, ACT.Copy).then_inc(t_act, 1)
                else:
                    act.activation(dst, src, ACT.Copy, scale=hcol[:, gain:gain + 1]).then_inc(t_act, 1)

            act.wait_ge(start_in, 32)
            for dst, src in LOADS["const"]:
                act.dma_start(dst, src).then_inc(const_in, 16)
            norm_hi("norm1", NORM1, 0)
            hi_to(0)
            norm_hi("norm1", NORM1, 1)
            hi_to(2)
            squares(NORM1, x, mix)
            act.dma_start(rel_row[:, 127:127 + 257], a["rel_bias"]).then_inc(rel_in, 16)
            for dst, src in LOADS["early"]:
                act.dma_start(dst, src).then_inc(early_in, 16)
            act.wait_ge(pool_zero, 1)
            for gr in range(4):
                r = (gr % 2) * HD
                act.dma_start(pool_w[r:r + HD, gr // 2, r:r + HD], a["pool_w"][0, gr]).then_inc(early_in, 16)
            act.wait_ge(rstd_made, 1)
            for k in range(5):
                g_end = at["in0"]["g"] + 2 * k + 1
                hi_to(g_end + 2)
                copy_out(at["in0"]["j"] + k, g_end, proj0[:, 0, 512 * k:512 * (k + 1)], NORM1)
                if k == 1:
                    act.wait_ge(rel_ext, 1)
                    act.dma_start(rel_rows_dram, rel_row[:]).then_inc(rel_out, 16)
                if k == 2:
                    act.wait_ge(rel_out, 16)
                    act.dma_start(rel_band_dram,
                                  bass.AP(rel_rows_dram.tensor, P - 1, [[REL_LEN + 1, REL_HEADS], [-1, P], [1, 384]]))\
                        .then_inc(rel_band, 16)
                if k == 3:
                    act.wait_ge(rel_band, 16)
                    act.dma_start(relT[:], rel_band_dram.rearrange("h p m -> p h m")).then_inc(rel_back, 16)
                    act.activation(ident_r[:], ident[:], ACT.Copy).then_inc(mask_made, 1)
                    act.wait_ge(const_in, 16 * len(LOADS["const"]))
                    act.activation(mask_r[:], pr[:], ACT.Copy).then_inc(mask_made, 1)
                if k == 1:
                    act.wait_ge(j_act, plain_jobs(at["in0"]["j"] + 1))
                    act.wait_ge(j_dve, plain_jobs(at["in0"]["j"] + 1))
                    square_heads(proj0, 0, REL_HEADS)
                if k == 2:
                    root_heads(0, REL_HEADS)
                    act.wait_ge(qss_made, 1)
                    square_heads(proj0, 512, REL_HEADS)
                if k == 3:
                    root_heads(1, REL_HEADS)
            hi_to(at["out0"]["g"] + 2)
            t = at["conv0"]["t"]
            for k, dst in enumerate((gbT, gcT, hiT, uT[:, :, 16:16 + S])):
                t_copy(t + k, dst)
            t = at["qk0"]["t"]
            for k in range(4):
                t_copy(t + k, (qT, kT)[k // 2][:, 2 * (k % 2):2 * (k % 2) + 2, :], (GQ0, GK0)[k // 2])
            exps(at["heads0"]["h"], HEADS0)
            act.wait_ge(w_used, at["out0"]["g"])
            act.wait_ge(y_made, 1)
            act.activation(a_at(a_hi, "mix0", 4, 2), yT[:], ACT.Copy).then_inc(cp_hi, 1)
            act.wait_ge(pool_psum, 1)
            act.activation(a_at(a_hi, "mix0", 6)[:, 0, :], bank[0][:, 0:S], ACT.Copy, scale=pscale[:, 0:1])
            act.activation(a_at(a_hi, "mix0", 7)[:, 0, :], bank[0][:, S:2 * S], ACT.Copy, scale=pscale[:, 1:2]).then_inc(cp_hi, 1)
            for k in range(2):
                t_hi(at["mix0"]["t"] + k, a_at(a_hi, "mix0", 2 * k, 2))
            g = at["ff0"]["g"]
            out_norm("out0", "norm2", NORM2)
            act.dma_start(mem[:], tokens(a["mem_2"][0])).then_inc(mem_in, 16)
            act.wait_ge(rstd_made, NORM2 + 1)
            t = at["ff0"]["t"]
            for c in range(FF0_CHUNKS + 1):
                first = g + (0 if c == 0 else 2 + 4 * (c - 1))
                if c == MEM_CHUNKS[0]:
                    act.wait_ge(mem_in, 16)
                    squares(NMEM0, mem, squares_ff)
                if c >= 1:
                    hi_to(first + 2)
                    t = mem_hi(t, c, NMEM0)
                    for k in range(2):
                        t_hi(t, f_hi[:, (c - 1) % 2, 2 * k:2 * k + 2, :])
                        t += 1
                if c < FF0_CHUNKS:
                    hi_to(first + 3)
                    act.wait_ge(w_used, first + 2)
                    for b in range(NB):
                        f = f_sb[:, c % 2, b, :]
                        chained(act.activation(f, bank[4 + b][:], ACT.Relu, scale=rstd[:, NORM2, b:b + 1]))
                        act.activation(f, f, ACT.Square).then_inc(f_made, 1)
            mem_out("mem0", "nmix0", NMIX0, NMEM0, kvm1[:, 0, :])
            for dst, src in LOADS["l1"]:
                act.dma_start(dst, src).then_inc(l1_in, 16)
            for k, (c0, n) in enumerate(FOX_JOBS):
                g_end = at["in1"]["g"] + 2 * k + 1
                hi_to(g_end + 2)
                copy_out(at["in1"]["j"] + k, g_end, proj1[:, 0, c0:c0 + n], NMIX0)
                if k == 1:
                    act.wait_ge(lf_x, 1)
                    chained(act.activation(lf[:, 1], lf[:, 1], ACT.Exp, scale=-1.0))
                    act.activation(lf[:, 2], lf[:, 1], ACT.Ln, bias=1.0).then_inc(lf_ln, 1)
                if k == 2:
                    act.wait_ge(j_act, plain_jobs(at["in1"]["j"] + 2))
                    act.wait_ge(j_dve, plain_jobs(at["in1"]["j"] + 2))
                    square_heads(proj1, 0, FOX_HEADS)
                if k == 4:
                    root_heads(2, FOX_HEADS)
                    act.wait_ge(j_act, plain_jobs(at["in1"]["j"] + 4))
                    act.wait_ge(j_dve, plain_jobs(at["in1"]["j"] + 4))
                    square_heads(proj1, FOXW, FOX_HEADS)
                if k == 5:
                    root_heads(3, FOX_HEADS)
            for k in range(FOX_HEADS // 2):
                act.wait_ge(dec_psum, k + 1)
                act.activation(decay[:, 2 * k:2 * k + 2, :], bank[4 + (k + 1) % 2][:].rearrange("p (k s) -> p k s", k=2),
                               ACT.Copy).then_inc(dec_sb, 1)
            hi_to(at["out1"]["g"] + 2)
            act.wait_ge(j_act, plain_jobs(at["in1"]["j"] + 7))
            act.wait_ge(j_dve, plain_jobs(at["in1"]["j"] + 7))
            square_heads(proj1, MQ1, MEM_HEADS)
            root_heads(4, MEM_HEADS)
            act.wait_ge(kv_act, 1)
            act.wait_ge(kv_dve, 1)
            square_heads(kvm1, 0, MEM_HEADS)
            root_heads(5, MEM_HEADS)
            t = at["qk1"]["t"]
            for k in range(6):
                t_copy(t + k, (qT, kT)[k // 3][:, 2 * (k % 3):2 * (k % 3) + 2, :], (GFQ, GFK)[k // 3])
            t_copy(t + 6, memq[:], GMQ0)
            t_copy(t + 7, memk[:], GMK0)
            exps(at["heads1"]["h"], HEADS1)
            act.wait_ge(w_used, at["out1"]["g"])
            for k in range(4):
                t_hi(at["mix1"]["t"] + k, a_at(a_hi, "mix1", 2 * k, 2))
            g = at["ff1"]["g"]
            out_norm("out1", "nffn0", NFFN0)
            act.dma_start(mem[:], tokens(a["mem_2"][0])).then_inc(mem_in, 16)
            act.wait_ge(rstd_made, NFFN0 + 1)
            t = at["ff1"]["t"]
            for c in range(FF1_CHUNKS + 1):
                first = g + (0 if c == 0 else 2 + 3 * (c - 1))
                if c == MEM_CHUNKS[0]:
                    act.wait_ge(mem_in, 32)
                    squares(NMEM1, mem, squares_ff)
                if c >= 1:
                    hi_to(first + 2)
                    t = mem_hi(t, c, NMEM1)
                    t_hi(t, f_hi[:, (c - 1) % 2, 0:2, :])
                    t += 1
                if c < FF1_CHUNKS:
                    hi_to(first + 3)
                    act.wait_ge(w_used, first + 2)
                    for b in range(NB):
                        act.activation(f_sb[:, c % 2, b, 256:512], bank[4 + b][:, 0:256], ACT.Silu,
                                       scale=rstd[:, NFFN0, b:b + 1]).then_inc(silu_made, 1)
            mem_out("mem1", "nmix1", NMIX1, NMEM1, kvm2[:, 0, :])
            for dst, src in LOADS["l2"]:
                act.dma_start(dst, src).then_inc(l2_in, 16)
            for k, (c0, n) in enumerate(CONV_JOBS):
                g_end = at["in2"]["g"] + 2 * k + 1
                hi_to(g_end + 2)
                copy_out(at["in2"]["j"] + k, g_end, proj2[:, 0, c0:c0 + n], NMIX1)
            act.wait_ge(j_act, plain_jobs(at["in2"]["j"] + 3))
            act.wait_ge(j_dve, plain_jobs(at["in2"]["j"] + 3))
            square_heads(proj2, MQ2, MEM_HEADS)
            root_heads(6, MEM_HEADS)
            act.wait_ge(kv_act, 2)
            act.wait_ge(kv_dve, 2)
            square_heads(kvm2, 0, MEM_HEADS)
            root_heads(7, MEM_HEADS)
            hi_to(at["out2"]["g"] + 2)
            t = at["glu"]["t"]
            act.wait_ge(l2_in, 16 * len(LOADS["l2"]))
            for k in range(3):
                act.wait_ge(t_psum, t + 2 * k + 1)
                if k >= 1:
                    act.wait_ge(t_dve, dve_steps(t + 2 * k - 1))
                for m in range(2):
                    ch = CONV_TILES + 2 * k + m
                    ins = act.activation(sig[:, m, :], bank[6 + (t + 2 * k) % 2][:, m * S:(m + 1) * S], ACT.Sigmoid,
                                         bias=cb_in[:, ch:ch + 1])
                ins.then_inc(t_act, 1)
            t = at["qk2"]["t"]
            t_copy(t, memq[:], GMQ1)
            t_copy(t + 1, memk[:], GMK1)

            def diagonals(k):
                for i in range(PE_TAPS):
                    n = k * PE_TAPS + i
                    if n >= N_DIAG:
                        act.wait_ge(tap_used, n - N_DIAG + 1)
                    act.activation(diag[:, n % N_DIAG, :], ident[:], ACT.Copy, scale=dw[:, k, i:i + 1]).then_inc(diag_made, 1)

            exps(at["heads2"]["h"], HEADS2, diagonals)
            diagonals(CONV_TILES - 1)
            act.wait_ge(w_used, at["out2"]["g"])
            t_hi(at["mix2"]["t"], a_at(a_hi, "mix2", 6, 2))
            act.wait_ge(cent_made, 1)
            act.activation(dwq[:], dwy[:], ACT.Square).then_inc(sqc_made, 1)
            act.wait_ge(var_psum, 1)
            act.activation(stat[:, 1, :], bank[1][:, 0:S], ACT.Sqrt, bias=eps[:]).then_inc(sd_made, 1)
            act.wait_ge(ln_made, 1)
            for k in range(CONV_TILES):
                act.activation(dwq[:, k, :], dwy[:, k, :], ACT.Silu, scale=lng[:, k:k + 1], bias=lnb[:, k:k + 1])\
                    .then_inc(silu2, 1)
            for k in range(0, CONV_TILES, 2):
                act.wait_ge(silu2, k + 2)
                act.activation(a_at(a_hi, "mix2", k, 2), dwq[:, k:k + 2, :], ACT.Copy).then_inc(ln_hi, 1)
            act.wait_ge(w_used, at["out2"]["g"] + 1)
            for dst, src in LOADS["moe"]:
                act.dma_start(dst, src).then_inc(moe_in, 16)
            act.wait_ge(moe_in, 16 * len(LOADS["moe"]))
            act.activation(router_hi[:], router[:], ACT.Copy).then_inc(router_hi_made, 1)
            out_norm("out2", "nffn1", NFFN1)
            act.wait_ge(z_made, 2)
            act.activation(z_hi[:], zrow[:], ACT.Copy).then_inc(zhi_made, 1)
            act.wait_ge(gap_made, 1)
            act.activation(gate[:, 1, :], gate[:, 0, :], ACT.Exp).then_inc(g_exp, 1)

            def xg_hi_out(k, src):
                act.activation(xg_hi[:, 4 * k:4 * k + 4, :], src[:].rearrange("p (k s) -> p k s", k=4), ACT.Copy)\
                    .then_inc(t_act, 1)

            def y_out():
                act.activation(y_sb[:, 0:512], bank[0][:], ACT.Copy).then_inc(y_act, 1)

            for k in range(2):
                act.wait_ge(t_psum, TM + k + 1)
                xg_hi_out(k, bank[6 + (TM + k) % 2])
            act.wait_ge(items_made, 1)
            items = act.value_load(n_items[0:1, 0:1], min_val=N_EXPERTS, max_val=2 * N_EXPERTS)
            with act.Fori(0, items) as i:
                def e_hi(k):
                    g = NG + k
                    act.wait_ge(raw_in[g % NRAW], i * (16 * (MOE_GRANULES // NRAW)) + (seen[g % NRAW] + 16 * (1 + (k // NRAW))))
                    act.wait_ge(w_used, i * MOE_GRANULES + (g - NSPLIT + 1))
                    act.activation(w_hi[:, g % NSPLIT, :], raw_at(g, GRAN), ACT.Copy).then_inc(hi_made, 1)

                def step_in(k):
                    act.wait_ge(t_psum, i * MOE_TSTEPS + (TM + 2 + k + 1))

                def chunk_hi(c):
                    step_in(CHUNK_STEP[c])
                    act.activation(mf_hi[:, (c - 1) % 2, :, :],
                                   bank[6 + (TM + CHUNK_STEP[c]) % 2][:].rearrange("p (k s) -> p k s", k=4), ACT.Copy)\
                        .then_inc(t_act, 1)

                for k in range(2):
                    e_hi(k)
                act.wait_ge(w_used, i * MOE_GRANULES + NG)
                y_out()
                k = 2
                for c in range(MOE_CHUNKS + 1):
                    while k <= min(moe_first(c) + (3 if c < MOE_CHUNKS else 1), MOE_GRANULES - 1):
                        e_hi(k)
                        k += 1
                    if c == PICKG_CHUNK:
                        step_in(PICKG_STEP)
                        act.activation(pickgT[:, 0:P], bank[6 + (TM + PICKG_STEP) % 2][:, 0:P], ACT.Copy).then_inc(t_act, 1)
                    if 1 <= c < MOE_CHUNKS:
                        chunk_hi(c)
                    if c < MOE_CHUNKS:
                        act.wait_ge(w_used, i * MOE_GRANULES + (NG + moe_first(c) + 2))
                        gb = bank[4] if c % 2 == 0 else bank[2]
                        act.activation(mf_sb[:, c % 2, 0, :], gb[:], ACT.Silu).then_inc(silu_made, 1)
                    if c == GATHER_CHUNK:
                        while k <= moe_first(c) + 5:
                            e_hi(k)
                            k += 1
                        for kk in range(2):
                            step_in(GATHER_STEP + kk)
                            xg_hi_out(kk, bank[6 + (TM + GATHER_STEP + kk) % 2])
                        chunk_hi(c + 1)
            act.wait_ge(w_used, items * MOE_GRANULES + NG)
            y_out()

        @block.vector
        def _(dve):
            own = [0]
            done = [0]

            def chained(ins):
                own[0] += 1
                ins.then_inc(dve_own, 1)
                dve.wait_ge(dve_own, own[0])

            def lo(g):
                dve.wait_ge(hi_made, g + 1)
                n = n_el(g)
                dve.tensor_tensor(w_lo[:, g % NSPLIT, 0:n], raw_at(g, n), w_hi[:, g % NSPLIT, 0:n].bitcast(F32),
                                  ALU.subtract).then_inc(lo_made, 1)

            def lo_to(g):
                while done[0] <= min(g, NG - 1):
                    lo(done[0])
                    done[0] += 1

            def t_lo(t, dst, hi_part, scales=(1.0, 1.0)):
                dve.wait_ge(t_act, act_steps(t))
                src = bank[6 + t % 2]
                if scales[0] == 1.0:
                    dve.tensor_tensor(dst, src[:].rearrange("p (k s) -> p k s", k=2), hi_part.bitcast(F32),
                                      ALU.subtract).then_inc(t_dve, 1)
                else:
                    for k in range(2):
                        ins = dve.scalar_tensor_tensor(dst[:, k, :], src[:, k * S:(k + 1) * S], scales[k],
                                                       hi_part[:, k, :].bitcast(F32), ALU.mult, ALU.subtract)
                    ins.then_inc(t_dve, 1)

            def gains(n, s):
                return [gcol[:, n, 2 * s + k:2 * s + k + 1] for k in range(2)]

            def norm_lo(name, n, half):
                for s in (2 * half, 2 * half + 1):
                    t_lo(at[name]["t"] + s, a_at(a_lo, name, 2 * s, 2), a_at(a_hi, name, 2 * s, 2), gains(n, s))

            def mem_lo(t, c, n):
                if c in MEM_CHUNKS:
                    s = c - MEM_CHUNKS[0]
                    t_lo(t, m_lo[:, 2 * s:2 * s + 2, :], m_hi[:, 2 * s:2 * s + 2, :], gains(n, s))
                    return t + 1
                return t

            def copy_out(j, g_end, dst, n):
                dve.wait_ge(w_used, g_end + 1)
                dve.tensor_scalar(dst, bank[2 * (j % 2) + 1][:, 0:dst.shape[-1]], rstd[:, n, 1:2], None, ALU.mult)\
                    .then_inc(j_dve, 1)

            def add_out(stage, name, n):
                for k in range(2):
                    j, g_end = at[stage]["j"] + k, at[stage]["g"] + 2 * k + 1
                    lo_to(g_end + (3, 2)[k])
                    dve.wait_ge(w_used, g_end + 1)
                    for b in range(NB):
                        xs = x[:, b, k * 512:(k + 1) * 512]
                        dve.tensor_tensor(xs, xs, bank[2 * (j % 2) + b][:], ALU.add).then_inc(x_upd, 1)
                    norm_lo(name, n, k)
                dve.wait_ge(rstd_made, n + 1)

            def add_acc(stage, name, n, m, dst):
                g = at[stage]["g"]
                lo_to(g + 1)
                dve.wait_ge(w_used, g)
                for h in range(2):
                    for b in range(NB):
                        xs = x[:, b, h * 512:(h + 1) * 512]
                        dve.tensor_tensor(xs, xs, bank[2 * b + h][:], ALU.add).then_inc(x_upd, 1)
                norm_lo(name, n, 0)
                lo_to(g + 3)
                norm_lo(name, n, 1)
                dve.wait_ge(w_used, g + 2)
                dve.wait_ge(rstd_made, m + 1)
                dve.tensor_scalar(dst, bank[5][:], rstd[:, m, 1:2], None, ALU.mult).then_inc(kv_dve, 1)
                lo_to(g + 4)
                dve.wait_ge(rstd_made, n + 1)

            def sum_heads(q, nh):
                dve.wait_ge(sq_made, q + 1)
                for b in range(NB):
                    ins = dve.tensor_reduce(qss[:, 0, b * nh:(b + 1) * nh],
                                            mix[:, b, 0:nh * HD].rearrange("p (h d) -> p h d", d=HD), AX_X, ALU.add)
                ins.then_inc(qss_made, 1)

            def scale_heads(q, src, c0, nh):
                dve.wait_ge(qsqrt_made, q + 1)
                chained(dve.reciprocal(qss[:, 1, 0:NB * nh], qss[:, 1, 0:NB * nh]))
                for b in range(NB):
                    v = src[:, b, c0:c0 + nh * HD].rearrange("p (h d) -> p h d", d=HD)
                    ins = dve.tensor_tensor(v, v, bcast(qss[:, 1, b * nh:(b + 1) * nh], HD), ALU.mult)
                ins.then_inc(qk_made, 1)

            def softmax_sides(first, todo, mixcol, between=None):
                for i in range(len(todo) + 2):
                    if i < len(todo):
                        h = first + i
                        kind, hh = todo[i][0], todo[i][6]
                        dve.wait_ge(s_psum, h + 1)
                        if i >= 2:
                            dve.wait_ge(s_exp, h - 1)
                        src = bank[i % 2][:].rearrange("p (b s) -> p b s", b=NB)
                        if kind == 0:
                            for b in range(NB):
                                c0 = P * (1 - b)
                                ins = dve.tensor_tensor(sc[:, i % 2, b, :], src[:, b, :], relT[:, hh, c0:c0 + S], ALU.add)
                            ins.then_inc(s_sb, 1)
                            dve.wait_ge(s_sb, h + 1)
                            src = sc[:, i % 2, :, :]
                        elif kind == 1:
                            for b in range(NB):
                                ins = dve.scalar_tensor_tensor(sc[:, i % 2, b, :], src[:, b, :], negc[:, b, hh:hh + 1],
                                                               decay[:, hh, :], ALU.subtract, ALU.add)
                            ins.then_inc(s_sb, 1)
                            dve.wait_ge(s_sb, h + 1)
                            src = sc[:, i % 2, :, :]
                        dve.tensor_reduce(nmax[:, i % 2, :], src, AX_X, ALU.max, negate=True).then_inc(s_max, 1)
                    if i >= 2:
                        h, k = first + i - 2, (i - 2) % 2
                        dve.wait_ge(s_exp, h + 1)
                        chained(dve.reciprocal(rinv[:, k, :], psumr[:, k, :]))
                        dve.wait_ge(o_psum, h + 1)
                        for b in range(NB):
                            c0 = mixcol + (i - 2) * HD
                            dve.tensor_scalar(mix[:, b, c0:c0 + HD], bank[4 + k][:, b * HD:(b + 1) * HD],
                                              rinv[:, k, b:b + 1], None, ALU.mult).then_inc(o_sb, 1)
                    if between is not None:
                        between(i)

            chained(dve.memset(eps[:], EPS))
            dve.memset(zT[:], 0.0)
            chained(dve.memset(uT[:], 0.0))
            norm_lo("norm1", NORM1, 0)
            lo_to(0)
            norm_lo("norm1", NORM1, 1)
            lo_to(2)
            dve.wait_ge(rstd_made, 1)
            for k in range(5):
                g_end = at["in0"]["g"] + 2 * k + 1
                lo_to(g_end + 2)
                copy_out(at["in0"]["j"] + k, g_end, proj0[:, 1, 512 * k:512 * (k + 1)], NORM1)
                if k == 0:
                    dve.wait_ge(const_in, 16 * len(LOADS["const"]))
                    for i in (GQ0, GFQ, GMQ0, GMQ1):
                        ins = dve.tensor_scalar(hcol[:, i:i + 1], hcol[:, i:i + 1], HD ** -0.5, None, ALU.mult)
                    chained(ins)
                    dve.wait_ge(rel_in, 16)
                    dve.tensor_copy(rel_row[:, 0:127], bcast(rel_row[:, 127], 127))
                    dve.tensor_copy(rel_row[:, 384:], bcast(rel_row[:, 383], REL_LEN + 1 - 384)).then_inc(rel_ext, 1)
                if k == 1:
                    sum_heads(0, REL_HEADS)
                if k == 2:
                    scale_heads(0, proj0, 0, REL_HEADS)
                    sum_heads(1, REL_HEADS)
                if k == 3:
                    scale_heads(1, proj0, 512, REL_HEADS)
            lo_to(at["out0"]["g"] + 2)
            dve.wait_ge(rel_back, 16)
            t = at["conv0"]["t"]
            dve.wait_ge(early_in, 16 * (len(LOADS["early"]) + 4))
            dve.wait_ge(t_act, act_steps(t + 3))
            chained(dve.tensor_tensor(zT[:, :, CONV_K - 1:], gcT, hiT, ALU.mult))
            for i in range(CONV_K):
                for k in range(2):
                    z = zT[:, k, i:i + S]
                    if i == 0:
                        ins = dve.tensor_scalar(yT[:, k, :], z, cw[:, k, 0:1], None, ALU.mult)
                    else:
                        ins = dve.scalar_tensor_tensor(yT[:, k, :], z, cw[:, k, i:i + 1], yT[:, k, :], ALU.mult, ALU.add)
                chained(ins)
            dve.tensor_tensor(yT[:], yT[:], gbT, ALU.mult).then_inc(y_made, 1)
            prev = uT
            for n, w in enumerate(POOL_WINDOWS):
                cur = win[:, n % 2]
                before = uT[:] if n == 0 else win[:, (n - 1) % 2]
                lo_i = w - 1
                chained(dve.tensor_tensor(cur[:, :, lo_i:], before[:, :, lo_i:], before[:, :, lo_i - w // 2:S + 16 - w // 2],
                                          ALU.add))
                k, r = n // 2, (n % 2) * HD
                ins = dve.tensor_tensor(mT[r:r + HD, k, :], cur[r:r + HD, k, 16:], invcnt[r:r + HD, k, :], ALU.mult)
            chained(ins)
            dve.tensor_tensor(mT, mT, uT[:, :, 16:], ALU.subtract).then_inc(m_made, 1)
            softmax_sides(at["heads0"]["h"], HEADS0, 0)
            dve.wait_ge(cp_hi, 1)
            dve.tensor_tensor(a_at(a_lo, "mix0", 4, 2), yT[:], a_at(a_hi, "mix0", 4, 2).bitcast(F32), ALU.subtract).then_inc(cp_lo, 1)
            dve.wait_ge(cp_hi, 2)
            for k in range(2):
                ins = dve.scalar_tensor_tensor(a_at(a_lo, "mix0", 6 + k)[:, 0, :], bank[0][:, k * S:(k + 1) * S], pscale[:, k:k + 1],
                                               a_at(a_hi, "mix0", 6 + k)[:, 0, :].bitcast(F32), ALU.mult, ALU.subtract)
            ins.then_inc(cp_lo, 1)
            for k in range(2):
                t_lo(at["mix0"]["t"] + k, a_at(a_lo, "mix0", 2 * k, 2), a_at(a_hi, "mix0", 2 * k, 2))
            add_out("out0", "norm2", NORM2)
            g = at["ff0"]["g"]
            t = at["ff0"]["t"]
            for c in range(FF0_CHUNKS + 1):
                first = g + (0 if c == 0 else 2 + 4 * (c - 1))
                if c >= 1:
                    lo_to(first + 2)
                    t = mem_lo(t, c, NMEM0)
                    for k in range(2):
                        t_lo(t, f_lo[:, (c - 1) % 2, 2 * k:2 * k + 2, :], f_hi[:, (c - 1) % 2, 2 * k:2 * k + 2, :])
                        t += 1
                lo_to(first + (3 if c < FF0_CHUNKS else 1))
            add_acc("mem0", "nmix0", NMIX0, NMEM0, kvm1[:, 1, :])
            for k, (c0, n) in enumerate(FOX_JOBS):
                g_end = at["in1"]["g"] + 2 * k + 1
                lo_to(g_end + 2)
                copy_out(at["in1"]["j"] + k, g_end, proj1[:, 1, c0:c0 + n], NMIX0)
                if k == 0:
                    dve.wait_ge(l1_in, 16)
                    dve.wait_ge(j_act, plain_jobs(at["in1"]["j"]))
                    dve.wait_ge(j_dve, plain_jobs(at["in1"]["j"]))
                    for b in range(NB):
                        ins = dve.tensor_tensor(lf[:, 0, b, :], proj1[:, b, c0:c0 + n], fb[:], ALU.add)
                    chained(ins)
                    dve.scalar_tensor_tensor(lf[:, 1], lf[:, 0], -1.0, lf[:, 0], ALU.mult, ALU.max).then_inc(lf_x, 1)
                if k == 2:
                    dve.wait_ge(lf_ln, 1)
                    dve.scalar_tensor_tensor(lf[:, 3], lf[:, 0], 0.0, lf[:, 2], ALU.min, ALU.subtract).then_inc(lf_made, 1)
                if k == 3:
                    sum_heads(2, FOX_HEADS)
                if k == 4:
                    scale_heads(2, proj1, 0, FOX_HEADS)
                    sum_heads(3, FOX_HEADS)
                if k == 6:
                    scale_heads(3, proj1, FOXW, FOX_HEADS)
            dve.wait_ge(c_psum, 1)
            dve.tensor_copy(negc[:], bank[4][:, 0:NB * FOX_HEADS].rearrange("p (b h) -> p b h", b=NB)).then_inc(c_sb, 1)
            sum_heads(4, MEM_HEADS)
            scale_heads(4, proj1, MQ1, MEM_HEADS)
            sum_heads(5, MEM_HEADS)
            scale_heads(5, kvm1, 0, MEM_HEADS)
            lo_to(at["out1"]["g"] + 2)
            dve.wait_ge(dec_sb, FOX_HEADS // 2)
            softmax_sides(at["heads1"]["h"], HEADS1, 0)
            for k in range(4):
                t_lo(at["mix1"]["t"] + k, a_at(a_lo, "mix1", 2 * k, 2), a_at(a_hi, "mix1", 2 * k, 2))
            add_out("out1", "nffn0", NFFN0)
            g = at["ff1"]["g"]
            t = at["ff1"]["t"]
            for c in range(FF1_CHUNKS + 1):
                first = g + (0 if c == 0 else 2 + 3 * (c - 1))
                if c >= 1:
                    lo_to(first + 2)
                    t = mem_lo(t, c, NMEM1)
                    t_lo(t, f_lo[:, (c - 1) % 2, 0:2, :], f_hi[:, (c - 1) % 2, 0:2, :])
                    t += 1
                if c < FF1_CHUNKS:
                    lo_to(first + 3)
                    for b in range(NB):
                        dve.wait_ge(silu_made, 2 * c + b + 1)
                        dve.scalar_tensor_tensor(f_sb[:, c % 2, b, 0:256], bank[4 + b][:, 256:512],
                                                 rstd[:, NFFN0, b:b + 1], f_sb[:, c % 2, b, 256:512],
                                                 ALU.mult, ALU.mult).then_inc(h_made, 1)
                else:
                    lo_to(first)
            add_acc("mem1", "nmix1", NMIX1, NMEM1, kvm2[:, 1, :])
            for k, (c0, n) in enumerate(CONV_JOBS):
                g_end = at["in2"]["g"] + 2 * k + 1
                lo_to(g_end + 2)
                copy_out(at["in2"]["j"] + k, g_end, proj2[:, 1, c0:c0 + n], NMIX1)
            dve.wait_ge(l2_in, 16 * len(LOADS["l2"]))
            chained(dve.memset(glu[:, :, 0:DW_K - 1], 0.0))
            chained(dve.memset(onesm[:], 1.0 / (CONV_TILES * P)))
            sum_heads(6, MEM_HEADS)
            scale_heads(6, proj2, MQ2, MEM_HEADS)
            sum_heads(7, MEM_HEADS)
            scale_heads(7, kvm2, 0, MEM_HEADS)
            lo_to(at["out2"]["g"] + 2)
            t = at["glu"]["t"]
            for k in range(3):
                dve.wait_ge(t_act, act_steps(t + 2 * k))
                dve.wait_ge(t_psum, t + 2 * k + 2)
                for m in range(2):
                    ch = 2 * k + m
                    ins = dve.scalar_tensor_tensor(glu[:, ch, DW_K - 1:], bank[6 + (t + 2 * k + 1) % 2][:, m * S:(m + 1) * S],
                                                   cb_in[:, ch:ch + 1], sig[:, m, :], ALU.add, ALU.mult)
                ins.then_inc(t_dve, 1)
            dve.wait_ge(t_dve, dve_steps(t + 5))

            def add_taps(k):
                return dve.tensor_tensor(dwy[:, k, :], dwy[:, k, :], bank[6 + k % 2][:, 0:S], ALU.add)

            def other_taps(k):
                for i in range(PE_TAPS, DW_K):
                    u, y = glu[:, k, i:i + S], (dwy[:, k, :], stat[:, 0, :])[(i - PE_TAPS) % 2]
                    if i == PE_TAPS:
                        ins = dve.tensor_scalar(y, u, dw[:, k, i:i + 1], dwb[:, k:k + 1], ALU.mult, ALU.add)
                    elif i == PE_TAPS + 1:
                        ins = dve.tensor_scalar(y, u, dw[:, k, i:i + 1], None, ALU.mult)
                    else:
                        dve.wait_ge(dve_own, own[0] - 1)
                        ins = dve.scalar_tensor_tensor(y, u, dw[:, k, i:i + 1], y, ALU.mult, ALU.add)
                    own[0] += 1
                    ins.then_inc(dve_own, 1)
                dve.wait_ge(dve_own, own[0])
                chained(dve.tensor_tensor(dwy[:, k, :], dwy[:, k, :], stat[:, 0, :], ALU.add))
                if k >= 1:
                    dve.wait_ge(tap_used, k * PE_TAPS)
                    add_taps(k - 1).then_inc(dw_acc, 1)

            softmax_sides(at["heads2"]["h"], HEADS2, 768, other_taps)
            dve.wait_ge(tap_used, CONV_TILES * PE_TAPS)
            add_taps(CONV_TILES - 1).then_inc(dw_acc, 1)
            dve.wait_ge(mu_psum, 1)
            dve.tensor_copy(stat[:, 0, :], bank[0][:, 0:S]).then_inc(mu_made, 1)
            dve.wait_ge(mu_made, 1)
            for k in range(CONV_TILES):
                ins = dve.tensor_tensor(dwy[:, k, :], dwy[:, k, :], stat[:, 0, :], ALU.subtract)
            ins.then_inc(cent_made, 1)
            t_lo(at["mix2"]["t"], a_at(a_lo, "mix2", 6, 2), a_at(a_hi, "mix2", 6, 2))
            dve.wait_ge(sd_made, 1)
            chained(dve.reciprocal(stat[:, 2, :], stat[:, 1, :]))
            dve.wait_ge(cent_made, 1)
            for k in range(CONV_TILES):
                ins = dve.tensor_tensor(dwy[:, k, :], dwy[:, k, :], stat[:, 2, :], ALU.mult)
            ins.then_inc(ln_made, 1)
            for k in range(0, CONV_TILES, 2):
                dve.wait_ge(ln_hi, k // 2 + 1)
                dve.tensor_tensor(a_at(a_lo, "mix2", k, 2), dwq[:, k:k + 2, :], a_at(a_hi, "mix2", k, 2).bitcast(F32),
                                  ALU.subtract).then_inc(ln_lo, 1)
            dve.wait_ge(router_hi_made, 1)
            dve.tensor_tensor(router_lo[:], router[:], router_hi[:].bitcast(F32), ALU.subtract).then_inc(router_lo_made, 1)
            add_out("out2", "nffn1", NFFN1)
            dve.wait_ge(moe_in, 16 * len(LOADS["moe"]))
            for b in range(NB):
                dve.scalar_tensor_tensor(zrow[:, b, :], x[:, b, :], rstd[:, NFFN1, b:b + 1], gain_b[:], ALU.mult, ALU.mult)\
                    .then_inc(z_made, 1)
            dve.wait_ge(r_psum, 1)
            dve.tensor_copy(logit_t[:], bank[4][0:N_EXPERTS, 0:S]).then_inc(r_sb, 1)
            dve.wait_ge(rt_psum, 1)
            for b in range(NB):
                ins = dve.tensor_scalar(logit[:, b, :], bank[5][:, b * N_EXPERTS:(b + 1) * N_EXPERTS],
                                        rstd[:, NFFN1, b:b + 1], None, ALU.mult)
            chained(ins)
            for b in range(NB):
                ins = dve.max(top[:, b, :], logit[:, b, :])
            chained(ins)
            for b in range(NB):
                ins = dve.max_index(topi[:, b, :], top[:, b, :], logit[:, b, :])
            chained(ins)
            chained(dve.tensor_copy(topf[:], topi[:]))
            dve.tensor_tensor(gate[:, 0, :], top[:, :, 1], top[:, :, 0], ALU.subtract).then_inc(gap_made, 1)
            for b in range(NB):
                for m in range(2):
                    ins = dve.tensor_scalar(onehot[:, m, b, :], iota[:, 0:N_EXPERTS], topf[:, b, m:m + 1], None, ALU.is_equal)
            chained(ins)
            dve.tensor_tensor(chosen[:], onehot[:, 0], onehot[:, 1], ALU.add).then_inc(ch_made, 1)
            dve.wait_ge(zhi_made, 1)
            dve.tensor_tensor(z_lo[:], zrow[:], z_hi[:].bitcast(F32), ALU.subtract).then_inc(zlo_made, 1)
            dve.wait_ge(g_exp, 1)
            chained(dve.tensor_scalar(gate[:, 2, :], gate[:, 1, :], 1.0, None, ALU.add))
            chained(dve.reciprocal(gate[:, 2, :], gate[:, 2, :]))
            chained(dve.tensor_tensor(gate[:, 3, :], gate[:, 1, :], gate[:, 2, :], ALU.mult))
            for b in range(NB):
                chained(dve.tensor_scalar(gates[:, b, 0:N_EXPERTS], onehot[:, 0, b, :], gate[:, 2, b:b + 1], None, ALU.mult))
                chained(dve.scalar_tensor_tensor(gates[:, b, 0:N_EXPERTS], onehot[:, 1, b, :], gate[:, 3, b:b + 1],
                                                 gates[:, b, 0:N_EXPERTS], ALU.mult, ALU.add))
            chained(dve.tensor_copy(gates[:, :, N_EXPERTS:], gates[:, :, 0:N_EXPERTS]))
            dve.wait_ge(rk_psum, 1)
            dve.wait_ge(ch_made, 1)
            chained(dve.scalar_tensor_tensor(rank[:, :, 0:N_EXPERTS],
                                             bank[4][:, 0:NB * N_EXPERTS].rearrange("p (b e) -> p b e", b=NB), -1.0,
                                             chosen[:], ALU.mult, ALU.mult))
            chained(dve.tensor_scalar(rank[:, :, 0:N_EXPERTS], rank[:, :, 0:N_EXPERTS], -1.0, None, ALU.add))
            chained(dve.tensor_scalar(rank[:, :, N_EXPERTS:2 * N_EXPERTS], rank[:, :, 0:N_EXPERTS], -float(P), None, ALU.add))
            for b in range(NB):
                ins = dve.tensor_scalar(pick[:, b, :], iota[:], rank[:, b, 0:1], None, ALU.is_equal)
            ins.then_inc(pick_made, 1)
            chained(dve.memset(rank[:, :, 2 * N_EXPERTS:], -1.0))
            dve.memset(pickgT[:], 0.0)
            chained(dve.tensor_reduce(count[:, 0:1], bank[4][:, 16:24], AX_X, ALU.min))
            chained(dve.tensor_scalar(count[:, 1:2], count[:, 0:1], -float(P), float(N_EXPERTS), ALU.is_lt, ALU.mult))
            dve.tensor_scalar(n_items[:], count[:, 1:2], float(N_EXPERTS), None, ALU.add).then_inc(items_made, 1)

            def xg_lo_out(k, src):
                dve.tensor_tensor(xg_lo[:, 4 * k:4 * k + 4, :], src[:].rearrange("p (k s) -> p k s", k=4),
                                  xg_hi[:, 4 * k:4 * k + 4, :].bitcast(F32), ALU.subtract).then_inc(t_dve, 1)

            def y_out():
                dve.tensor_copy(y_sb[:, 512:D], bank[1][:]).then_inc(y_dve, 1)

            def add_y(n):
                b, half = n // 2, n % 2
                xs = x[:, b, half * 512:(half + 1) * 512]
                dve.tensor_tensor(xs, xs, bank[2 - 2 * b + half][:], ALU.add).then_inc(x_upd, 1)

            for k in range(2):
                dve.wait_ge(t_act, TA + k + 1)
                xg_lo_out(k, bank[6 + (TM + k) % 2])
            dve.wait_ge(items_made, 1)
            items = dve.value_load(n_items[0:1, 0:1], min_val=N_EXPERTS, max_val=2 * N_EXPERTS)
            with dve.Fori(0, items) as i:
                def e_lo(k):
                    g = NG + k
                    dve.wait_ge(hi_made, i * MOE_GRANULES + (g + 1))
                    dve.tensor_tensor(w_lo[:, g % NSPLIT, :], raw_at(g, GRAN), w_hi[:, g % NSPLIT, :].bitcast(F32),
                                      ALU.subtract).then_inc(lo_made, 1)

                def step_hi(k):
                    dve.wait_ge(t_act, i * MOE_TSTEPS + (TA + 2 + k + 1))

                def chunk_lo(c):
                    step_hi(CHUNK_STEP[c])
                    dve.tensor_tensor(mf_lo[:, (c - 1) % 2, :, :],
                                      bank[6 + (TM + CHUNK_STEP[c]) % 2][:].rearrange("p (k s) -> p k s", k=4),
                                      mf_hi[:, (c - 1) % 2, :, :].bitcast(F32), ALU.subtract).then_inc(t_dve, 1)

                for k in range(2):
                    e_lo(k)
                dve.wait_ge(w_used, i * MOE_GRANULES + NG)
                y_out()
                k = 2
                for c in range(MOE_CHUNKS + 1):
                    while k <= min(moe_first(c) + (3 if c < MOE_CHUNKS else 1), MOE_GRANULES - 1):
                        e_lo(k)
                        k += 1
                    if c == 0:
                        for n in range(4):
                            dve.wait_ge(sc_psum, i * 4 + (n + 1))
                            add_y(n)
                    if c == PICKG_CHUNK - 1:
                        for b in range(NB):
                            ins = dve.tensor_scalar(pickg[:, b, :], iota[:], rank[:, b, bass.ds(i, 1)],
                                                    gates[:, b, bass.ds(i, 1)], ALU.is_equal, ALU.mult)
                        ins.then_inc(pickg_made, 1)
                    if c == PICKG_CHUNK:
                        step_hi(PICKG_STEP)
                        dve.tensor_copy(pickgT[:, P:S], bank[6 + (TM + PICKG_STEP) % 2][:, P:S]).then_inc(t_dve, 1)
                    if c == GATHER_CHUNK - 1:
                        for b in range(NB):
                            ins = dve.tensor_scalar(pick[:, b, :], iota[:], rank[:, b, bass.ds(i + 1, 1)], None, ALU.is_equal)
                        ins.then_inc(pick_made, 1)
                    if 1 <= c < MOE_CHUNKS:
                        chunk_lo(c)
                    if c < MOE_CHUNKS:
                        while k <= min(moe_first(c) + 5, MOE_GRANULES - 1):
                            e_lo(k)
                            k += 1
                        ub = bank[5] if c % 2 == 0 else bank[3]
                        dve.wait_ge(silu_made, i * MOE_CHUNKS + (SM + c + 1))
                        dve.wait_ge(w_used, i * MOE_GRANULES + (NG + moe_first(c) + 4))
                        dve.tensor_tensor(mf_sb[:, c % 2, 1, :], mf_sb[:, c % 2, 0, :], ub[:], ALU.mult).then_inc(h_made, 1)
                    if c == GATHER_CHUNK:
                        for kk in range(2):
                            step_hi(GATHER_STEP + kk)
                            xg_lo_out(kk, bank[6 + (TM + GATHER_STEP + kk) % 2])
                        chunk_lo(c + 1)
            dve.wait_ge(w_used, items * MOE_GRANULES + NG)
            y_out()
            for n in range(4):
                dve.wait_ge(sc_psum, items * 4 + (n + 1))
                add_y(n)


def kernel(**inputs):
    import numpy as np
    from concourse import bacc
    from concourse.bass_utils import run_bass_kernel_spmd

    v = {name: np.ascontiguousarray(array) for name, array in inputs.items()}

    def cols(array, tiles):
        r = array.reshape(*array.shape[:-1], tiles, P)
        return np.ascontiguousarray(np.moveaxis(r, -1, 0))

    norms = [v["norm1_g"][0], v["norm2_g"][0], v["norm_mem_2"][0], v["norm_mix_2"][0], v["norm_ffn_2"][0],
             v["norm_mem_2"][1], v["norm_mix_2"][1], v["norm_ffn_2"][1]]
    heads = [v["q_norm_g"][0], v["k_norm_g"][0], v["fox_g_q_2"][0], v["fox_g_k_2"][0], v["g_mq_2"][0], v["g_mk_2"][0],
             v["g_mq_2"][1], v["g_mk_2"][1]]
    arrays = dict(
        g_norms=cols(np.stack(norms), KT),
        g_heads=np.ascontiguousarray(np.stack(heads).T),
        rel_bias=np.ascontiguousarray(v["rel_bias"][0][:, ::-1]),
        conv_w=np.ascontiguousarray(cols(v["conv_w"][0], 2).transpose(0, 2, 1)),
        pool_scale=cols(v["pool_scale"][0], 2),
        conv_b_in_2=cols(v["conv_b_in_2"][0], 2 * CONV_TILES),
        conv_dw_2=np.ascontiguousarray(cols(v["conv_dw_2"][0], CONV_TILES).transpose(0, 2, 1)),
        conv_dw_b_2=cols(v["conv_dw_b_2"][0], CONV_TILES),
        conv_ln_g_2=cols(v["conv_ln_g_2"][0], CONV_TILES),
        conv_ln_b_2=cols(v["conv_ln_b_2"][0], CONV_TILES),
    )
    for name in ("x", "w_in", "pool_w", "w_out", "w_mlp1", "w_mlp2", "mem_2", "norm_ffn_2", "w_mem_kv_2",
                 "fox_w_in_2", "fox_b_f_2", "fox_w_out_2", "conv_w_in_2", "conv_w_out_2", "ffn_w_gate_2",
                 "ffn_w_up_2", "ffn_w_down_2", "moe_router_2", "moe_w_gate_2", "moe_w_up_2", "moe_w_down_2"):
        arrays[name] = v[name]

    f = np.float32
    p, t = np.arange(P), np.arange(S)
    key, query = t[None, None, :], p[:, None, None] + P * np.arange(NB)[None, :, None]
    arrays["c_ident"] = np.eye(P, dtype=f)
    arrays["c_iota"] = np.broadcast_to(p.astype(f), (P, P)).copy()
    arrays["c_negtri"] = np.where(query <= key, f(-1), f(0)).astype(f)
    arrays["c_masks"] = np.stack([np.where(key // 64 <= query // 64, f(0), f(-1e30)),
                                  np.where(key <= query, f(0), f(-1e30))], axis=1).astype(f)
    windows = np.array(POOL_WINDOWS).reshape(2, 2).repeat(HD, axis=1).T
    arrays["c_invcnt"] = (1.0 / np.minimum(t[None, None, :] + 1, windows[:, :, None])).astype(f)

    nc = bacc.Bacc("TRN2", target_bir_lowering=False, num_devices=1, dynamic_dma_scratch_size=1024)
    a = {name: nc.dram_tensor(f"in_{name}", array.shape, F32, kind="ExternalInput").ap()
         for name, array in arrays.items()}
    out = nc.dram_tensor("out", (1, S, D), F32, kind="ExternalOutput").ap()
    block_kernel(nc, a, out)
    r = run_bass_kernel_spmd(nc, [{f"in_{name}": array for name, array in arrays.items()}], core_ids=[0])
    return r.results[0]["out"]
```

```python
from contextlib import ExitStack

import concourse.bass as bass
from concourse import mybir

F32 = mybir.dt.float32
F32R = mybir.dt.float32r
I32 = mybir.dt.int32
U32 = mybir.dt.uint32
ALU = mybir.AluOpType
ACT = mybir.ActivationFunctionType
AX_X = mybir.AxisListType.X

P = 128
D = 1024
KT = D // P
S = 256
NB = S // P
HD = 64
EPS = 1e-6
GRAN = 2048
NRAW = 6
NSPLIT = 3

REL_HEADS = 8
FOX_HEADS = 12
MEM_HEADS = 4
CONV_K = 3
POOL_WINDOWS = (2, 4, 8, 16)
DW_K = 31
CONV_TILES = 6
PE_TAPS = 16
N_DIAG = 12
N_EXPERTS = 8
EXPERT_FF = 3584
MOE_CHUNKS = EXPERT_FF // 512
MOE_GRANULES = 6 * MOE_CHUNKS
MOE_TSTEPS = 3 + MOE_CHUNKS
AHEAD = 3
PICKG_CHUNK, GATHER_CHUNK = 3, MOE_CHUNKS - 1

NORM1, NORM2, NMEM0, NMIX0, NFFN0, NMEM1, NMIX1, NFFN1 = range(8)
A_STAGES = ("norm1", "mix0", "norm2", "nmix0", "mix1", "nffn0", "nmix1", "mix2", "nffn1")
A_TILES = 12
MEM_CHUNKS = range(2, 6)
GQ0, GK0, GFQ, GFK, GMQ0, GMK0, GMQ1, GMK1 = range(8)

REL_LEN = 2 * 255 + 1


def bcast(ap, n):
    return bass.AP(ap.tensor, ap.offset, [*[list(d) for d in ap.ap], [0, n]])


def a_at(buf, name, kt, n=1):
    i = (A_STAGES.index(name) * KT + kt) % A_TILES
    return buf[:, i:i + n, :]


def plan():
    at, n = {}, dict(g=0, t=0, j=0, h=0)
    kinds = []

    def stage(name, g=0, t="", j=0, h=0):
        at[name] = dict(n)
        n["g"] += g
        n["t"] += len(t)
        kinds.extend(t)
        n["j"] += j
        n["h"] += h

    stage("norm1", t="bbbb")
    stage("in0", g=10, j=5)
    stage("conv0", t="aaaa")
    stage("qk0", t="aaaa")
    stage("heads0", h=REL_HEADS)
    stage("mix0", t="bb")
    stage("out0", g=4, j=2)
    stage("norm2", t="bbbb")
    stage("ff0", g=33, t="b" * (16 + len(MEM_CHUNKS)))
    stage("mem0", g=1)
    stage("nmix0", t="bbbb")
    stage("in1", g=16, j=8)
    stage("qk1", t="a" * 8)
    stage("heads1", h=FOX_HEADS + MEM_HEADS)
    stage("mix1", t="bbbb")
    stage("out1", g=4, j=2)
    stage("nffn0", t="bbbb")
    stage("ff1", g=34, t="b" * (11 + len(MEM_CHUNKS)))
    stage("mem1", g=1)
    stage("nmix1", t="bbbb")
    stage("in2", g=8, j=4)
    stage("glu", t="adadad")
    stage("qk2", t="aa")
    stage("heads2", h=MEM_HEADS)
    stage("mix2", t="b")
    stage("out2", g=4, j=2)
    stage("nffn1", t="bbbb")
    stage("moe")
    return at, "".join(kinds)


def block_kernel(nc, a, out):
    at, tkinds = plan()
    is_out_job = [False] * at["moe"]["j"]
    for name in ("out0", "out1", "out2"):
        for k in range(2):
            is_out_job[at[name]["j"] + k] = True

    stream = []

    def rows(w, r0, kts, c0, n):
        return w[r0:r0 + kts * P, c0:c0 + n].rearrange("(t p) n -> p t n", p=P)

    def project(w, c0, n):
        for half in range(2):
            stream.append(([rows(w, half * 512, 4, c0, n)], 4, n))

    w_in, w_out, w1, w2 = a["w_in"][0], a["w_out"][0], a["w_mlp1"][0], a["w_mlp2"][0]
    fox_in, fox_out = a["fox_w_in_2"][0], a["fox_w_out_2"][0]
    fg, fu, fd = a["ffn_w_gate_2"][0], a["ffn_w_up_2"][0], a["ffn_w_down_2"][0]
    conv_in, conv_out = a["conv_w_in_2"][0], a["conv_w_out_2"][0]
    kv = a["w_mem_kv_2"]
    eg, eu, ed = a["moe_w_gate_2"][0], a["moe_w_up_2"][0], a["moe_w_down_2"][0]
    FF0_CHUNKS = w1.shape[1] // 512
    FF1_CHUNKS = fg.shape[1] // 256
    FOXW = FOX_HEADS * HD
    FOX_JOBS = [(3 * FOXW, FOX_HEADS)] + [(c * 384, 384) for c in range(6)] + [(3 * FOXW + FOX_HEADS, 256)]
    CONV_JOBS = [(0, 512), (512, 512), (1024, 512), (1536, 256)]

    for c in range(5):
        project(w_in, c * 512, 512)
    for c in range(2):
        project(w_out, c * 512, 512)
    for c in range(FF0_CHUNKS + 1):
        if c < FF0_CHUNKS:
            project(w1, c * 512, 512)
        else:
            stream.append(([rows(kv[0], 0, 4, 0, 512)], 4, 512))
        if c >= 1:
            for k in range(2):
                stream.append(([rows(w2, (c - 1) * 512 + k * 256, 2, 0, D)], 2, D))
    stream.append(([rows(kv[0], 512, 4, 0, 512)], 4, 512))
    for c0, n in FOX_JOBS:
        project(fox_in, c0, n)
    for c in range(2):
        project(fox_out, c * 512, 512)
    for c in range(FF1_CHUNKS + 1):
        if c < FF1_CHUNKS:
            for half in range(2):
                stream.append(([rows(fg, half * 512, 4, c * 256, 256), rows(fu, half * 512, 4, c * 256, 256)], 4, 512))
        else:
            stream.append(([rows(kv[1], 0, 4, 0, 512)], 4, 512))
        if c >= 1:
            stream.append(([rows(fd, (c - 1) * 256, 2, 0, D)], 2, D))
    stream.append(([rows(kv[1], 512, 4, 0, 512)], 4, 512))
    for c0, n in CONV_JOBS:
        project(conv_in, c0, n)
    for c in range(2):
        project(conv_out, c * 512, 512)
    NG = len(stream)
    assert NG == at["moe"]["g"] and MOE_GRANULES % NRAW == 0 and MOE_GRANULES % NSPLIT == 0

    raw_count, seen = [], [0] * NRAW
    for g, (parts, _, _) in enumerate(stream):
        seen[g % NRAW] += 16 * len(parts)
        raw_count.append(seen[g % NRAW])
    raw_count += [seen[g % NRAW] + 16 for g in range(NG, NG + AHEAD)]

    def moe_first(c):
        return 0 if c == 0 else 4 + 6 * (c - 1)

    ctx = ExitStack()
    with ctx:
        def sb(name, shape, dt=F32, stack=ctx):
            return stack.enter_context(nc.sbuf_tensor(name, shape, dt))

        def sem(name):
            return ctx.enter_context(nc.semaphore(name))

        x = sb("x", [P, NB, D])
        raw = sb("raw", [P, NRAW, GRAN])
        w_hi = sb("w_hi", [P, NSPLIT, GRAN], F32R)
        w_lo = sb("w_lo", [P, NSPLIT, GRAN], F32R)
        a_hi = sb("a_hi", [P, A_TILES, S], F32R)
        a_lo = sb("a_lo", [P, A_TILES, S], F32R)
        ident = sb("ident", [P, P])
        ident_r = sb("ident_r", [P, P], F32R)
        gcol = sb("gcol", [P, 8, KT])
        hcol = sb("hcol", [P, 8])
        ss = sb("ss", [P, 8, NB])
        ms = sb("ms", [P, 8, NB])
        rstd = sb("rstd", [P, 8, NB])
        mhalf = sb("mhalf", [P, NB * FOX_HEADS])
        eps = sb("eps", [P, 1])
        negtri = sb("negtri", [P, NB, S])
        iota = sb("iota", [P, P])
        mask_r = sb("mask_r", [P, 2, NB, S], F32R)

        mixers = ExitStack()
        mix = sb("mix", [P, NB, D], stack=mixers)
        qT = sb("qT", [P, 8, S], stack=mixers)
        kT = sb("kT", [P, 8, S], stack=mixers)
        sc = sb("sc", [P, 2, NB, S], stack=mixers)
        pr = sb("pr", [P, 2, NB, S], stack=mixers)
        pT = sb("pT", [P, 2, NB * S], stack=mixers)
        nmax = sb("nmax", [P, 2, NB], stack=mixers)
        psumr = sb("psumr", [P, 4, NB], stack=mixers)
        rinv = sb("rinv", [P, 4, NB], stack=mixers)
        qss = sb("qss", [P, 3, NB * FOX_HEADS], stack=mixers)
        layer = ExitStack()
        proj0 = sb("proj0", [P, NB, 2560], stack=layer)
        relT = sb("relT", [P, REL_HEADS, 384], stack=layer)
        rel_row = sb("rel_row", [REL_HEADS, REL_LEN + 1], stack=layer)
        gbT, gcT = qT[:, 4:6, :], qT[:, 6:8, :]
        hiT, mT = kT[:, 4:6, :], kT[:, 6:8, :]
        zT = sb("zT", [P, 2, S + 2], stack=layer)
        uT = sb("uT", [P, 2, S + 16], stack=layer)
        win = sb("win", [P, 2, 2, S + 16], stack=layer)
        invcnt = sb("invcnt", [P, 2, S], stack=layer)
        yT = sb("yT", [P, 2, S], stack=layer)
        cw = sb("cw", [P, 2, CONV_K], stack=layer)
        pscale = sb("pscale", [P, 2], stack=layer)
        pool_w = sb("pool_w", [P, 2, P], stack=layer)
        layer.close()
        layer = ExitStack()
        proj1 = sb("proj1", [P, NB, 2572], stack=layer)
        kvm1 = sb("kvm1", [P, NB, 512], stack=layer)
        decay = sb("decay", [P, FOX_HEADS, S], stack=layer)
        fb = sb("fb", [P, FOX_HEADS], stack=layer)
        lf = sb("lf", [P, 4, NB, FOX_HEADS], stack=layer)
        lf_hi = sb("lf_hi", [P, NB, FOX_HEADS], F32R, stack=layer)
        lf_lo = sb("lf_lo", [P, NB, FOX_HEADS], F32R, stack=layer)
        negtri_r = sb("negtri_r", [P, NB, S], F32R, stack=layer)
        negc = sb("negc", [P, NB, FOX_HEADS], stack=layer)
        layer.close()
        layer = ExitStack()
        proj2 = sb("proj2", [P, NB, 1792], stack=layer)
        sig = qT[:, 0:2, :]
        glu = sb("glu", [P, CONV_TILES, S + DW_K - 1], stack=layer)
        kvm2 = sb("kvm2", [P, NB, 512], stack=layer)
        dwy = sb("dwy", [P, CONV_TILES, S], stack=layer)
        dwq = sb("dwq", [P, CONV_TILES, S], stack=layer)
        diag = dwq[:].rearrange("p k s -> p (k s)").rearrange("p (n c) -> p n c", c=P)
        stat = sb("stat", [P, 3, S], stack=layer)
        cb_in = sb("cb_in", [P, 2 * CONV_TILES], stack=layer)
        dw = sb("dw", [P, CONV_TILES, DW_K], stack=layer)
        dwb = sb("dwb", [P, CONV_TILES], stack=layer)
        lng = sb("lng", [P, CONV_TILES], stack=layer)
        lnb = sb("lnb", [P, CONV_TILES], stack=layer)
        onesm = sb("onesm", [P, P], stack=layer)
        layer.close()
        mixers.close()
        ffs = ExitStack()
        f_sb = sb("f_sb", [P, 2, NB, 512], stack=ffs)
        f_hi = sb("f_hi", [P, 2, 4, S], F32R, stack=ffs)
        f_lo = sb("f_lo", [P, 2, 4, S], F32R, stack=ffs)
        m_hi = sb("m_hi", [P, KT, S], F32R, stack=ffs)
        m_lo = sb("m_lo", [P, KT, S], F32R, stack=ffs)
        mem = sb("mem", [P, NB, D], stack=ffs)
        squares_ff = sb("squares_ff", [P, NB, D], stack=ffs)
        ffs.close()
        moes = ExitStack()
        mf_sb = sb("mf_sb", [P, 2, 2, 512], stack=moes)
        mf_hi = sb("mf_hi", [P, 2, 4, P], F32R, stack=moes)
        mf_lo = sb("mf_lo", [P, 2, 4, P], F32R, stack=moes)
        xg_hi = sb("xg_hi", [P, KT, P], F32R, stack=moes)
        xg_lo = sb("xg_lo", [P, KT, P], F32R, stack=moes)
        y_sb = sb("y_sb", [P, D], stack=moes)
        zrow = sb("zrow", [P, NB, D], stack=moes)
        z_hi = sb("z_hi", [P, NB, D], F32R, stack=moes)
        z_lo = sb("z_lo", [P, NB, D], F32R, stack=moes)
        pick = sb("pick", [P, NB, P], F32R, stack=moes)
        pickg = sb("pickg", [P, NB, P], stack=moes)
        pickgT = sb("pickgT", [P, S], stack=moes)
        gain_b = sb("gain_b", [P, D], stack=moes)
        router = sb("router", [P, KT, N_EXPERTS], stack=moes)
        router_hi = sb("router_hi", [P, KT, N_EXPERTS], F32R, stack=moes)
        router_lo = sb("router_lo", [P, KT, N_EXPERTS], F32R, stack=moes)
        logit_t = sb("logit_t", [N_EXPERTS, S], stack=moes)
        logit = sb("logit", [P, NB, N_EXPERTS], stack=moes)
        top = sb("top", [P, NB, N_EXPERTS], stack=moes)
        topi = sb("topi", [P, NB, N_EXPERTS], U32, stack=moes)
        topf = sb("topf", [P, NB, N_EXPERTS], stack=moes)
        gate = sb("gate", [P, 4, NB], stack=moes)
        onehot = sb("onehot", [P, 2, NB, N_EXPERTS], stack=moes)
        chosen = sb("chosen", [P, NB, N_EXPERTS], stack=moes)
        rank = sb("rank", [P, NB, 2 * N_EXPERTS + 1], stack=moes)
        gates = sb("gates", [P, NB, 2 * N_EXPERTS], stack=moes)
        count = sb("count", [P, 2], stack=moes)
        n_items = sb("n_items", [P, 1], I32, stack=moes)
        moes.close()

        bank = [ctx.enter_context(nc.psum_tensor(f"bank{i}", [P, 512], F32)) for i in range(8)]

        rel_rows_dram = nc.dram_tensor("rel_rows_dram", (REL_HEADS, REL_LEN + 1), F32, kind="Internal").ap()
        rel_band_dram = nc.dram_tensor("rel_band_dram", (REL_HEADS, P, 384), F32, kind="Internal").ap()

        x_in = [sem(f"x_in{h}") for h in range(2)]
        raw_in = [sem(f"raw_in{i}") for i in range(NRAW)]
        hi_made, lo_made, w_used = sem("hi_made"), sem("lo_made"), sem("w_used")
        start_in, mem_in, const_in, early_in, l1_in, l2_in, moe_in = (
            sem(n) for n in ("start_in", "mem_in", "const_in", "early_in", "l1_in", "l2_in", "moe_in"))
        rel_in, rel_ext, rel_out, rel_band, rel_back = (
            sem(n) for n in ("rel_in", "rel_ext", "rel_out", "rel_band", "rel_back"))
        pool_zero, mask_made = sem("pool_zero"), sem("mask_made")
        ss_made, rstd_made = sem("ss_made"), sem("rstd_made")
        kv_act, kv_dve = sem("kv_act"), sem("kv_dve")
        t_psum, t_act, t_dve = sem("t_psum"), sem("t_act"), sem("t_dve")
        j_act, j_dve, x_upd = sem("j_act"), sem("j_dve"), sem("x_upd")
        sq_made, qss_made, qroot_made, qk_made = (sem(n) for n in ("sq_made", "qss_made", "qroot_made", "qk_made"))
        s_psum, s_sb, s_max, s_exp = sem("s_psum"), sem("s_sb"), sem("s_max"), sem("s_exp")
        p_psum, p_sb, o_psum, o_sb = sem("p_psum"), sem("p_sb"), sem("o_psum"), sem("o_sb")
        y_made, m_made, pool_psum, cp_hi, cp_lo = (sem(n) for n in ("y_made", "m_made", "pool_psum", "cp_hi", "cp_lo"))
        f_made, silu_made, h_made = sem("f_made"), sem("silu_made"), sem("h_made")
        lf_x, lf_ln, lf_made, lf_hi_made, lf_lo_made, c_psum, c_sb, dec_psum, dec_sb = (
            sem(n) for n in ("lf_x", "lf_ln", "lf_made", "lf_hi_made", "lf_lo_made", "c_psum", "c_sb", "dec_psum", "dec_sb"))
        diag_made, tap_used, dw_acc = sem("diag_made"), sem("tap_used"), sem("dw_acc")
        mu_psum, cent_made, sqc_made, var_psum, sd_made, ln_made, silu2 = (
            sem(n) for n in ("mu_psum", "cent_made", "sqc_made", "var_psum", "sd_made", "ln_made", "silu2"))
        ln_hi, ln_lo = sem("ln_hi"), sem("ln_lo")
        z_made, zhi_made, zlo_made, gap_made, router_hi_made, router_lo_made, r_sb, rt_psum, r_psum, g_exp, ch_made, rk_psum, items_made = (
            sem(n) for n in ("z_made", "zhi_made", "zlo_made", "gap_made", "router_hi_made", "router_lo_made", "r_sb", "rt_psum", "r_psum", "g_exp", "ch_made", "rk_psum", "items_made"))
        pickg_zero, pickg_made, pick_made, y_act, y_dve, sc_psum = sem("pickg_zero"), sem("pickg_made"), sem("pick_made"), sem("y_act"), sem("y_dve"), sem("sc_psum")
        act_own, dve_own, pool_own = sem("act_own"), sem("dve_own"), sem("pool_own")
        out_done = sem("out_done")

        def raw_at(g, n):
            return raw[:, g % NRAW, 0:n]

        def n_el(g):
            return stream[g][1] * stream[g][2] if g < NG else GRAN

        def act_steps(t):
            return sum(k in "ab" for k in tkinds[:t + 1])

        def dve_steps(t):
            return sum(k in "bd" for k in tkinds[:t + 1])

        CHUNK_STEP = {c: c - 1 + (c >= PICKG_CHUNK) + 2 * (c > GATHER_CHUNK) for c in range(1, MOE_CHUNKS + 1)}
        PICKG_STEP, GATHER_STEP = PICKG_CHUNK - 1, GATHER_CHUNK + 1
        TA, TD, TM = act_steps(len(tkinds)), dve_steps(len(tkinds)), len(tkinds)

        def plain_jobs(j):
            return sum(not o for o in is_out_job[:j + 1])

        LOADS = dict(
            const=[(hcol[0:HD, :], a["g_heads"]),
                   (hcol[HD:P, :], a["g_heads"]), (negtri[:], a["c_negtri"]), (iota[:], a["c_iota"]),
                   (pr[:], a["c_masks"])],
            early=[(invcnt[:], a["c_invcnt"]), (cw[:], a["conv_w"]), (pscale[:], a["pool_scale"])],
            l1=[(fb[:], bass.AP(a["fox_b_f_2"].tensor, 0, [[0, P], [1, FOX_HEADS]]))],
            l2=[(cb_in[:], a["conv_b_in_2"]), (dw[:], a["conv_dw_2"]), (dwb[:], a["conv_dw_b_2"]),
                (lng[:], a["conv_ln_g_2"]), (lnb[:], a["conv_ln_b_2"])],
            moe=[(router[:], a["moe_router_2"][0].rearrange("(t p) e -> p t e", p=P)),
                 (gain_b[:], bass.AP(a["norm_ffn_2"].tensor, D, [[0, P], [1, D]]))],
        )

        HEADS0 = [(0, h // 2, h // 2, h % 2 * HD, proj0, 1024 + h * HD, h) for h in range(REL_HEADS)]
        HEADS1 = [(1, h // 2, h // 2, h % 2 * HD, proj1, 2 * FOXW + h * HD, h) for h in range(FOX_HEADS)]
        HEADS1 += [(None, 6 + h // 2, 6 + h // 2, h % 2 * HD, kvm1, 256 + h * HD, h) for h in range(MEM_HEADS)]
        HEADS2 = [(None, 6 + h // 2, 6 + h // 2, h % 2 * HD, kvm2, 256 + h * HD, h) for h in range(MEM_HEADS)]

        def keys(kind, b):
            return S if kind is None else (b + 1) * P

        def pt_at(kind, b, kt):
            return (kt * NB + b if kind is None else kt + b) * P

        MQ1, MQ2 = 3 * FOXW + FOX_HEADS, 1536
        memq, memk = qT[:, 6:8, :], kT[:, 6:8, :]
        at_x = dict(norm2=4, ff0=4, nmix0=8, nffn0=12, ff1=12, nmix1=16, nffn1=20, moe=20)
        HM = SM = 2 * FF1_CHUNKS

        def tokens(t):
            return t.rearrange("(b p) d -> p b d", p=P)

        block = ctx.enter_context(nc.Block())

        @block.sync
        def _(sp):
            sp.dma_start(ident[:], a["c_ident"]).then_inc(start_in, 16)
            sp.dma_start(gcol[:], a["g_norms"]).then_inc(start_in, 16)
            for h in range(2):
                sp.dma_start(x[:, :, h * 512:(h + 1) * 512], tokens(a["x"][0])[:, :, h * 512:(h + 1) * 512])\
                    .then_inc(x_in[h], 16)
            for g, (parts, kts, n) in enumerate(stream):
                if g >= NRAW:
                    sp.wait_ge(lo_made, g - NRAW + 1)
                if len(parts) == 1:
                    sp.dma_start(raw_at(g, kts * n).rearrange("p (t n) -> p t n", t=kts), parts[0])\
                        .then_inc(raw_in[g % NRAW], 16)
                else:
                    dst = raw_at(g, kts * n).rearrange("p (t u n) -> p t u n", t=kts, u=2)
                    for u in range(2):
                        sp.dma_start(dst[:, :, u, :], parts[u]).then_inc(raw_in[g % NRAW], 16)

            def load(i, k, src, kts):
                g = NG + k
                sp.wait_ge(lo_made, i * MOE_GRANULES + (g - NRAW + 1))
                sp.dma_start(raw_at(g, GRAN).rearrange("p (t n) -> p t n", t=kts),
                             src.rearrange("a (t p) n -> p (a t) n", p=P)).then_inc(raw_in[g % NRAW], 16)

            def load_expert(i):
                e = i % N_EXPERTS
                for c in range(MOE_CHUNKS + 1):
                    k = moe_first(c)
                    if c < MOE_CHUNKS:
                        for m, w in enumerate((eg, eu)):
                            for half in range(2):
                                load(i, k, w[bass.ds(e, 1), half * 512:(half + 1) * 512, c * 512:(c + 1) * 512], 4)
                                k += 1
                    if c >= 1:
                        for half in range(2):
                            r0 = (c - 1) * 512 + half * 256
                            load(i, k, ed[bass.ds(e, 1), r0:r0 + 256, :], 2)
                            k += 1

            with sp.Fori(0, N_EXPERTS) as i:
                load_expert(i)
            sp.wait_ge(items_made, 1)
            items = sp.value_load(n_items[0:1, 0:1], min_val=N_EXPERTS, max_val=2 * N_EXPERTS)
            with sp.If(items - N_EXPERTS):
                with sp.Fori(N_EXPERTS, 2 * N_EXPERTS) as i:
                    load_expert(i)
            for k, (w, half) in enumerate(((eg, 0), (eg, 1), (eu, 0))[:AHEAD]):
                load(items, k, w[0:1, half * 512:(half + 1) * 512, 0:512], 4)
            for b in range(NB):
                sp.wait_ge(x_upd, items * 4 + (at_x["moe"] + 2 * (b + 1)))
                sp.dma_start(out[0, b * P:(b + 1) * P, :], x[:, b, :]).then_inc(out_done, 16)
            sp.wait_ge(out_done, 16 * NB)

        @block.gpsimd
        def _(pool):
            pool.memset(pool_w[:], 0.0).then_inc(pool_zero, 1)
            own = [1]
            pool.memset(mhalf[:], -0.5).then_inc(pool_own, 1)

            def roots(mean, sums, count, width, done):
                own[0] += 1
                pool.tensor_scalar(mean, sums, 1.0 / count, EPS, ALU.mult, ALU.add).then_inc(pool_own, 1)
                pool.wait_ge(pool_own, own[0])
                pool.tensor_tensor(done, mean, mhalf[:, 0:width], ALU.pow)\
                    .then_inc(rstd_made if count == D else qroot_made, 1)

            def norm(n):
                pool.wait_ge(ss_made, 2 * (n + 1))
                roots(ms[:, n, :], ss[:, n, :], D, NB, rstd[:, n, :])

            def heads_norm(q, nh):
                pool.wait_ge(qss_made, q + 1)
                if q >= 1:
                    pool.wait_ge(qk_made, q)
                roots(qss[:, 1, 0:NB * nh], qss[:, 0, 0:NB * nh], HD, NB * nh, qss[:, 2, 0:NB * nh])

            norm(NORM1)
            heads_norm(0, REL_HEADS)
            heads_norm(1, REL_HEADS)
            for n in (NORM2, NMEM0, NMIX0):
                norm(n)
            heads_norm(2, FOX_HEADS)
            heads_norm(3, FOX_HEADS)
            heads_norm(4, MEM_HEADS)
            heads_norm(5, MEM_HEADS)
            for n in (NFFN0, NMEM1, NMIX1):
                norm(n)
            heads_norm(6, MEM_HEADS)
            heads_norm(7, MEM_HEADS)
            pool.wait_ge(moe_in, 16 * len(LOADS["moe"]))
            for h in range(2):
                pool.wait_ge(x_upd, at_x["nffn1"] - 2 + 2 * h)
                part = slice(h * 512, (h + 1) * 512)
                for b in range(NB):
                    pool.tensor_tensor(zrow[:, b, part], x[:, b, part], gain_b[:, part], ALU.mult).then_inc(z_made, 1)
            norm(NFFN1)
            pool.memset(y_sb[:, 0:512], 0.0).then_inc(y_act, 1)
            pool.memset(y_sb[:, 512:D], 0.0).then_inc(y_dve, 1)
            pool.memset(pickgT[:], 0.0).then_inc(pickg_zero, 1)

        @block.tensor
        def _(pe):
            def tstep(t, sources, base=None):
                if base is None:
                    if t >= 2:
                        if tkinds[t - 2] in "bd":
                            pe.wait_ge(t_dve, dve_steps(t - 2))
                        else:
                            pe.wait_ge(t_act, act_steps(t - 2))
                    b = bank[6 + t % 2]
                for k, src in enumerate(sources):
                    mm = pe.transpose(b[:, k * P:(k + 1) * P], src, ident[:])
                mm.then_inc(t_psum, 1)

            def parts3(outs, hi, lo, wh, wl, start, stop):
                for o, h, l in zip(outs, wh, wl):
                    pe.matmul(o, hi, h, start=start, stop=False)
                    pe.matmul(o, hi, l, start=False, stop=False)
                for o, h in zip(outs, wh):
                    mm = pe.matmul(o, lo, h, start=False, stop=stop)
                return mm

            def across(g, n, lhs, kt0, outs, first, last, middle=None):
                slot = g % NSPLIT
                for kk in range(4):
                    if kk == 1 and middle is not None:
                        middle()
                    wh = w_hi[:, slot, kk * n:(kk + 1) * n]
                    wl = w_lo[:, slot, kk * n:(kk + 1) * n]
                    for b, o in enumerate(outs):
                        mm = parts3([o], lhs(0, kt0 + kk, b), lhs(1, kt0 + kk, b), [wh], [wl],
                                    first and kk == 0, last and kk == 3)
                mm.then_inc(w_used, 1)

            def down(g, lhs, kt0, outs, first, last):
                slot = g % NSPLIT
                for kk in range(2):
                    wh = [w_hi[:, slot, kk * D + h * 512:kk * D + (h + 1) * 512] for h in range(2)]
                    wl = [w_lo[:, slot, kk * D + h * 512:kk * D + (h + 1) * 512] for h in range(2)]
                    for b, o in enumerate(outs):
                        mm = parts3(o, lhs(0, kt0 + kk, b), lhs(1, kt0 + kk, b), wh, wl,
                                    first and kk == 0, last and kk == 1)
                mm.then_inc(w_used, 1)

            def a_tile(name):
                return lambda part, kt, b: a_at((a_hi, a_lo)[part], name, kt)[:, 0, b * P:(b + 1) * P]

            def norm_t(name, half, src, made, count):
                pe.wait_ge(made, count)
                for s in (2 * half, 2 * half + 1):
                    tstep(at[name]["t"] + s, [src[:, b, kt * P:(kt + 1) * P] for kt in (2 * s, 2 * s + 1)
                                              for b in range(NB)])

            def x_t(name, half):
                norm_t(name, half, x, x_upd, at_x[name] - 2 + 2 * half)

            def norm_ready(name, half):
                pe.wait_ge(t_dve, dve_steps(at[name]["t"] + 2 * half + 1))

            def job(j, g, n, name, norm, middle):
                outs = [bank[2 * (j % 2) + b][:, 0:n] for b in range(NB)]
                for half in range(2):
                    if norm:
                        norm_ready(name, half)
                    pe.wait_ge(lo_made, g + half + 1)
                    across(g + half, n, a_tile(name), 4 * half, outs, half == 0, half == 1,
                           middle if half == 0 else None)

            def jobs(stage, widths, name, norm=False):
                for k, n in enumerate(widths):
                    j = at[stage]["j"] + k
                    if j >= 2:
                        pe.wait_ge(j_act, plain_jobs(j - 2))
                        pe.wait_ge(j_dve, plain_jobs(j - 2))
                    job(j, at[stage]["g"] + 2 * k, n, name, norm and k == 0, None)

            def out_jobs(stage, mixed, name, second_half=None):
                j, g = at[stage]["j"], at[stage]["g"]
                for k in range(2):
                    pe.wait_ge(j_act, plain_jobs(j + k - 2))
                    pe.wait_ge(j_dve, plain_jobs(j + k - 2))
                    outs = [bank[2 * ((j + k) % 2) + b][:] for b in range(NB)]
                    for half in range(2):
                        if k == 0 and half == 1 and second_half is not None:
                            second_half()
                        if k == 1 and half == 1:
                            x_t(name, 0)
                        pe.wait_ge(lo_made, g + 2 * k + half + 1)
                        across(g + 2 * k + half, 512, a_tile(mixed), 4 * half, outs, half == 0, half == 1)

            def mem_half(g, half, middle=None):
                pe.wait_ge(lo_made, g + 1)
                across(g, 512, lambda part, kt, b: (m_hi, m_lo)[part][:, kt, b * P:(b + 1) * P], 4 * half,
                       [bank[4][:], bank[5][:]], half == 0, half == 1, middle)

            def mem_job(stage, name):
                mem_half(at[stage]["g"], 1, lambda: x_t(name, 0))
                x_t(name, 1)

            def mem_t(t, c, loads):
                if c in MEM_CHUNKS:
                    pe.wait_ge(mem_in, 16 * loads)
                    s = c - MEM_CHUNKS[0]
                    tstep(t, [mem[:, b, kt * P:(kt + 1) * P] for kt in (2 * s, 2 * s + 1) for b in range(NB)])
                    return t + 1
                return t

            def cols_t(t, src, cols):
                tstep(t, [src[:, b, c:c + P] for c in cols for b in range(NB)])

            def heads(first, todo, between=None):
                for i in range(len(todo) + 2):
                    if i < len(todo):
                        h = first + i
                        kind, qt, kt_, r = todo[i][:4]
                        if i >= 2:
                            pe.wait_ge(s_exp, NB * (h - 1))
                        for b in range(NB):
                            o = bank[i % 2][:, b * S:b * S + keys(kind, b)]
                            mm = pe.matmul(o, qT[r:r + HD, qt, b * P:(b + 1) * P], kT[r:r + HD, kt_, 0:keys(kind, b)],
                                           start=True, stop=kind is None)
                            if kind is not None:
                                mm = pe.matmul(o[:, b * P:(b + 1) * P], ident_r[:], mask_r[:, kind, b, b * P:(b + 1) * P],
                                               start=False, stop=True)
                        mm.then_inc(s_psum, 1)
                    if 1 <= i <= len(todo):
                        h = first + i - 1
                        kind = todo[i - 1][0]
                        if i - 1 >= 2:
                            pe.wait_ge(p_sb, h - 1)
                        for b in range(NB):
                            pe.wait_ge(s_exp, NB * h + b + 1)
                            for kt in range(keys(kind, b) // P):
                                at_col = pt_at(kind, b, kt)
                                mm = pe.transpose(bank[2 + (i - 1) % 2][:, at_col:at_col + P],
                                                  pr[:, (i - 1) % 2, b, kt * P:(kt + 1) * P], ident[:])
                        mm.then_inc(p_psum, 1)
                    if i >= 2:
                        h = first + i - 2
                        kind, v, vc = todo[i - 2][0], *todo[i - 2][4:6]
                        pe.wait_ge(p_sb, h + 1)
                        if i - 2 >= 2:
                            pe.wait_ge(o_sb, 2 * (h - 1))
                        for b in range(NB):
                            tiles = keys(kind, b) // P
                            for kt in range(tiles):
                                at_col = pt_at(kind, b, kt)
                                mm = pe.matmul(bank[4 + (i - 2) % 2][:, b * HD:(b + 1) * HD],
                                               pT[:, (i - 2) % 2, at_col:at_col + P],
                                               v[:, kt, vc:vc + HD], start=kt == 0, stop=kt == tiles - 1)
                        mm.then_inc(o_psum, 1)
                    if between is not None:
                        between(i)

            pe.wait_ge(start_in, 32)
            for half in range(2):
                norm_t("norm1", half, x, x_in[half], 16)
            jobs("in0", [512] * 5, "norm1", norm=True)
            t = at["conv0"]["t"]
            pe.wait_ge(j_act, plain_jobs(at["in0"]["j"] + 4))
            pe.wait_ge(j_dve, plain_jobs(at["in0"]["j"] + 4))
            for k in range(4):
                cols_t(t + k, proj0, [1536 + 256 * k, 1536 + 256 * k + P])
            pe.wait_ge(qk_made, 2)
            t = at["qk0"]["t"]
            for k in range(4):
                cols_t(t + k, proj0, [256 * k, 256 * k + P])
            pe.wait_ge(t_act, act_steps(t + 3))
            pe.wait_ge(mask_made, 2)
            heads(at["heads0"]["h"], HEADS0)
            pe.wait_ge(m_made, 1)
            pe.wait_ge(s_exp, NB * (at["heads0"]["h"] + REL_HEADS))
            for k in range(2):
                mm = pe.matmul(bank[0][:, k * S:(k + 1) * S], pool_w[:, k, :], mT[:, k, :], start=True, stop=True)
            mm.then_inc(pool_psum, 1)
            pe.wait_ge(o_sb, 2 * (at["heads0"]["h"] + REL_HEADS))
            for k in range(2):
                cols_t(at["mix0"]["t"] + k, mix, [256 * k, 256 * k + P])
            pe.wait_ge(t_dve, dve_steps(at["mix0"]["t"] + 1))
            pe.wait_ge(cp_lo, 2)
            out_jobs("out0", "mix0", "norm2")

            def f_tile(buf):
                return lambda p, kt, b: (f_hi, f_lo)[p][:, buf, kt, b * P:(b + 1) * P]

            accs = [[bank[2 * b + h][:] for h in range(2)] for b in range(NB)]

            g, t = at["ff0"]["g"], at["ff0"]["t"]
            norm_ready("norm2", 0)
            for c in range(FF0_CHUNKS + 1):
                ups = [bank[4 + b][:] for b in range(NB)]
                if c < FF0_CHUNKS:
                    if c >= 1:
                        pe.wait_ge(f_made, 2 * c)
                    pe.wait_ge(lo_made, g + 1)
                    across(g, 512, a_tile("norm2"), 0, ups, True, False, (lambda: x_t("norm2", 1)) if c == 0 else None)
                    g += 1
                if c >= 1:
                    pe.wait_ge(f_made, 2 * c)
                    for k in range(2):
                        tstep(t, [f_sb[:, (c - 1) % 2, b, kt * P:(kt + 1) * P] for kt in (2 * k, 2 * k + 1)
                                  for b in range(NB)])
                        t += 1
                if c == FF0_CHUNKS:
                    mem_half(g, 0)
                    g += 1
                if c < FF0_CHUNKS:
                    pe.wait_ge(lo_made, g + 1)
                    if c == 0:
                        norm_ready("norm2", 1)
                    across(g, 512, a_tile("norm2"), 4, ups, False, True)
                    g += 1
                ready = dve_steps(t - 1)
                t = mem_t(t, c, 1)
                if c >= 1:
                    pe.wait_ge(t_dve, ready)
                    if c == 1:
                        pe.wait_ge(x_upd, at_x["ff0"])
                    for k in range(2):
                        pe.wait_ge(lo_made, g + 1)
                        down(g, f_tile((c - 1) % 2), 2 * k, accs, c == 1 and k == 0, c == FF0_CHUNKS and k == 1)
                        g += 1

            mem_job("mem0", "nmix0")
            jobs("in1", [n for _, n in FOX_JOBS], "nmix0", norm=True)
            pe.wait_ge(kv_act, 1)
            pe.wait_ge(kv_dve, 1)
            pe.wait_ge(lf_made, 1)
            for b in range(NB):
                for s in range(b + 1):
                    mm = pe.matmul(bank[4][:, b * FOX_HEADS:(b + 1) * FOX_HEADS],
                                   negtri[:, s, b * P:(b + 1) * P], lf[:, 3, s, :], start=s == 0, stop=s == b)
            mm.then_inc(c_psum, 1)
            pe.wait_ge(lf_lo_made, 1)
            for k in range(FOX_HEADS // 2):
                bk = bank[4 + (k + 1) % 2]
                if k >= 2:
                    pe.wait_ge(dec_sb, k - 1)
                if k == 1:
                    pe.wait_ge(c_sb, 1)
                for hh in range(2):
                    for s in range(NB):
                        for part in (lf_hi, lf_lo):
                            mm = pe.matmul(bk[:, hh * S:(hh + 1) * S], bcast(part[:, s, 2 * k + hh], P), negtri_r[:, s, :],
                                           start=s == 0 and part is lf_hi, stop=s == 1 and part is lf_lo)
                mm.then_inc(dec_psum, 1)
            t = at["qk1"]["t"]
            pe.wait_ge(qk_made, 4)
            for k in range(6):
                cols_t(t + k, proj1, [256 * k, 256 * k + P])
            pe.wait_ge(t_act, act_steps(t + 5))
            pe.wait_ge(dec_sb, FOX_HEADS // 2)

            def beside_heads1(i):
                if i == 3:
                    pe.wait_ge(qk_made, 6)
                    cols_t(at["qk1"]["t"] + 6, proj1, [MQ1, MQ1 + P])
                    cols_t(at["qk1"]["t"] + 7, kvm1, [0, P])
                if i == 7:
                    pe.wait_ge(t_act, act_steps(at["qk1"]["t"] + 7))

            heads(at["heads1"]["h"], HEADS1, beside_heads1)
            pe.wait_ge(o_sb, 2 * (at["heads1"]["h"] + len(HEADS1)))
            for k in range(4):
                cols_t(at["mix1"]["t"] + k, mix, [256 * k, 256 * k + P])
            pe.wait_ge(t_dve, dve_steps(at["mix1"]["t"] + 3))
            out_jobs("out1", "mix1", "nffn0")

            g, t = at["ff1"]["g"], at["ff1"]["t"]
            norm_ready("nffn0", 0)
            for c in range(FF1_CHUNKS + 1):
                ups = [bank[4 + b][:] for b in range(NB)]
                if c < FF1_CHUNKS:
                    if c >= 1:
                        pe.wait_ge(h_made, 2 * c)
                    pe.wait_ge(lo_made, g + 1)
                    across(g, 512, a_tile("nffn0"), 0, ups, True, False, (lambda: x_t("nffn0", 1)) if c == 0 else None)
                    g += 1
                t = mem_t(t, c, 2)
                if c >= 1:
                    pe.wait_ge(h_made, 2 * c)
                    tstep(t, [f_sb[:, (c - 1) % 2, b, kt * P:(kt + 1) * P] for kt in range(2) for b in range(NB)])
                    t += 1
                if c == FF1_CHUNKS:
                    mem_half(g, 0)
                    g += 1
                if c < FF1_CHUNKS:
                    pe.wait_ge(lo_made, g + 1)
                    if c == 0:
                        norm_ready("nffn0", 1)
                    across(g, 512, a_tile("nffn0"), 4, ups, False, True)
                    g += 1
                if c >= 1:
                    pe.wait_ge(t_dve, dve_steps(t - 1))
                    if c == 1:
                        pe.wait_ge(x_upd, at_x["ff1"])
                    pe.wait_ge(lo_made, g + 1)
                    down(g, f_tile((c - 1) % 2), 0, accs, c == 1, c == FF1_CHUNKS)
                    g += 1

            mem_job("mem1", "nmix1")
            jobs("in2", [n for _, n in CONV_JOBS], "nmix1", norm=True)
            t = at["glu"]["t"]
            pe.wait_ge(j_act, plain_jobs(at["in2"]["j"] + 3))
            pe.wait_ge(j_dve, plain_jobs(at["in2"]["j"] + 3))
            for k in range(3):
                cols_t(t + 2 * k, proj2, [768 + 256 * k, 768 + 256 * k + P])
                cols_t(t + 2 * k + 1, proj2, [256 * k, 256 * k + P])
            pe.wait_ge(qk_made, 8)
            t = at["qk2"]["t"]
            cols_t(t, proj2, [MQ2, MQ2 + P])
            cols_t(t + 1, kvm2, [0, P])
            pe.wait_ge(t_act, act_steps(t + 1))

            def taps(k):
                if k >= 2:
                    pe.wait_ge(dw_acc, k - 1)
                for i in range(PE_TAPS):
                    pe.wait_ge(diag_made, k * PE_TAPS + i + 1)
                    mm = pe.matmul(bank[6 + k % 2][:, 0:S], diag[:, (k * PE_TAPS + i) % N_DIAG, :], glu[:, k, i:i + S],
                                   start=i == 0, stop=i == PE_TAPS - 1)
                    mm.then_inc(tap_used, 1)
                means = {4: (0, 1, 2), 5: (3,)}.get(k, ())
                for done in means:
                    channel_mean(done)

            def channel_mean(k):
                return pe.matmul(bank[0][:, 0:S], onesm[:], dwy[:, k, :], start=k == 0, stop=k == CONV_TILES - 1)

            pe.wait_ge(t_dve, dve_steps(at["glu"]["t"] + 5))
            heads(at["heads2"]["h"], HEADS2, taps)
            pe.wait_ge(dw_acc, CONV_TILES)
            pe.wait_ge(o_sb, 2 * (at["heads2"]["h"] + len(HEADS2)))
            for k in range(4, CONV_TILES):
                mm = channel_mean(k)
            mm.then_inc(mu_psum, 1)
            cols_t(at["mix2"]["t"], mix, [768, 768 + P])
            for k in range(CONV_TILES):
                pe.wait_ge(sqc_made, k + 1)
                mm = pe.matmul(bank[1][:, 0:S], onesm[:], dwq[:, k, :], start=k == 0, stop=k == CONV_TILES - 1)
            mm.then_inc(var_psum, 1)

            def mix2_ready():
                pe.wait_ge(ln_lo, 3)
                pe.wait_ge(t_dve, dve_steps(at["mix2"]["t"]))

            pe.wait_ge(ln_lo, 2)
            out_jobs("out2", "mix2", "nffn1", mix2_ready)

            pe.wait_ge(router_lo_made, 1)
            for half in range(2):
                if half == 1:
                    x_t("nffn1", 1)
                norm_ready("nffn1", half)
                for kt in range(4 * half, 4 * half + 4):
                    hi, lo = (a_at(part, "nffn1", kt)[:, 0, :] for part in (a_hi, a_lo))
                    for n, (w, tile) in enumerate(((router_hi, hi), (router_lo, hi), (router_hi, lo))):
                        mm = pe.matmul(bank[4][0:N_EXPERTS, 0:S], w[:, kt, :], tile,
                                       start=kt == 0 and n == 0, stop=kt == KT - 1 and n == 2)
            mm.then_inc(r_psum, 1)
            pe.wait_ge(r_sb, 1)
            for b in range(NB):
                mm = pe.transpose(bank[5][:, b * N_EXPERTS:(b + 1) * N_EXPERTS], logit_t[:, b * P:(b + 1) * P],
                                  ident[0:N_EXPERTS, 0:N_EXPERTS])
            mm.then_inc(rt_psum, 1)
            pe.wait_ge(ch_made, 1)
            for b in range(NB):
                for s in range(b + 1):
                    pe.matmul(bank[4][:, b * N_EXPERTS:(b + 1) * N_EXPERTS],
                              negtri[:, s, b * P:(b + 1) * P], chosen[:, s, :], start=s == 0, stop=s == b)
            for s in range(NB):
                mm = pe.matmul(bank[4][:, 16:24], negtri[:, 0, P:S], chosen[:, s, :], start=s == 0, stop=s == 1)
            mm.then_inc(rk_psum, 1)

            def xg_tile(part, kt, b):
                return (xg_hi, xg_lo)[part][:, kt, :]

            pe.wait_ge(x_upd, at_x["moe"])

            def gather(k, dst):
                for kk in range(4):
                    kt = 4 * k + kk
                    for b in range(NB):
                        for part in (z_hi, z_lo):
                            mm = pe.matmul(dst[:, kk * P:(kk + 1) * P], part[:, b, kt * P:(kt + 1) * P], pick[:, b, :],
                                           start=b == 0 and part is z_hi, stop=b == NB - 1 and part is z_lo)
                mm.then_inc(t_psum, 1)

            def scatter():
                for b in range(NB):
                    for half in range(2):
                        pe.matmul(bank[2 - 2 * b + half][:], pickgT[:, b * P:(b + 1) * P],
                                  y_sb[:, half * 512:(half + 1) * 512], start=True, stop=True).then_inc(sc_psum, 1)

            pe.wait_ge(zlo_made, NB)
            pe.wait_ge(pick_made, 1)
            for k in range(2):
                pe.wait_ge(t_dve, TD + k - 1)
                gather(k, bank[6 + (TM + k) % 2])
            pe.wait_ge(items_made, 1)
            items = pe.value_load(n_items[0:1, 0:1], min_val=N_EXPERTS, max_val=2 * N_EXPERTS)
            with pe.Fori(0, items) as i:
                def t_free(k):
                    pe.wait_ge(t_dve, i * MOE_TSTEPS + (TD + 2 + k - 1))

                def w_ready(k):
                    pe.wait_ge(lo_made, i * MOE_GRANULES + (NG + k + 1))

                def chunk_t(c):
                    pe.wait_ge(h_made, i * MOE_CHUNKS + (HM + c))
                    t_free(CHUNK_STEP[c])
                    for kt in range(4):
                        mm = pe.transpose(bank[6 + (TM + CHUNK_STEP[c]) % 2][:, kt * P:(kt + 1) * P],
                                          mf_sb[:, (c - 1) % 2, 1, kt * P:(kt + 1) * P], ident[:])
                    mm.then_inc(t_psum, 1)

                pe.wait_ge(t_dve, i * MOE_TSTEPS + (TD + 2))
                for c in range(MOE_CHUNKS + 1):
                    k = moe_first(c)
                    gb, ub = (bank[4], bank[5]) if c % 2 == 0 else (bank[2], bank[3])
                    if c < MOE_CHUNKS:
                        if c == 1:
                            pe.wait_ge(x_upd, i * 4 + (at_x["moe"] + 4))
                        if c >= 2:
                            pe.wait_ge(h_made, i * MOE_CHUNKS + (HM + c - 1))
                        for half in range(2):
                            w_ready(k)
                            across(NG + k, 512, xg_tile, 4 * half, [gb[:]], half == 0, half == 1)
                            k += 1
                    if c == 0:
                        pe.wait_ge(y_act, i + 1)
                        pe.wait_ge(y_dve, i + 1)
                        scatter()
                    if c == PICKG_CHUNK:
                        pe.wait_ge(pickg_made, i + 1)
                        t_free(PICKG_STEP)
                        for b in range(NB):
                            mm = pe.transpose(bank[6 + (TM + PICKG_STEP) % 2][:, b * P:(b + 1) * P], pickg[:, b, :], ident[:])
                        mm.then_inc(t_psum, 1)
                    if 1 <= c < MOE_CHUNKS:
                        chunk_t(c)
                    if c < MOE_CHUNKS:
                        for half in range(2):
                            w_ready(k)
                            across(NG + k, 512, xg_tile, 4 * half, [ub[:]], half == 0, half == 1)
                            k += 1
                    if c == GATHER_CHUNK:
                        pe.wait_ge(pick_made, i + 2)
                        for kk in range(2):
                            t_free(GATHER_STEP + kk)
                            gather(kk, bank[6 + (TM + GATHER_STEP + kk) % 2])
                        chunk_t(c + 1)
                    if c >= 1:
                        pe.wait_ge(t_dve, i * MOE_TSTEPS + (TD + 2 + CHUNK_STEP[c] + 1))
                        for half in range(2):
                            w_ready(k)
                            down(NG + k, lambda p, kt, b: (mf_hi, mf_lo)[p][:, (c - 1) % 2, kt, :], 2 * half,
                                 [[bank[0][:], bank[1][:]]], c == 1 and half == 0, c == MOE_CHUNKS and half == 1)
                            k += 1
            pe.wait_ge(y_act, items + 1)
            pe.wait_ge(y_dve, items + 1)
            scatter()

        @block.scalar
        def _(act):
            own = [0]
            squared = [0]
            done = [0]

            def chained(ins):
                own[0] += 1
                ins.then_inc(act_own, 1)
                act.wait_ge(act_own, own[0])

            def hi(g):
                act.wait_ge(raw_in[g % NRAW], raw_count[g])
                if g >= NSPLIT:
                    act.wait_ge(w_used, g - NSPLIT + 1)
                n = n_el(g)
                act.activation(w_hi[:, g % NSPLIT, 0:n], raw_at(g, n), ACT.Copy).then_inc(hi_made, 1)

            def hi_to(g):
                while done[0] <= min(g, NG + AHEAD - 1):
                    hi(done[0])
                    done[0] += 1

            def gains(n, s):
                return [gcol[:, n, 2 * s + k:2 * s + k + 1] for k in range(2)]

            def t_hi(t, dst, scales=(1.0, 1.0)):
                act.wait_ge(t_psum, t + 1)
                src = bank[6 + t % 2]
                if scales[0] == 1.0:
                    act.activation(dst, src[:].rearrange("p (k s) -> p k s", k=2), ACT.Copy).then_inc(t_act, 1)
                else:
                    act.activation(dst[:, 0, :], src[:, 0:S], ACT.Copy, scale=scales[0])
                    act.activation(dst[:, 1, :], src[:, S:2 * S], ACT.Copy, scale=scales[1]).then_inc(t_act, 1)

            def squares(n, src, scratch):
                if n >= 1:
                    act.wait_ge(ss_made, 2 * n)
                for b in range(NB):
                    act.activation(scratch[:, b, :], src[:, b, :], ACT.Square, accum_out=ss[:, n, b:b + 1])\
                        .then_inc(ss_made, 1)

            def norm_hi(name, n, half):
                for s in (2 * half, 2 * half + 1):
                    t_hi(at[name]["t"] + s, a_at(a_hi, name, 2 * s, 2), gains(n, s))

            def mem_hi(t, c, n):
                if c in MEM_CHUNKS:
                    s = c - MEM_CHUNKS[0]
                    t_hi(t, m_hi[:, 2 * s:2 * s + 2, :], gains(n, s))
                    return t + 1
                return t

            def out_norm(stage, name, n):
                g = at[stage]["g"]
                hi_to(g + 4)
                norm_hi(name, n, 0)
                hi_to(g + 5)
                act.wait_ge(w_used, g + 3)
                norm_hi(name, n, 1)
                squares(n, x, mix)
                if g + 6 < NG:
                    hi_to(g + 6)

            def mem_out(stage, name, n, m, dst):
                g = at[stage]["g"]
                hi_to(g + 2)
                norm_hi(name, n, 0)
                norm_hi(name, n, 1)
                hi_to(g + 3)
                act.wait_ge(w_used, g + 1)
                act.wait_ge(rstd_made, m + 1)
                act.activation(dst, bank[4][:], ACT.Copy, scale=rstd[:, m, 0:1]).then_inc(kv_act, 1)
                squares(n, x, squares_ff)
                act.wait_ge(rstd_made, n + 1)

            def copy_out(j, g_end, dst, n):
                act.wait_ge(w_used, g_end + 1)
                act.activation(dst, bank[2 * (j % 2)][:, 0:dst.shape[-1]], ACT.Copy, scale=rstd[:, n, 0:1]).then_inc(j_act, 1)

            def exps(first, todo, before=None):
                for i in range(len(todo) + 1):
                    if before is not None:
                        before(i)
                    h = first + i
                    if i < len(todo):
                        if i >= 2:
                            act.wait_ge(p_psum, h - 1)
                        if i >= 4:
                            act.wait_ge(o_sb, 2 * (h - 3))
                        for b in range(NB):
                            act.wait_ge(s_max, NB * h + (NB if todo[i][0] is None else b + 1))
                            n = keys(todo[i][0], b)
                            src = bank[i % 2][:, b * S:b * S + n] if todo[i][0] is None else sc[:, i % 2, b, 0:n]
                            act.activation(pr[:, i % 2, b, 0:n], src, ACT.Exp, bias=nmax[:, i % 2, b:b + 1],
                                           accum_out=psumr[:, i % 4, b:b + 1]).then_inc(s_exp, 1)
                    if i >= 1:
                        act.wait_ge(p_psum, h)
                        if i - 1 >= 2:
                            act.wait_ge(o_psum, h - 2)
                        n = NB * S if todo[i - 1][0] is None else 3 * P
                        act.activation(pT[:, (i - 1) % 2, 0:n], bank[2 + (i - 1) % 2][:, 0:n], ACT.Copy).then_inc(p_sb, 1)

            def square_heads(src, c0, nh, at_col=0):
                if squared[0] >= 1:
                    act.wait_ge(qss_made, squared[0])
                squared[0] += 1
                act.activation(mix[:, :, at_col:at_col + nh * HD], src[:, :, c0:c0 + nh * HD], ACT.Square).then_inc(sq_made, 1)

            def t_copy(t, dst, gain=None):
                act.wait_ge(t_psum, t + 1)
                src = bank[6 + t % 2][:].rearrange("p (k s) -> p k s", k=2)
                if gain is None:
                    act.activation(dst, src, ACT.Copy).then_inc(t_act, 1)
                else:
                    act.activation(dst, src, ACT.Copy, scale=hcol[:, gain:gain + 1]).then_inc(t_act, 1)

            act.wait_ge(start_in, 32)
            for dst, src in LOADS["const"]:
                act.dma_start(dst, src).then_inc(const_in, 16)
            norm_hi("norm1", NORM1, 0)
            hi_to(0)
            norm_hi("norm1", NORM1, 1)
            hi_to(2)
            squares(NORM1, x, mix)
            act.dma_start(rel_row[:, 127:127 + 257], a["rel_bias"]).then_inc(rel_in, 16)
            for dst, src in LOADS["early"]:
                act.dma_start(dst, src).then_inc(early_in, 16)
            act.wait_ge(pool_zero, 1)
            for gr in range(4):
                r = (gr % 2) * HD
                act.dma_start(pool_w[r:r + HD, gr // 2, r:r + HD], a["pool_w"][0, gr]).then_inc(early_in, 16)
            act.wait_ge(rstd_made, 1)
            for k in range(5):
                g_end = at["in0"]["g"] + 2 * k + 1
                hi_to(g_end + 2)
                copy_out(at["in0"]["j"] + k, g_end, proj0[:, 0, 512 * k:512 * (k + 1)], NORM1)
                if k == 1:
                    act.wait_ge(rel_ext, 1)
                    act.dma_start(rel_rows_dram, rel_row[:]).then_inc(rel_out, 16)
                if k == 2:
                    act.wait_ge(rel_out, 16)
                    act.dma_start(rel_band_dram,
                                  bass.AP(rel_rows_dram.tensor, P - 1, [[REL_LEN + 1, REL_HEADS], [-1, P], [1, 384]]))\
                        .then_inc(rel_band, 16)
                if k == 3:
                    act.wait_ge(rel_band, 16)
                    act.dma_start(relT[:], rel_band_dram.rearrange("h p m -> p h m")).then_inc(rel_back, 16)
                    act.activation(ident_r[:], ident[:], ACT.Copy).then_inc(mask_made, 1)
                    act.wait_ge(const_in, 16 * len(LOADS["const"]))
                    act.activation(mask_r[:], pr[:], ACT.Copy).then_inc(mask_made, 1)
                if k == 1:
                    act.wait_ge(j_act, plain_jobs(at["in0"]["j"] + 1))
                    act.wait_ge(j_dve, plain_jobs(at["in0"]["j"] + 1))
                    square_heads(proj0, 0, REL_HEADS)
                if k == 2:
                    act.wait_ge(qss_made, 1)
                    square_heads(proj0, 512, REL_HEADS)
            t = at["conv0"]["t"]
            for k, dst in enumerate((gbT, gcT, hiT, uT[:, :, 16:16 + S])):
                t_copy(t + k, dst)
            t = at["qk0"]["t"]
            for k in range(4):
                t_copy(t + k, (qT, kT)[k // 2][:, 2 * (k % 2):2 * (k % 2) + 2, :], (GQ0, GK0)[k // 2])
            exps(at["heads0"]["h"], HEADS0)
            hi_to(at["out0"]["g"] + 2)
            act.wait_ge(w_used, at["out0"]["g"])
            act.wait_ge(y_made, 1)
            act.activation(a_at(a_hi, "mix0", 4, 2), yT[:], ACT.Copy).then_inc(cp_hi, 1)
            act.wait_ge(pool_psum, 1)
            act.activation(a_at(a_hi, "mix0", 6)[:, 0, :], bank[0][:, 0:S], ACT.Copy, scale=pscale[:, 0:1])
            act.activation(a_at(a_hi, "mix0", 7)[:, 0, :], bank[0][:, S:2 * S], ACT.Copy, scale=pscale[:, 1:2]).then_inc(cp_hi, 1)
            for k in range(2):
                t_hi(at["mix0"]["t"] + k, a_at(a_hi, "mix0", 2 * k, 2))
            g = at["ff0"]["g"]
            out_norm("out0", "norm2", NORM2)
            act.dma_start(mem[:], tokens(a["mem_2"][0])).then_inc(mem_in, 16)
            act.wait_ge(rstd_made, NORM2 + 1)
            t = at["ff0"]["t"]
            for c in range(FF0_CHUNKS + 1):
                first = g + (0 if c == 0 else 2 + 4 * (c - 1))
                if c == MEM_CHUNKS[0]:
                    act.wait_ge(mem_in, 16)
                    squares(NMEM0, mem, squares_ff)
                if c >= 1:
                    hi_to(first + (2 if c < FF0_CHUNKS else 0))
                    for k in range(2):
                        t_hi(t, f_hi[:, (c - 1) % 2, 2 * k:2 * k + 2, :])
                        t += 1
                if c < FF0_CHUNKS:
                    hi_to(first + 3)
                    t = mem_hi(t, c, NMEM0)
                    act.wait_ge(w_used, first + 2)
                    for b in range(NB):
                        f = f_sb[:, c % 2, b, :]
                        chained(act.activation(f, bank[4 + b][:], ACT.Relu, scale=rstd[:, NORM2, b:b + 1]))
                        act.activation(f, f, ACT.Square).then_inc(f_made, 1)
            mem_out("mem0", "nmix0", NMIX0, NMEM0, kvm1[:, 0, :])
            for dst, src in LOADS["l1"]:
                act.dma_start(dst, src).then_inc(l1_in, 16)
            for k, (c0, n) in enumerate(FOX_JOBS):
                g_end = at["in1"]["g"] + 2 * k + 1
                hi_to(g_end + 2)
                copy_out(at["in1"]["j"] + k, g_end, proj1[:, 0, c0:c0 + n], NMIX0)
                if k == 1:
                    act.wait_ge(lf_x, 1)
                    chained(act.activation(lf[:, 1], lf[:, 1], ACT.Exp, scale=-1.0))
                    act.activation(lf[:, 2], lf[:, 1], ACT.Ln, bias=1.0).then_inc(lf_ln, 1)
                if k == 2:
                    act.wait_ge(j_act, plain_jobs(at["in1"]["j"] + 2))
                    act.wait_ge(j_dve, plain_jobs(at["in1"]["j"] + 2))
                    square_heads(proj1, 0, FOX_HEADS)
                if k == 3:
                    act.activation(negtri_r[:], negtri[:], ACT.Copy)
                    act.wait_ge(lf_made, 1)
                    act.activation(lf_hi[:], lf[:, 3], ACT.Copy).then_inc(lf_hi_made, 1)
                if k == 4:
                    act.wait_ge(j_act, plain_jobs(at["in1"]["j"] + 4))
                    act.wait_ge(j_dve, plain_jobs(at["in1"]["j"] + 4))
                    square_heads(proj1, FOXW, FOX_HEADS)
                if k == 6:
                    act.wait_ge(kv_act, 1)
                    act.wait_ge(kv_dve, 1)
                    square_heads(kvm1, 0, MEM_HEADS)
            for k in range(FOX_HEADS // 2):
                act.wait_ge(dec_psum, k + 1)
                act.activation(decay[:, 2 * k:2 * k + 2, :], bank[4 + (k + 1) % 2][:].rearrange("p (k s) -> p k s", k=2),
                               ACT.Copy).then_inc(dec_sb, 1)
            act.wait_ge(j_act, plain_jobs(at["in1"]["j"] + 7))
            act.wait_ge(j_dve, plain_jobs(at["in1"]["j"] + 7))
            square_heads(proj1, MQ1, MEM_HEADS, FOXW)
            t = at["qk1"]["t"]
            for k in range(6):
                t_copy(t + k, (qT, kT)[k // 3][:, 2 * (k % 3):2 * (k % 3) + 2, :], (GFQ, GFK)[k // 3])

            def beside_heads1(i):
                if i == 5:
                    t_copy(at["qk1"]["t"] + 6, memq[:], GMQ0)
                    t_copy(at["qk1"]["t"] + 7, memk[:], GMK0)

            exps(at["heads1"]["h"], HEADS1, beside_heads1)
            hi_to(at["out1"]["g"] + 2)
            act.wait_ge(w_used, at["out1"]["g"])
            for k in range(4):
                t_hi(at["mix1"]["t"] + k, a_at(a_hi, "mix1", 2 * k, 2))
            g = at["ff1"]["g"]
            out_norm("out1", "nffn0", NFFN0)
            act.dma_start(mem[:], tokens(a["mem_2"][0])).then_inc(mem_in, 16)
            act.wait_ge(rstd_made, NFFN0 + 1)
            t = at["ff1"]["t"]
            for c in range(FF1_CHUNKS + 1):
                first = g + (0 if c == 0 else 2 + 3 * (c - 1))
                if c == MEM_CHUNKS[0]:
                    act.wait_ge(mem_in, 32)
                    squares(NMEM1, mem, squares_ff)
                if c >= 1:
                    hi_to(first + (2 if c < FF1_CHUNKS else 0))
                    t = mem_hi(t, c, NMEM1)
                    t_hi(t, f_hi[:, (c - 1) % 2, 0:2, :])
                    t += 1
                if c < FF1_CHUNKS:
                    hi_to(first + 3)
                    act.wait_ge(w_used, first + 2)
                    for b in range(NB):
                        act.activation(f_sb[:, c % 2, b, 256:512], bank[4 + b][:, 0:256], ACT.Silu,
                                       scale=rstd[:, NFFN0, b:b + 1]).then_inc(silu_made, 1)
            mem_out("mem1", "nmix1", NMIX1, NMEM1, kvm2[:, 0, :])
            for dst, src in LOADS["l2"]:
                act.dma_start(dst, src).then_inc(l2_in, 16)
            for k, (c0, n) in enumerate(CONV_JOBS):
                g_end = at["in2"]["g"] + 2 * k + 1
                hi_to(g_end + 2)
                copy_out(at["in2"]["j"] + k, g_end, proj2[:, 0, c0:c0 + n], NMIX1)
                if k == 1:
                    act.wait_ge(kv_act, 2)
                    act.wait_ge(kv_dve, 2)
                    square_heads(kvm2, 0, MEM_HEADS)
            act.wait_ge(j_act, plain_jobs(at["in2"]["j"] + 3))
            act.wait_ge(j_dve, plain_jobs(at["in2"]["j"] + 3))
            square_heads(proj2, MQ2, MEM_HEADS)
            t = at["glu"]["t"]
            act.wait_ge(l2_in, 16 * len(LOADS["l2"]))
            for k in range(3):
                act.wait_ge(t_psum, t + 2 * k + 1)
                if k >= 1:
                    act.wait_ge(t_dve, dve_steps(t + 2 * k - 1))
                for m in range(2):
                    ch = CONV_TILES + 2 * k + m
                    ins = act.activation(sig[:, m, :], bank[6 + (t + 2 * k) % 2][:, m * S:(m + 1) * S], ACT.Sigmoid,
                                         bias=cb_in[:, ch:ch + 1])
                ins.then_inc(t_act, 1)
            t = at["qk2"]["t"]
            t_copy(t, memq[:], GMQ1)
            t_copy(t + 1, memk[:], GMK1)

            def diagonals(k):
                for i in range(PE_TAPS):
                    n = k * PE_TAPS + i
                    if n >= N_DIAG:
                        act.wait_ge(tap_used, n - N_DIAG + 1)
                    act.activation(diag[:, n % N_DIAG, :], ident[:], ACT.Copy, scale=dw[:, k, i:i + 1]).then_inc(diag_made, 1)

            exps(at["heads2"]["h"], HEADS2, diagonals)
            hi_to(at["out2"]["g"] + 2)
            diagonals(CONV_TILES - 1)
            act.wait_ge(w_used, at["out2"]["g"])
            for k in range(CONV_TILES):
                act.wait_ge(cent_made, k + 1)
                act.activation(dwq[:, k, :], dwy[:, k, :], ACT.Square).then_inc(sqc_made, 1)
            t_hi(at["mix2"]["t"], a_at(a_hi, "mix2", 6, 2))
            act.wait_ge(var_psum, 1)
            act.activation(stat[:, 1, :], bank[1][:, 0:S], ACT.Sqrt, bias=eps[:]).then_inc(sd_made, 1)
            for k in range(CONV_TILES):
                act.wait_ge(ln_made, k + 1)
                act.activation(dwq[:, k, :], dwy[:, k, :], ACT.Silu, scale=lng[:, k:k + 1], bias=lnb[:, k:k + 1])\
                    .then_inc(silu2, 1)
                if k % 2 == 1:
                    act.wait_ge(silu2, k + 1)
                    act.activation(a_at(a_hi, "mix2", k - 1, 2), dwq[:, k - 1:k + 1, :], ACT.Copy).then_inc(ln_hi, 1)
            act.wait_ge(w_used, at["out2"]["g"] + 1)
            for dst, src in LOADS["moe"]:
                act.dma_start(dst, src).then_inc(moe_in, 16)
            act.wait_ge(moe_in, 16 * len(LOADS["moe"]))
            act.activation(router_hi[:], router[:], ACT.Copy).then_inc(router_hi_made, 1)
            out_norm("out2", "nffn1", NFFN1)
            act.wait_ge(rstd_made, NFFN1 + 1)
            act.wait_ge(z_made, 2 * NB)
            for b in range(NB):
                act.activation(z_hi[:, b, :], zrow[:, b, :], ACT.Copy, scale=rstd[:, NFFN1, b:b + 1]).then_inc(zhi_made, 1)
            hi_to(NG + 2)
            act.wait_ge(gap_made, 1)
            act.activation(gate[:, 1, :], gate[:, 0, :], ACT.Exp).then_inc(g_exp, 1)

            def xg_hi_out(k, src):
                act.activation(xg_hi[:, 4 * k:4 * k + 4, :], src[:].rearrange("p (k s) -> p k s", k=4), ACT.Copy)\
                    .then_inc(t_act, 1)

            def y_out():
                act.activation(y_sb[:, 0:512], bank[0][:], ACT.Copy).then_inc(y_act, 1)

            for k in range(2):
                act.wait_ge(t_psum, TM + k + 1)
                xg_hi_out(k, bank[6 + (TM + k) % 2])
            act.wait_ge(items_made, 1)
            items = act.value_load(n_items[0:1, 0:1], min_val=N_EXPERTS, max_val=2 * N_EXPERTS)
            with act.Fori(0, items) as i:
                def e_hi(k):
                    g = NG + k
                    act.wait_ge(raw_in[g % NRAW], i * (16 * (MOE_GRANULES // NRAW)) + (seen[g % NRAW] + 16 * (1 + (k // NRAW))))
                    act.wait_ge(w_used, i * MOE_GRANULES + (g - NSPLIT + 1))
                    act.activation(w_hi[:, g % NSPLIT, :], raw_at(g, GRAN), ACT.Copy).then_inc(hi_made, 1)

                def step_in(k):
                    act.wait_ge(t_psum, i * MOE_TSTEPS + (TM + 2 + k + 1))

                def chunk_hi(c):
                    step_in(CHUNK_STEP[c])
                    act.activation(mf_hi[:, (c - 1) % 2, :, :],
                                   bank[6 + (TM + CHUNK_STEP[c]) % 2][:].rearrange("p (k s) -> p k s", k=4), ACT.Copy)\
                        .then_inc(t_act, 1)

                k = AHEAD
                for c in range(MOE_CHUNKS + 1):
                    while k <= min(moe_first(c) + (3 if c < MOE_CHUNKS else 1), MOE_GRANULES - 1):
                        e_hi(k)
                        k += 1
                    if c == PICKG_CHUNK:
                        step_in(PICKG_STEP)
                        act.activation(pickgT[:, 0:P], bank[6 + (TM + PICKG_STEP) % 2][:, 0:P], ACT.Copy).then_inc(t_act, 1)
                    if 1 <= c < MOE_CHUNKS:
                        chunk_hi(c)
                    if c < MOE_CHUNKS:
                        act.wait_ge(w_used, i * MOE_GRANULES + (NG + moe_first(c) + 2))
                        gb = bank[4] if c % 2 == 0 else bank[2]
                        act.activation(mf_sb[:, c % 2, 0, :], gb[:], ACT.Silu).then_inc(silu_made, 1)
                    if c == GATHER_CHUNK:
                        while k <= moe_first(c) + 5:
                            e_hi(k)
                            k += 1
                        for kk in range(2):
                            step_in(GATHER_STEP + kk)
                            xg_hi_out(kk, bank[6 + (TM + GATHER_STEP + kk) % 2])
                        chunk_hi(c + 1)
                for k in range(AHEAD):
                    if k == AHEAD - 1:
                        act.wait_ge(w_used, i * MOE_GRANULES + (NG + MOE_GRANULES))
                        y_out()
                    e_hi(MOE_GRANULES + k)

        @block.vector
        def _(dve):
            own = [0]
            done = [0]

            def chained(ins):
                own[0] += 1
                ins.then_inc(dve_own, 1)
                dve.wait_ge(dve_own, own[0])

            def lo(g):
                dve.wait_ge(hi_made, g + 1)
                n = n_el(g)
                dve.tensor_tensor(w_lo[:, g % NSPLIT, 0:n], raw_at(g, n), w_hi[:, g % NSPLIT, 0:n].bitcast(F32),
                                  ALU.subtract).then_inc(lo_made, 1)

            def lo_to(g):
                while done[0] <= min(g, NG + AHEAD - 1):
                    lo(done[0])
                    done[0] += 1

            def t_lo(t, dst, hi_part, scales=(1.0, 1.0)):
                dve.wait_ge(t_act, act_steps(t))
                src = bank[6 + t % 2]
                if scales[0] == 1.0:
                    dve.tensor_tensor(dst, src[:].rearrange("p (k s) -> p k s", k=2), hi_part.bitcast(F32),
                                      ALU.subtract).then_inc(t_dve, 1)
                else:
                    for k in range(2):
                        ins = dve.scalar_tensor_tensor(dst[:, k, :], src[:, k * S:(k + 1) * S], scales[k],
                                                       hi_part[:, k, :].bitcast(F32), ALU.mult, ALU.subtract)
                    ins.then_inc(t_dve, 1)

            def gains(n, s):
                return [gcol[:, n, 2 * s + k:2 * s + k + 1] for k in range(2)]

            def norm_lo(name, n, half):
                for s in (2 * half, 2 * half + 1):
                    t_lo(at[name]["t"] + s, a_at(a_lo, name, 2 * s, 2), a_at(a_hi, name, 2 * s, 2), gains(n, s))

            def mem_lo(t, c, n):
                if c in MEM_CHUNKS:
                    s = c - MEM_CHUNKS[0]
                    t_lo(t, m_lo[:, 2 * s:2 * s + 2, :], m_hi[:, 2 * s:2 * s + 2, :], gains(n, s))
                    return t + 1
                return t

            def copy_out(j, g_end, dst, n):
                dve.wait_ge(w_used, g_end + 1)
                dve.tensor_scalar(dst, bank[2 * (j % 2) + 1][:, 0:dst.shape[-1]], rstd[:, n, 1:2], None, ALU.mult)\
                    .then_inc(j_dve, 1)

            def add_out(stage, name, n):
                for k in range(2):
                    j, g_end = at[stage]["j"] + k, at[stage]["g"] + 2 * k + 1
                    lo_to(g_end + (3, 2)[k])
                    dve.wait_ge(w_used, g_end + 1)
                    for b in range(NB):
                        xs = x[:, b, k * 512:(k + 1) * 512]
                        dve.tensor_tensor(xs, xs, bank[2 * (j % 2) + b][:], ALU.add).then_inc(x_upd, 1)
                    norm_lo(name, n, k)
                dve.wait_ge(rstd_made, n + 1)

            def add_acc(stage, name, n, m, dst):
                g = at[stage]["g"]
                lo_to(g + 1)
                dve.wait_ge(w_used, g)
                for h in range(2):
                    for b in range(NB):
                        xs = x[:, b, h * 512:(h + 1) * 512]
                        dve.tensor_tensor(xs, xs, bank[2 * b + h][:], ALU.add).then_inc(x_upd, 1)
                norm_lo(name, n, 0)
                norm_lo(name, n, 1)
                lo_to(g + 2)
                dve.wait_ge(w_used, g + 1)
                dve.wait_ge(rstd_made, m + 1)
                dve.tensor_scalar(dst, bank[5][:], rstd[:, m, 1:2], None, ALU.mult).then_inc(kv_dve, 1)
                lo_to(g + 3)
                dve.wait_ge(rstd_made, n + 1)

            def sum_heads(q, nh, at_col=0):
                dve.wait_ge(sq_made, q + 1)
                for b in range(NB):
                    ins = dve.tensor_reduce(qss[:, 0, b * nh:(b + 1) * nh],
                                            mix[:, b, at_col:at_col + nh * HD].rearrange("p (h d) -> p h d", d=HD), AX_X, ALU.add)
                ins.then_inc(qss_made, 1)

            def scale_heads(q, src, c0, nh):
                dve.wait_ge(qroot_made, q + 1)
                for b in range(NB):
                    v = src[:, b, c0:c0 + nh * HD].rearrange("p (h d) -> p h d", d=HD)
                    ins = dve.tensor_tensor(v, v, bcast(qss[:, 2, b * nh:(b + 1) * nh], HD), ALU.mult)
                ins.then_inc(qk_made, 1)

            def softmax_sides(first, todo, mixcol, between=None):
                for i in range(len(todo) + 2):
                    if i < len(todo):
                        h = first + i
                        kind, hh = todo[i][0], todo[i][6]
                        dve.wait_ge(s_psum, h + 1)
                        if i >= 2:
                            dve.wait_ge(s_exp, NB * (h - 1))
                        src = bank[i % 2][:].rearrange("p (b s) -> p b s", b=NB)
                        if kind == 0:
                            for b in range(NB):
                                c0, n = P * (1 - b), keys(kind, b)
                                dve.tensor_tensor(sc[:, i % 2, b, 0:n], src[:, b, 0:n], relT[:, hh, c0:c0 + n], ALU.add)\
                                    .then_inc(s_sb, 1)
                            src = sc[:, i % 2, :, :]
                        elif kind == 1:
                            for b in range(NB):
                                n = keys(kind, b)
                                dve.scalar_tensor_tensor(sc[:, i % 2, b, 0:n], src[:, b, 0:n], negc[:, b, hh:hh + 1],
                                                         decay[:, hh, 0:n], ALU.subtract, ALU.add).then_inc(s_sb, 1)
                            src = sc[:, i % 2, :, :]
                        if kind is None:
                            dve.tensor_reduce(nmax[:, i % 2, :], src, AX_X, ALU.max, negate=True).then_inc(s_max, NB)
                        else:
                            for b in range(NB):
                                dve.wait_ge(s_sb, NB * h + b + 1)
                                dve.tensor_reduce(nmax[:, i % 2, b:b + 1], src[:, b, 0:keys(kind, b)], AX_X, ALU.max,
                                                  negate=True).then_inc(s_max, 1)
                    if i >= 2:
                        h, k = first + i - 2, (i - 2) % 2
                        dve.wait_ge(s_exp, NB * (h + 1))
                        chained(dve.reciprocal(rinv[:, (i - 2) % 4, :], psumr[:, (i - 2) % 4, :]))
                        dve.wait_ge(o_psum, h + 1)
                        for b in range(NB):
                            c0 = mixcol + (i - 2) * HD
                            dve.tensor_scalar(mix[:, b, c0:c0 + HD], bank[4 + k][:, b * HD:(b + 1) * HD],
                                              rinv[:, (i - 2) % 4, b:b + 1], None, ALU.mult).then_inc(o_sb, 1)
                    if between is not None:
                        between(i)

            chained(dve.memset(eps[:], EPS))
            dve.memset(zT[:], 0.0)
            chained(dve.memset(uT[:], 0.0))
            norm_lo("norm1", NORM1, 0)
            lo_to(0)
            norm_lo("norm1", NORM1, 1)
            lo_to(2)
            dve.wait_ge(rstd_made, 1)
            for k in range(5):
                g_end = at["in0"]["g"] + 2 * k + 1
                lo_to(g_end + 2)
                copy_out(at["in0"]["j"] + k, g_end, proj0[:, 1, 512 * k:512 * (k + 1)], NORM1)
                if k == 0:
                    dve.wait_ge(const_in, 16 * len(LOADS["const"]))
                    for i in (GQ0, GFQ, GMQ0, GMQ1):
                        ins = dve.tensor_scalar(hcol[:, i:i + 1], hcol[:, i:i + 1], HD ** -0.5, None, ALU.mult)
                    chained(ins)
                    dve.wait_ge(rel_in, 16)
                    dve.tensor_copy(rel_row[:, 0:127], bcast(rel_row[:, 127], 127))
                    dve.tensor_copy(rel_row[:, 384:], bcast(rel_row[:, 383], REL_LEN + 1 - 384)).then_inc(rel_ext, 1)
                if k == 1:
                    sum_heads(0, REL_HEADS)
                if k == 2:
                    scale_heads(0, proj0, 0, REL_HEADS)
                    sum_heads(1, REL_HEADS)
                if k == 3:
                    scale_heads(1, proj0, 512, REL_HEADS)
            dve.wait_ge(rel_back, 16)
            t = at["conv0"]["t"]
            dve.wait_ge(early_in, 16 * (len(LOADS["early"]) + 4))
            dve.wait_ge(t_act, act_steps(t + 3))

            def conv_tap(i):
                if i == 0:
                    chained(dve.tensor_tensor(zT[:, :, CONV_K - 1:], gcT, hiT, ALU.mult))
                for k in range(2):
                    z = zT[:, k, i:i + S]
                    if i == 0:
                        ins = dve.tensor_scalar(yT[:, k, :], z, cw[:, k, 0:1], None, ALU.mult)
                    else:
                        ins = dve.scalar_tensor_tensor(yT[:, k, :], z, cw[:, k, i:i + 1], yT[:, k, :], ALU.mult, ALU.add)
                chained(ins)
                if i == CONV_K - 1:
                    dve.tensor_tensor(yT[:], yT[:], gbT, ALU.mult).then_inc(y_made, 1)

            def pool_window(n):
                w = POOL_WINDOWS[n]
                cur = win[:, n % 2]
                before = uT[:] if n == 0 else win[:, (n - 1) % 2]
                lo_i = w - 1
                chained(dve.tensor_tensor(cur[:, :, lo_i:], before[:, :, lo_i:], before[:, :, lo_i - w // 2:S + 16 - w // 2],
                                          ALU.add))
                k, r = n // 2, (n % 2) * HD
                chained(dve.tensor_tensor(mT[r:r + HD, k, :], cur[r:r + HD, k, 16:], invcnt[r:r + HD, k, :], ALU.mult))
                if n == len(POOL_WINDOWS) - 1:
                    dve.tensor_tensor(mT, mT, uT[:, :, 16:], ALU.subtract).then_inc(m_made, 1)

            def beside_heads0(i):
                if i < CONV_K:
                    conv_tap(i)
                elif i < CONV_K + len(POOL_WINDOWS):
                    pool_window(i - CONV_K)

            softmax_sides(at["heads0"]["h"], HEADS0, 0, beside_heads0)
            lo_to(at["out0"]["g"] + 2)
            dve.wait_ge(cp_hi, 1)
            dve.tensor_tensor(a_at(a_lo, "mix0", 4, 2), yT[:], a_at(a_hi, "mix0", 4, 2).bitcast(F32), ALU.subtract).then_inc(cp_lo, 1)
            dve.wait_ge(cp_hi, 2)
            for k in range(2):
                ins = dve.scalar_tensor_tensor(a_at(a_lo, "mix0", 6 + k)[:, 0, :], bank[0][:, k * S:(k + 1) * S], pscale[:, k:k + 1],
                                               a_at(a_hi, "mix0", 6 + k)[:, 0, :].bitcast(F32), ALU.mult, ALU.subtract)
            ins.then_inc(cp_lo, 1)
            for k in range(2):
                t_lo(at["mix0"]["t"] + k, a_at(a_lo, "mix0", 2 * k, 2), a_at(a_hi, "mix0", 2 * k, 2))
            add_out("out0", "norm2", NORM2)
            g = at["ff0"]["g"]
            t = at["ff0"]["t"]
            for c in range(FF0_CHUNKS + 1):
                first = g + (0 if c == 0 else 2 + 4 * (c - 1))
                if c >= 1:
                    lo_to(first + (2 if c < FF0_CHUNKS else 0))
                    for k in range(2):
                        t_lo(t, f_lo[:, (c - 1) % 2, 2 * k:2 * k + 2, :], f_hi[:, (c - 1) % 2, 2 * k:2 * k + 2, :])
                        t += 1
                lo_to(first + (3 if c < FF0_CHUNKS else 2))
                t = mem_lo(t, c, NMEM0)
            add_acc("mem0", "nmix0", NMIX0, NMEM0, kvm1[:, 1, :])
            for k, (c0, n) in enumerate(FOX_JOBS):
                g_end = at["in1"]["g"] + 2 * k + 1
                lo_to(g_end + 2)
                copy_out(at["in1"]["j"] + k, g_end, proj1[:, 1, c0:c0 + n], NMIX0)
                if k == 0:
                    dve.wait_ge(l1_in, 16)
                    dve.wait_ge(j_act, plain_jobs(at["in1"]["j"]))
                    dve.wait_ge(j_dve, plain_jobs(at["in1"]["j"]))
                    for b in range(NB):
                        ins = dve.tensor_tensor(lf[:, 0, b, :], proj1[:, b, c0:c0 + n], fb[:], ALU.add)
                    chained(ins)
                    dve.scalar_tensor_tensor(lf[:, 1], lf[:, 0], -1.0, lf[:, 0], ALU.mult, ALU.max).then_inc(lf_x, 1)
                if k == 2:
                    dve.wait_ge(lf_ln, 1)
                    dve.scalar_tensor_tensor(lf[:, 3], lf[:, 0], 0.0, lf[:, 2], ALU.min, ALU.subtract).then_inc(lf_made, 1)
                if k == 3:
                    sum_heads(2, FOX_HEADS)
                if k == 4:
                    dve.wait_ge(lf_hi_made, 1)
                    dve.tensor_tensor(lf_lo[:], lf[:, 3], lf_hi[:].bitcast(F32), ALU.subtract).then_inc(lf_lo_made, 1)
                    scale_heads(2, proj1, 0, FOX_HEADS)
                    sum_heads(3, FOX_HEADS)
                if k == 6:
                    scale_heads(3, proj1, FOXW, FOX_HEADS)
                    sum_heads(4, MEM_HEADS)
                if k == 7:
                    scale_heads(4, kvm1, 0, MEM_HEADS)
            dve.wait_ge(c_psum, 1)
            dve.tensor_copy(negc[:], bank[4][:, 0:NB * FOX_HEADS].rearrange("p (b h) -> p b h", b=NB)).then_inc(c_sb, 1)
            dve.wait_ge(dec_sb, FOX_HEADS // 2)

            def beside_heads1(i):
                if i == 0:
                    sum_heads(5, MEM_HEADS, FOXW)
                if i == 1:
                    scale_heads(5, proj1, MQ1, MEM_HEADS)

            softmax_sides(at["heads1"]["h"], HEADS1, 0, beside_heads1)
            lo_to(at["out1"]["g"] + 2)
            for k in range(4):
                t_lo(at["mix1"]["t"] + k, a_at(a_lo, "mix1", 2 * k, 2), a_at(a_hi, "mix1", 2 * k, 2))
            add_out("out1", "nffn0", NFFN0)
            g = at["ff1"]["g"]
            t = at["ff1"]["t"]
            for c in range(FF1_CHUNKS + 1):
                first = g + (0 if c == 0 else 2 + 3 * (c - 1))
                if c >= 1:
                    lo_to(first + (2 if c < FF1_CHUNKS else 0))
                    t = mem_lo(t, c, NMEM1)
                    t_lo(t, f_lo[:, (c - 1) % 2, 0:2, :], f_hi[:, (c - 1) % 2, 0:2, :])
                    t += 1
                if c < FF1_CHUNKS:
                    lo_to(first + 3)
                    for b in range(NB):
                        dve.wait_ge(silu_made, 2 * c + b + 1)
                        dve.scalar_tensor_tensor(f_sb[:, c % 2, b, 0:256], bank[4 + b][:, 256:512],
                                                 rstd[:, NFFN0, b:b + 1], f_sb[:, c % 2, b, 256:512],
                                                 ALU.mult, ALU.mult).then_inc(h_made, 1)
                else:
                    lo_to(first + 1)
            add_acc("mem1", "nmix1", NMIX1, NMEM1, kvm2[:, 1, :])
            for k, (c0, n) in enumerate(CONV_JOBS):
                g_end = at["in2"]["g"] + 2 * k + 1
                lo_to(g_end + 2)
                copy_out(at["in2"]["j"] + k, g_end, proj2[:, 1, c0:c0 + n], NMIX1)
                if k == 1:
                    sum_heads(6, MEM_HEADS)
                if k == 2:
                    scale_heads(6, kvm2, 0, MEM_HEADS)
            dve.wait_ge(l2_in, 16 * len(LOADS["l2"]))
            chained(dve.memset(glu[:, :, 0:DW_K - 1], 0.0))
            chained(dve.memset(onesm[:], 1.0 / (CONV_TILES * P)))
            sum_heads(7, MEM_HEADS)
            t = at["glu"]["t"]
            for k in range(3):
                dve.wait_ge(t_act, act_steps(t + 2 * k))
                dve.wait_ge(t_psum, t + 2 * k + 2)
                for m in range(2):
                    ch = 2 * k + m
                    ins = dve.scalar_tensor_tensor(glu[:, ch, DW_K - 1:], bank[6 + (t + 2 * k + 1) % 2][:, m * S:(m + 1) * S],
                                                   cb_in[:, ch:ch + 1], sig[:, m, :], ALU.add, ALU.mult)
                ins.then_inc(t_dve, 1)
            scale_heads(7, proj2, MQ2, MEM_HEADS)
            dve.wait_ge(t_dve, dve_steps(t + 5))

            def add_taps(k):
                return dve.tensor_tensor(dwy[:, k, :], dwy[:, k, :], bank[6 + k % 2][:, 0:S], ALU.add)

            def other_taps(k):
                for i in range(PE_TAPS, DW_K):
                    u, y = glu[:, k, i:i + S], (dwy[:, k, :], stat[:, 0, :])[(i - PE_TAPS) % 2]
                    if i == PE_TAPS:
                        ins = dve.tensor_scalar(y, u, dw[:, k, i:i + 1], dwb[:, k:k + 1], ALU.mult, ALU.add)
                    elif i == PE_TAPS + 1:
                        ins = dve.tensor_scalar(y, u, dw[:, k, i:i + 1], None, ALU.mult)
                    else:
                        dve.wait_ge(dve_own, own[0] - 1)
                        ins = dve.scalar_tensor_tensor(y, u, dw[:, k, i:i + 1], y, ALU.mult, ALU.add)
                    own[0] += 1
                    ins.then_inc(dve_own, 1)
                dve.wait_ge(dve_own, own[0])
                chained(dve.tensor_tensor(dwy[:, k, :], dwy[:, k, :], stat[:, 0, :], ALU.add))
                if k >= 1:
                    dve.wait_ge(tap_used, k * PE_TAPS)
                    add_taps(k - 1).then_inc(dw_acc, 1)

            softmax_sides(at["heads2"]["h"], HEADS2, 768, other_taps)
            dve.wait_ge(tap_used, CONV_TILES * PE_TAPS)
            add_taps(CONV_TILES - 1).then_inc(dw_acc, 1)
            dve.wait_ge(mu_psum, 1)
            for k in range(CONV_TILES):
                dve.tensor_tensor(dwy[:, k, :], dwy[:, k, :], bank[0][:, 0:S], ALU.subtract).then_inc(cent_made, 1)
            lo_to(at["out2"]["g"] + 2)
            t_lo(at["mix2"]["t"], a_at(a_lo, "mix2", 6, 2), a_at(a_hi, "mix2", 6, 2))
            dve.wait_ge(sd_made, 1)
            chained(dve.reciprocal(stat[:, 2, :], stat[:, 1, :]))
            dve.wait_ge(cent_made, CONV_TILES)
            for k in range(CONV_TILES):
                dve.tensor_tensor(dwy[:, k, :], dwy[:, k, :], stat[:, 2, :], ALU.mult).then_inc(ln_made, 1)
            for k in range(0, CONV_TILES, 2):
                dve.wait_ge(ln_hi, k // 2 + 1)
                dve.tensor_tensor(a_at(a_lo, "mix2", k, 2), dwq[:, k:k + 2, :], a_at(a_hi, "mix2", k, 2).bitcast(F32),
                                  ALU.subtract).then_inc(ln_lo, 1)
            dve.wait_ge(router_hi_made, 1)
            dve.tensor_tensor(router_lo[:], router[:], router_hi[:].bitcast(F32), ALU.subtract).then_inc(router_lo_made, 1)
            add_out("out2", "nffn1", NFFN1)
            dve.wait_ge(r_psum, 1)
            dve.tensor_copy(logit_t[:], bank[4][0:N_EXPERTS, 0:S]).then_inc(r_sb, 1)
            dve.wait_ge(rt_psum, 1)
            chained(dve.tensor_copy(logit[:], bank[5][:, 0:NB * N_EXPERTS].rearrange("p (b e) -> p b e", b=NB)))
            for b in range(NB):
                ins = dve.max(top[:, b, :], logit[:, b, :])
            chained(ins)
            for b in range(NB):
                ins = dve.max_index(topi[:, b, :], top[:, b, :], logit[:, b, :])
            chained(ins)
            chained(dve.tensor_copy(topf[:], topi[:]))
            for b in range(NB):
                for m in range(2):
                    ins = dve.tensor_scalar(onehot[:, m, b, :], iota[:, 0:N_EXPERTS], topf[:, b, m:m + 1], None, ALU.is_equal)
            chained(ins)
            dve.tensor_tensor(chosen[:], onehot[:, 0], onehot[:, 1], ALU.add).then_inc(ch_made, 1)
            chained(dve.tensor_tensor(gate[:, 1, :], top[:, :, 1], top[:, :, 0], ALU.subtract))
            dve.tensor_tensor(gate[:, 0, :], gate[:, 1, :], rstd[:, NFFN1, :], ALU.mult).then_inc(gap_made, 1)

            dve.wait_ge(zhi_made, NB)
            for b in range(NB):
                dve.scalar_tensor_tensor(z_lo[:, b, :], zrow[:, b, :], rstd[:, NFFN1, b:b + 1], z_hi[:, b, :].bitcast(F32),
                                         ALU.mult, ALU.subtract).then_inc(zlo_made, 1)
            dve.wait_ge(rk_psum, 1)
            dve.wait_ge(ch_made, 1)
            chained(dve.scalar_tensor_tensor(rank[:, :, 0:N_EXPERTS],
                                             bank[4][:, 0:NB * N_EXPERTS].rearrange("p (b e) -> p b e", b=NB), -1.0,
                                             chosen[:], ALU.mult, ALU.mult))
            chained(dve.tensor_scalar(rank[:, :, 0:N_EXPERTS], rank[:, :, 0:N_EXPERTS], -1.0, None, ALU.add))
            for b in range(NB):
                ins = dve.tensor_scalar(pick[:, b, :], iota[:], rank[:, b, 0:1], None, ALU.is_equal)
            ins.then_inc(pick_made, 1)
            chained(dve.tensor_reduce(count[:, 0:1], bank[4][:, 16:24], AX_X, ALU.min))
            chained(dve.tensor_scalar(count[:, 1:2], count[:, 0:1], -float(P), float(N_EXPERTS), ALU.is_lt, ALU.mult))
            dve.tensor_scalar(n_items[:], count[:, 1:2], float(N_EXPERTS), None, ALU.add).then_inc(items_made, 1)
            lo_to(NG + 2)
            chained(dve.tensor_scalar(rank[:, :, N_EXPERTS:2 * N_EXPERTS], rank[:, :, 0:N_EXPERTS], -float(P), None, ALU.add))
            chained(dve.memset(rank[:, :, 2 * N_EXPERTS:], -1.0))
            dve.wait_ge(pickg_zero, 1)
            def xg_lo_out(k, src):
                dve.tensor_tensor(xg_lo[:, 4 * k:4 * k + 4, :], src[:].rearrange("p (k s) -> p k s", k=4),
                                  xg_hi[:, 4 * k:4 * k + 4, :].bitcast(F32), ALU.subtract).then_inc(t_dve, 1)

            def y_out():
                dve.tensor_copy(y_sb[:, 512:D], bank[1][:]).then_inc(y_dve, 1)

            def add_y(n):
                b, half = n // 2, n % 2
                xs = x[:, b, half * 512:(half + 1) * 512]
                dve.tensor_tensor(xs, xs, bank[2 - 2 * b + half][:], ALU.add).then_inc(x_upd, 1)

            for k in range(2):
                dve.wait_ge(t_act, TA + k + 1)
                xg_lo_out(k, bank[6 + (TM + k) % 2])
            dve.wait_ge(g_exp, 1)
            chained(dve.tensor_scalar(gate[:, 2, :], gate[:, 1, :], 1.0, None, ALU.add))
            chained(dve.reciprocal(gate[:, 2, :], gate[:, 2, :]))
            chained(dve.tensor_tensor(gate[:, 3, :], gate[:, 1, :], gate[:, 2, :], ALU.mult))
            for b in range(NB):
                chained(dve.tensor_scalar(gates[:, b, 0:N_EXPERTS], onehot[:, 0, b, :], gate[:, 2, b:b + 1], None, ALU.mult))
                chained(dve.scalar_tensor_tensor(gates[:, b, 0:N_EXPERTS], onehot[:, 1, b, :], gate[:, 3, b:b + 1],
                                                 gates[:, b, 0:N_EXPERTS], ALU.mult, ALU.add))
            chained(dve.tensor_copy(gates[:, :, N_EXPERTS:], gates[:, :, 0:N_EXPERTS]))
            dve.wait_ge(items_made, 1)
            items = dve.value_load(n_items[0:1, 0:1], min_val=N_EXPERTS, max_val=2 * N_EXPERTS)
            with dve.Fori(0, items) as i:
                def e_lo(k):
                    g = NG + k
                    dve.wait_ge(hi_made, i * MOE_GRANULES + (g + 1))
                    dve.tensor_tensor(w_lo[:, g % NSPLIT, :], raw_at(g, GRAN), w_hi[:, g % NSPLIT, :].bitcast(F32),
                                      ALU.subtract).then_inc(lo_made, 1)

                def step_hi(k):
                    dve.wait_ge(t_act, i * MOE_TSTEPS + (TA + 2 + k + 1))

                def chunk_lo(c):
                    step_hi(CHUNK_STEP[c])
                    dve.tensor_tensor(mf_lo[:, (c - 1) % 2, :, :],
                                      bank[6 + (TM + CHUNK_STEP[c]) % 2][:].rearrange("p (k s) -> p k s", k=4),
                                      mf_hi[:, (c - 1) % 2, :, :].bitcast(F32), ALU.subtract).then_inc(t_dve, 1)

                k = AHEAD
                for c in range(MOE_CHUNKS + 1):
                    while k <= min(moe_first(c) + (3 if c < MOE_CHUNKS else 1), MOE_GRANULES - 1):
                        e_lo(k)
                        k += 1
                    if c == 0:
                        for n in range(4):
                            dve.wait_ge(sc_psum, i * 4 + (n + 1))
                            add_y(n)
                    if c == PICKG_CHUNK - 1:
                        for b in range(NB):
                            ins = dve.tensor_scalar(pickg[:, b, :], iota[:], rank[:, b, bass.ds(i, 1)],
                                                    gates[:, b, bass.ds(i, 1)], ALU.is_equal, ALU.mult)
                        ins.then_inc(pickg_made, 1)
                    if c == PICKG_CHUNK:
                        step_hi(PICKG_STEP)
                        dve.tensor_copy(pickgT[:, P:S], bank[6 + (TM + PICKG_STEP) % 2][:, P:S]).then_inc(t_dve, 1)
                    if c == GATHER_CHUNK - 1:
                        for b in range(NB):
                            ins = dve.tensor_scalar(pick[:, b, :], iota[:], rank[:, b, bass.ds(i + 1, 1)], None, ALU.is_equal)
                        ins.then_inc(pick_made, 1)
                    if 1 <= c < MOE_CHUNKS:
                        chunk_lo(c)
                    if c < MOE_CHUNKS:
                        while k <= min(moe_first(c) + 5, MOE_GRANULES - 1):
                            e_lo(k)
                            k += 1
                        ub = bank[5] if c % 2 == 0 else bank[3]
                        dve.wait_ge(silu_made, i * MOE_CHUNKS + (SM + c + 1))
                        dve.wait_ge(w_used, i * MOE_GRANULES + (NG + moe_first(c) + 4))
                        dve.tensor_tensor(mf_sb[:, c % 2, 1, :], mf_sb[:, c % 2, 0, :], ub[:], ALU.mult).then_inc(h_made, 1)
                    if c == GATHER_CHUNK:
                        for kk in range(2):
                            step_hi(GATHER_STEP + kk)
                            xg_lo_out(kk, bank[6 + (TM + GATHER_STEP + kk) % 2])
                        chunk_lo(c + 1)
                for k in range(AHEAD):
                    if k == AHEAD - 2:
                        dve.wait_ge(w_used, i * MOE_GRANULES + (NG + MOE_GRANULES))
                        y_out()
                    e_lo(MOE_GRANULES + k)
            for n in range(4):
                dve.wait_ge(sc_psum, items * 4 + (n + 1))
                add_y(n)


def kernel(**inputs):
    import numpy as np
    from concourse import bacc
    from concourse.bass_utils import run_bass_kernel_spmd

    v = {name: np.ascontiguousarray(array) for name, array in inputs.items()}

    def cols(array, tiles):
        r = array.reshape(*array.shape[:-1], tiles, P)
        return np.ascontiguousarray(np.moveaxis(r, -1, 0))

    norms = [v["norm1_g"][0], v["norm2_g"][0], v["norm_mem_2"][0], v["norm_mix_2"][0], v["norm_ffn_2"][0],
             v["norm_mem_2"][1], v["norm_mix_2"][1], v["norm_ffn_2"][1]]
    heads = [v["q_norm_g"][0], v["k_norm_g"][0], v["fox_g_q_2"][0], v["fox_g_k_2"][0], v["g_mq_2"][0], v["g_mk_2"][0],
             v["g_mq_2"][1], v["g_mk_2"][1]]
    arrays = dict(
        g_norms=cols(np.stack(norms), KT),
        g_heads=np.ascontiguousarray(np.stack(heads).T),
        rel_bias=np.ascontiguousarray(v["rel_bias"][0][:, ::-1]),
        conv_w=np.ascontiguousarray(cols(v["conv_w"][0], 2).transpose(0, 2, 1)),
        pool_scale=cols(v["pool_scale"][0], 2),
        conv_b_in_2=cols(v["conv_b_in_2"][0], 2 * CONV_TILES),
        conv_dw_2=np.ascontiguousarray(cols(v["conv_dw_2"][0], CONV_TILES).transpose(0, 2, 1)),
        conv_dw_b_2=cols(v["conv_dw_b_2"][0], CONV_TILES),
        conv_ln_g_2=cols(v["conv_ln_g_2"][0], CONV_TILES),
        conv_ln_b_2=cols(v["conv_ln_b_2"][0], CONV_TILES),
    )
    for name in ("x", "w_in", "pool_w", "w_out", "w_mlp1", "w_mlp2", "mem_2", "norm_ffn_2", "w_mem_kv_2",
                 "fox_w_in_2", "fox_b_f_2", "fox_w_out_2", "conv_w_in_2", "conv_w_out_2", "ffn_w_gate_2",
                 "ffn_w_up_2", "ffn_w_down_2", "moe_router_2", "moe_w_gate_2", "moe_w_up_2", "moe_w_down_2"):
        arrays[name] = v[name]

    f = np.float32
    p, t = np.arange(P), np.arange(S)
    key, query = t[None, None, :], p[:, None, None] + P * np.arange(NB)[None, :, None]
    arrays["c_ident"] = np.eye(P, dtype=f)
    arrays["c_iota"] = np.broadcast_to(p.astype(f), (P, P)).copy()
    arrays["c_negtri"] = np.where(query <= key, f(-1), f(0)).astype(f)
    arrays["c_masks"] = np.stack([np.where(key // 64 <= query // 64, f(0), f(-1e30)),
                                  np.where(key <= query, f(0), f(-1e30))], axis=1).astype(f)
    windows = np.array(POOL_WINDOWS).reshape(2, 2).repeat(HD, axis=1).T
    arrays["c_invcnt"] = (1.0 / np.minimum(t[None, None, :] + 1, windows[:, :, None])).astype(f)

    nc = bacc.Bacc("TRN2", target_bir_lowering=False, num_devices=1, dynamic_dma_scratch_size=1024)
    a = {name: nc.dram_tensor(f"in_{name}", array.shape, F32, kind="ExternalInput").ap()
         for name, array in arrays.items()}
    out = nc.dram_tensor("out", (1, S, D), F32, kind="ExternalOutput").ap()
    block_kernel(nc, a, out)
    r = run_bass_kernel_spmd(nc, [{f"in_{name}": array for name, array in arrays.items()}], core_ids=[0])
    return r.results[0]["out"]
```
